# Optimizing a Trainium2 kernel written in Bass

```python
import jax
import jax.numpy as jnp
from jax import lax
import numpy as np

D_MODEL = 1024
BATCH = 1
SEQ = 1024
DEPTH = 2
DEC_BATCH = 8
DEC_SEQ = 8
PAST_LEN = 8192
PAGE_SIZE = 128

N_BRANCH = 4
D_BRANCH = D_MODEL // N_BRANCH
N_GROUPS = 4
GROUP_DIM = D_BRANCH // N_GROUPS
CONV_A_W = 3
CONV_B_W = 31
POOL_WINDOWS = (2, 4, 8, 16)
POOL_MAX = 16
CHUNK = 128
D_PLE = 256
D_FF = 2816
N_EXPERTS = 8
TOP_K = 2
D_FF_EXPERT = 3584
N_DENSE = (DEPTH + 1) // 2
N_MOE = DEPTH // 2
EPS = 1e-6

OFF_A_H = 0
OFF_A_B = OFF_A_H + D_BRANCH
OFF_A_C = OFF_A_B + D_BRANCH
OFF_CF_A = OFF_A_C + D_BRANCH
OFF_CF_B = OFF_CF_A + D_BRANCH
OFF_POOL = OFF_CF_B + D_BRANCH
OFF_U = OFF_POOL + D_BRANCH
OFF_V = OFF_U + D_BRANCH
OFF_GATE = OFF_V + D_BRANCH
IN_COLS = OFF_GATE + N_BRANCH * D_MODEL

kernel_name = 'gated_conv_pool_sgu_hybrid_step'

def _rmsnorm(x, g):
    xf = x.astype(jnp.float32)
    y = xf * lax.rsqrt(jnp.mean(xf * xf, axis=-1, keepdims=True) + EPS)
    return (y * g.astype(jnp.float32)).astype(x.dtype)

def _layernorm(x, g, b):
    xf = x.astype(jnp.float32)
    xc = xf - jnp.mean(xf, axis=-1, keepdims=True)
    var = jnp.mean(xc * xc, axis=-1, keepdims=True)
    y = xc * lax.rsqrt(var + EPS) * g.astype(jnp.float32) + b.astype(jnp.float32)
    return y.astype(x.dtype)

def _cols(z, off):
    return z[..., off:off + D_BRANCH]

def _causal_depthwise_conv(x, buf, w):
    width, ch = w.shape
    xp = jnp.concatenate([buf.astype(x.dtype), x], axis=1)
    y = lax.conv_general_dilated(xp, w.astype(x.dtype)[:, None, :], window_strides=(1,), padding='VALID',
                                 dimension_numbers=('NWC', 'WIO', 'NWC'), feature_group_count=ch)
    return y, xp[:, xp.shape[1] - (width - 1):]

def _multiscale_pool(z, buf, pos0, w_pool, scale):
    n, seq, _ = z.shape
    zp = jnp.concatenate([buf.astype(z.dtype), z], axis=1)
    zf = zp.astype(jnp.float32).reshape(n, seq + POOL_MAX - 1, N_GROUPS, GROUP_DIM)
    cs = jnp.concatenate([jnp.zeros_like(zf[:, :1]), jnp.cumsum(zf, axis=1)], axis=1)
    top = cs[:, POOL_MAX:]
    pos = pos0 + jnp.arange(seq)
    means = []
    for g, w in enumerate(POOL_WINDOWS):
        s = top[:, :, g] - cs[:, POOL_MAX - w:POOL_MAX - w + seq, g]
        cnt = jnp.minimum(w, pos + 1).astype(jnp.float32)[None, :, None]
        means.append(s / cnt)
    pooled = jnp.stack(means, axis=2) - zf[:, POOL_MAX - 1:]
    y = jnp.einsum('blgc,gcd->blgd', pooled.astype(z.dtype), w_pool).reshape(n, seq, D_BRANCH)
    return y * scale, zp[:, zp.shape[1] - (POOL_MAX - 1):]

def _chunk_sgu(u, v, ws, bs):
    n, seq, _ = v.shape
    n_chunks = -(-seq // CHUNK)
    pad = n_chunks * CHUNK - seq
    vp = jnp.pad(v, ((0, 0), (0, pad), (0, 0))).reshape(n, n_chunks, CHUNK, N_GROUPS, GROUP_DIM)
    mask = jnp.tril(jnp.ones((CHUNK, CHUNK), dtype=bool))
    wm = jnp.where(mask, ws, 0).astype(v.dtype)
    s = jnp.einsum('gts,bnsgc->bntgc', wm, vp) + bs.T[:, :, None].astype(v.dtype)
    s = s.reshape(n, n_chunks * CHUNK, D_BRANCH)[:, :seq]
    last = ((seq - 1) // CHUNK) * CHUNK
    return u * s, v[:, last:]

def _swiglu(x, wg, wu, wd):
    h = jax.nn.silu(jnp.einsum('bld,df->blf', x, wg)) * jnp.einsum('bld,df->blf', x, wu)
    return jnp.einsum('blf,fd->bld', h, wd)

def _moe_swiglu(x, w_router, wg, wu, wd):
    shp = x.shape
    xt = x.reshape(-1, D_MODEL)
    logits = jnp.dot(xt.astype(jnp.float32), w_router.astype(jnp.float32))
    top_v, top_i = lax.top_k(logits, TOP_K)
    top_w = jax.nn.softmax(top_v, axis=-1)
    flat_e = top_i.reshape(-1)
    order = jnp.argsort(flat_e)
    tok = order // TOP_K
    xs = xt[tok]
    sizes = jnp.bincount(flat_e, length=N_EXPERTS).astype(jnp.int32)
    h = jax.nn.silu(lax.ragged_dot(xs, wg, sizes)) * lax.ragged_dot(xs, wu, sizes)
    ys = lax.ragged_dot(h, wd, sizes) * top_w.reshape(-1)[order][:, None].astype(x.dtype)
    y = jnp.zeros_like(xt).at[tok].add(ys)
    return y.reshape(shp)

def _trunk(x, p, buf_a, buf_b, buf_pool, pos0, W):
    n, seq, _ = x.shape
    if buf_a is None:
        buf_a = jnp.zeros((DEPTH, n, CONV_A_W - 1, D_BRANCH), x.dtype)
        buf_b = jnp.zeros((DEPTH, n, CONV_B_W - 1, D_BRANCH), x.dtype)
        buf_pool = jnp.zeros((DEPTH, n, POOL_MAX - 1, D_BRANCH), x.dtype)
    new_a, new_b, new_pool, new_v = [], [], [], []
    for i in range(DEPTH):
        xn = _rmsnorm(x, W['norm_mix_g'][i])
        z = jnp.einsum('bld,dk->blk', xn, W['w_in'][i])
        za = _cols(z, OFF_A_C) * _cols(z, OFF_A_H)
        ya, st_a = _causal_depthwise_conv(za, buf_a[i], W['conv_a_w'][i])
        br_a = _cols(z, OFF_A_B) * ya
        glu = _cols(z, OFF_CF_A) * jax.nn.sigmoid(_cols(z, OFF_CF_B))
        yb, st_b = _causal_depthwise_conv(glu, buf_b[i], W['conv_b_w'][i])
        br_b = jax.nn.silu(_layernorm(yb + W['conv_b_bias'][i], W['conv_b_ln_g'][i], W['conv_b_ln_b'][i]))
        br_c, st_p = _multiscale_pool(_cols(z, OFF_POOL), buf_pool[i], pos0, W['pool_w'][i], W['pool_scale'][i])
        v = _layernorm(_cols(z, OFF_V), W['sgu_ln_g'][i], W['sgu_ln_b'][i])
        br_d, st_v = _chunk_sgu(_cols(z, OFF_U), v, W['sgu_w'][i], W['sgu_b'][i])
        branches = jnp.stack([br_a, br_b, br_c, br_d], axis=2)
        proj = jnp.einsum('blic,icd->blid', branches, W['w_branch'][i])
        gates = jax.nn.sigmoid(z[..., OFF_GATE:].reshape(n, seq, N_BRANCH, D_MODEL))
        mixed = jnp.sum(gates * proj, axis=2)
        x = x + jnp.einsum('bld,de->ble', mixed, W['w_out'][i])
        xn = _rmsnorm(x, W['norm_ffn_g'][i])
        j = i // 2
        if i % 2 == 0:
            f = _swiglu(xn, W['ffn_w_gate'][j], W['ffn_w_up'][j], W['ffn_w_down'][j])
        else:
            f = _moe_swiglu(xn, W['router_w'][j], W['moe_w_gate'][j], W['moe_w_up'][j], W['moe_w_down'][j])
        x = x + f
        g = jax.nn.sigmoid(jnp.einsum('bld,de->ble', _rmsnorm(x, W['norm_ple_g'][i]), W['ple_w_gate'][i]))
        x = x + g * jnp.einsum('blp,pd->bld', p[i], W['ple_w_proj'][i])
        new_a.append(st_a)
        new_b.append(st_b)
        new_pool.append(st_p)
        new_v.append(st_v)
    y = _rmsnorm(x, W['final_norm_g'])
    return y, jnp.stack(new_a), jnp.stack(new_b), jnp.stack(new_pool), jnp.stack(new_v)

def setup_inputs(seed: int = 0) -> dict:
    key = jax.random.key(seed)
    ks = iter(jax.random.split(key, 48))

    def nrm(shape, scale=1.0):
        return jax.random.normal(next(ks), shape, jnp.float32) * scale

    def gain(shape):
        return 1.0 + 0.05 * nrm(shape)

    return {
        'x_prompt': nrm((BATCH, SEQ, D_MODEL)),
        'x_sample': nrm((DEC_BATCH, DEC_SEQ, D_MODEL)),
        'state_conv_a': nrm((DEPTH, DEC_BATCH, CONV_A_W - 1, D_BRANCH)),
        'state_conv_b': nrm((DEPTH, DEC_BATCH, CONV_B_W - 1, D_BRANCH)),
        'state_pool': nrm((DEPTH, DEC_BATCH, POOL_MAX - 1, D_BRANCH)),
        'p_prompt': nrm((DEPTH, BATCH, SEQ, D_PLE)),
        'p_sample': nrm((DEPTH, DEC_BATCH, DEC_SEQ, D_PLE)),
        'norm_mix_g': gain((DEPTH, D_MODEL)),
        'w_in': nrm((DEPTH, D_MODEL, IN_COLS), D_MODEL ** -0.5),
        'conv_a_w': nrm((DEPTH, CONV_A_W, D_BRANCH), CONV_A_W ** -0.5),
        'conv_b_w': nrm((DEPTH, CONV_B_W, D_BRANCH), CONV_B_W ** -0.5),
        'conv_b_bias': nrm((DEPTH, D_BRANCH), 0.02),
        'conv_b_ln_g': gain((DEPTH, D_BRANCH)),
        'conv_b_ln_b': nrm((DEPTH, D_BRANCH), 0.02),
        'pool_w': nrm((DEPTH, N_GROUPS, GROUP_DIM, GROUP_DIM), GROUP_DIM ** -0.5),
        'pool_scale': gain((DEPTH, D_BRANCH)),
        'sgu_ln_g': gain((DEPTH, D_BRANCH)),
        'sgu_ln_b': nrm((DEPTH, D_BRANCH), 0.02),
        'sgu_w': nrm((DEPTH, N_GROUPS, CHUNK, CHUNK), CHUNK ** -0.5),
        'sgu_b': gain((DEPTH, N_GROUPS, CHUNK)),
        'w_branch': nrm((DEPTH, N_BRANCH, D_BRANCH, D_MODEL), D_BRANCH ** -0.5),
        'w_out': nrm((DEPTH, D_MODEL, D_MODEL), D_MODEL ** -0.5),
        'norm_ffn_g': gain((DEPTH, D_MODEL)),
        'ffn_w_gate': nrm((N_DENSE, D_MODEL, D_FF), D_MODEL ** -0.5),
        'ffn_w_up': nrm((N_DENSE, D_MODEL, D_FF), D_MODEL ** -0.5),
        'ffn_w_down': nrm((N_DENSE, D_FF, D_MODEL), D_FF ** -0.5),
        'router_w': nrm((N_MOE, D_MODEL, N_EXPERTS), D_MODEL ** -0.5),
        'moe_w_gate': nrm((N_MOE, N_EXPERTS, D_MODEL, D_FF_EXPERT), D_MODEL ** -0.5),
        'moe_w_up': nrm((N_MOE, N_EXPERTS, D_MODEL, D_FF_EXPERT), D_MODEL ** -0.5),
        'moe_w_down': nrm((N_MOE, N_EXPERTS, D_FF_EXPERT, D_MODEL), D_FF_EXPERT ** -0.5),
        'norm_ple_g': gain((DEPTH, D_MODEL)),
        'ple_w_gate': nrm((DEPTH, D_MODEL, D_MODEL), D_MODEL ** -0.5),
        'ple_w_proj': nrm((DEPTH, D_PLE, D_MODEL), D_PLE ** -0.5),
        'final_norm_g': gain((D_MODEL,)),
    }

def reference(x_prompt, x_sample, state_conv_a, state_conv_b, state_pool, p_prompt, p_sample,
              norm_mix_g, w_in, conv_a_w, conv_b_w, conv_b_bias, conv_b_ln_g, conv_b_ln_b,
              pool_w, pool_scale, sgu_ln_g, sgu_ln_b, sgu_w, sgu_b, w_branch, w_out,
              norm_ffn_g, ffn_w_gate, ffn_w_up, ffn_w_down, router_w, moe_w_gate, moe_w_up, moe_w_down,
              norm_ple_g, ple_w_gate, ple_w_proj, final_norm_g):
    W = {
        'norm_mix_g': norm_mix_g, 'w_in': w_in, 'conv_a_w': conv_a_w, 'conv_b_w': conv_b_w,
        'conv_b_bias': conv_b_bias, 'conv_b_ln_g': conv_b_ln_g, 'conv_b_ln_b': conv_b_ln_b,
        'pool_w': pool_w, 'pool_scale': pool_scale, 'sgu_ln_g': sgu_ln_g, 'sgu_ln_b': sgu_ln_b,
        'sgu_w': sgu_w, 'sgu_b': sgu_b, 'w_branch': w_branch, 'w_out': w_out,
        'norm_ffn_g': norm_ffn_g, 'ffn_w_gate': ffn_w_gate, 'ffn_w_up': ffn_w_up, 'ffn_w_down': ffn_w_down,
        'router_w': router_w, 'moe_w_gate': moe_w_gate, 'moe_w_up': moe_w_up, 'moe_w_down': moe_w_down,
        'norm_ple_g': norm_ple_g, 'ple_w_gate': ple_w_gate, 'ple_w_proj': ple_w_proj,
        'final_norm_g': final_norm_g,
    }
    y_prompt, a_p, b_p, pool_p, v_p = _trunk(x_prompt, p_prompt, None, None, None, 0, W)
    y_sample, a_s, b_s, pool_s, v_s = _trunk(x_sample, p_sample, state_conv_a, state_conv_b, state_pool,
                                             PAST_LEN, W)
    return (y_prompt, y_sample, a_p, b_p, pool_p, v_p, a_s, b_s, pool_s, v_s)


_drawn_inputs = setup_inputs


def setup_inputs(seed=0):
    import zlib

    import numpy as np

    out = dict(_drawn_inputs(seed))
    spreads = {}
    factors = {'conv_b_bias': 2.92, 'conv_b_ln_b': 4.911, 'sgu_ln_b': 2.915, 'norm_ple_g': 3.63}
    for name, (base, spread) in spreads.items():
        noise = np.random.default_rng([zlib.crc32(name.encode()), seed]).standard_normal(out[name].shape)
        drawn = base * np.exp(spread * noise) if base else spread * noise
        out[name] = jnp.asarray(drawn.astype(out[name].dtype))
    for name, factor in factors.items():
        out[name] = (out[name] * factor).astype(out[name].dtype)
    return out
```

```python
from contextlib import ExitStack

import concourse.bass as bass
from concourse import mybir

F32 = mybir.dt.float32
F32R = mybir.dt.float32r
I32 = mybir.dt.int32
U32 = mybir.dt.uint32
ALU = mybir.AluOpType
ACT = mybir.ActivationFunctionType
AXX = mybir.AxisListType.X

P = 128
D = 1024
KC = D // P
DEPTH = 2
SEQ = 1024
NSEQ, DSEQ = 8, 8
NTOK = SEQ + NSEQ * DSEQ
NT = -(-NTOK // P)
DB = 256
DFF = 2816
NE = 8
DFE = 3584
EPS = 1e-6
BLOCKS = ((0, 384), (384, 384), (768, 320))
GROUPS = 4
WINDOWS = (2, 4, 8, 16)
POOL_MAX = max(WINDOWS)

OFF_H, OFF_AB, OFF_AC, OFF_CFA, OFF_CFB, OFF_POOL, OFF_U, OFF_V, OFF_GATE = (DB * i for i in range(9))
BR_A, BR_B, BR_C, BR_D = range(4)

CAP = 336
EXTRA = -(-NTOK // CAP) - 1
PAIRS = 2 * NTOK
SLOTS = NE + PAIRS // CAP
FFN_GROUPS = DFF // 256
MOE_GROUPS = DFE // 256
XBLK = ((0, 128), (128, 128), (256, CAP - 256))

RAW, HL, BANKS, LOOK = 2, 4, 6, 3


class Count:

    def __init__(self, sem=None):
        self.sem, self.n, self.terms = sem, 0, []

    def next(self):
        self.n += 1
        return self.sem

    def take(self, k=1):
        self.n += k
        return self.at(self.n)

    def at(self, n, mul=1, div=1):
        v = n // div * mul
        for reg, per in self.terms:
            assert per % div == 0
            v = v + reg * (per // div * mul)
        return v

    def before(self, back, mul=1):
        if self.n - back <= 0:
            assert not self.terms, "a wait in a loop against a value that may be zero"
            return None
        return self.at(self.n - back, mul)


def wait(eng, sem, value):
    if value is not None:
        eng.wait_ge(sem, value)


class Engine:

    def __init__(self, eng, own):
        self.eng, self.own, self.last = eng, Count(own), None

    def do(self, ins, sig=None):
        sig = sig or self.own
        ins.then_inc(sig.next(), 1)
        self.last = (sig, sig.n)
        return self.last

    def sync(self, mark=None):
        sig, n = mark or self.last
        self.eng.wait_ge(sig.sem, sig.at(n))


def looped(counts, reg, per):
    for c in counts:
        c.terms.append((reg, per[c]))
    return [c.n for c in counts]


def leave(counts, starts, per, times):
    for c, n0 in zip(counts, starts):
        assert c.n - n0 == per[c], (c.sem, c.n - n0, per[c])
        c.terms.pop()
        c.n = n0 + times * per[c]


def leave_items(counts, starts, per, reg):
    for c, n0 in zip(counts, starts):
        assert c.n - n0 == per[c], (c.sem, c.n - n0, per[c])
        c.terms.pop()
        c.n = n0
        c.terms.append((reg, per[c]))


def build(nc, A, O):
    es = ExitStack()
    sem = lambda name: es.enter_context(nc.semaphore(name))
    place = [16512]
    names = {}

    def at(name, shape, dt, off):
        return nc.alloc_sbuf_tensor_at(name, list(shape), dt, offset=off)

    def sb(name, shape, dt=F32):
        size = 4
        for s in shape[1:]:
            size *= s
        off = place[0]
        place[0] += -(-size // 32) * 32
        names[name] = off
        return at(name, shape, dt, off)

    XHI = sb("XHI", [P, KC, NTOK], F32R)
    XLO = sb("XLO", [P, KC, NTOK], F32R)
    WRAW = [sb(f"WRAW{i}", [P, 2048]) for i in range(RAW)]
    WHI = [sb(f"WHI{i}", [P, KC, P], F32R) for i in range(HL)]
    WLO = [sb(f"WLO{i}", [P, KC, P], F32R) for i in range(HL)]
    RSTD = sb("RSTD", [P, NTOK])
    T = [sb(f"T{i}", [P, 384]) for i in range(4)]
    IDF = sb("IDF", [P, P])
    IDR = sb("IDR", [P, P], F32R)
    TRIL = sb("TRIL", [P, P])
    ONES = sb("ONES", [P, P])
    PAR = sb("PAR", [P, 4 * 38 + 7 * KC])
    RTOK = sb("RTOK", [P, NT])
    EPSC = sb("EPSC", [P, 1])
    WIN = sb("WIN", [P, 2])
    WINV = sb("WINV", [P, 2])
    FIXT = sb("FIXT", [P, 2, 16])
    PH = place[0]
    END = nc.sbuf_usable_end
    XHF, XLF = XHI[:].bitcast(F32), XLO[:].bitcast(F32)

    MIXED = at("MIXED", [P, KC, NTOK], F32, PH)
    MLO = at("MLO", [P, KC, NTOK], F32R, PH)
    MHI = at("MHI", [P, KC, NTOK], F32R, PH + 34816)
    o = PH
    sub = {}
    for name, shape in (("V", [P, NT, DB]), ("SWRAW", [P, GROUPS, P]), ("BDRAW", [64, GROUPS, 64]), ("WT", [P, GROUPS, P]),
                        ("BD", [64, GROUPS, 64]), ("BIAS", [P, 2, P]), ("LNG", [P, DB]), ("LNB", [P, DB]),
                        ("ST", [120, 4, DB]), ("PRS", [38, 2, DB]), ("NRS", [7 * KC, P]), ("BNS", [P, NT, 6]), ("MV", [P, NT, 2]),
                        ("VR", [P, NT])):
        size = 4
        for s in shape[1:]:
            size *= s
        sub[name] = at(name, shape, F32, o)
        o += -(-size // 32) * 32
    assert o <= PH + 32768
    V, SWRAW, BDRAW, WT, BD, BIAS, LNG, LNB, ST, PRS, NRS, BNS, MV, VR = sub.values()
    PA, PB, PC = 2, 30, 15
    WA, WB, WC = (p + SEQ + NSEQ * (p + DSEQ) for p in (PA, PB, PC))
    AR1 = PH + 34816
    GLU = at("GLU", [P, 2, WB], F32, AR1)
    SQB = at("SQB", [P, 2, NTOK], F32, AR1)
    up = lambda size: -(-size // 32) * 32
    YB = at("YB", [P, 2, NTOK], F32, AR1 + up(2 * WB * 4))
    AR2 = AR1 + up(2 * WB * 4) + 2 * NTOK * 4
    UB = at("UB", [P, 2, NTOK], F32, AR2)
    ZA = at("ZA", [P, 2, WA], F32, AR2)
    YA = at("YA", [P, 2, NTOK], F32, AR2 + up(2 * WA * 4))
    ZP = at("ZP", [P, 2, WC], F32, AR2)
    YP = at("YP", [P, 2, NTOK], F32, AR2 + up(2 * WC * 4))
    KEEP = at("KEEP", [P, 272], F32, PH + 72896)
    assert AR2 + up(2 * WC * 4) + 2 * NTOK * 4 <= PH + 72896
    XIN = at("XIN", [P, NT, D], F32, PH + 32768)
    SQS = at("SQS", [P, NTOK], F32, PH + 69632)
    PW = [at(f"PW{i}", [P, 2, DB], F32, PH + 69632 + 4352 + 2048 * i) for i in range(2)]
    OUTST = at("OUTST", [120, DB], F32, PH + 78080)
    PBD = at("PBD", [P, 2, P], F32, PH + 78080 + 1024)
    assert PH + 78080 + 2048 <= END, (PH, END)
    ACC = at("ACC", [P, KC, NTOK], F32, PH)
    HHI = [at(f"HHI{i}", [P, 2, NTOK], F32R, PH + 34816 + 17408 * i) for i in range(2)]
    HLO = [at(f"HLO{i}", [P, 2, NTOK], F32R, PH + 34816 + 17408 * i + 8704) for i in range(2)]
    GS = at("GS", [P, 2, NTOK], F32, PH + 69632)
    XNEW = at("XNEW", [P, KC, NTOK], F32, PH)
    PTOK = at("PTOK", [P, NT, DB], F32, PH + 52224)
    PT = at("PT", [P, 2, NTOK], F32, PH + 34816)
    YOUT = [at(f"YOUT{i}", [P, D], F32, PH + 34816 + 4096 * i) for i in range(2)]
    o = [PH]

    def mo(name, shape, dt=F32):
        size = 4
        for s in shape[1:]:
            size *= s
        t = at(name, shape, dt, o[0])
        o[0] += -(-size // 32) * 32
        return t

    XG = mo("XG", [P, 3, D])
    XSH = mo("XSH", [P, KC, CAP], F32R)
    XSL = mo("XSL", [P, KC, CAP], F32R)
    EHI = [mo(f"EHI{i}", [P, 2, CAP], F32R) for i in range(2)]
    ELO = [mo(f"ELO{i}", [P, 2, CAP], F32R) for i in range(2)]
    EG = mo("EG", [P, 2, CAP])
    EACC = mo("EACC", [P, KC, CAP])
    YT = [mo(f"YT{i}", [P, D]) for i in range(2)]
    RW = mo("RW", [P, KC, NE])
    LG = mo("LG", [P, NT, NE])
    MX = mo("MX", [P, NT, NE])
    IX = mo("IX", [P, NT, NE], U32)
    IXF = mo("IXF", [P, NT, NE])
    OH = [mo(f"OH{i}", [P, NT, NE]) for i in range(2)]
    SS = mo("SS", [P, NT, NE])
    CS = mo("CS", [P, NT, NE])
    TM = mo("TM", [P, NT, NE])
    POSF = mo("POSF", [P, 2, NT])
    POSI = mo("POSI", [P, 2, NT], I32)
    TW = mo("TW", [P, 2, NT])
    IOT = mo("IOT", [P, NE])
    CNT = mo("CNT", [P, NE])
    BASE = mo("BASE", [P, NE])
    ITEMS = mo("ITEMS", [1, 3 * SLOTS], I32)
    assert o[0] <= PH + 69632, o[0] - PH
    NJ = NE * (EXTRA + 1)
    lo = PH + 73984 + 4096
    LROW = at("LROW", [1, 5, NJ], F32, lo)
    LSEL = at("LSEL", [1, SLOTS, NJ], F32, PH + 73984)
    LOUT = at("LOUT", [1, 3, SLOTS], F32, up(lo + 20 * NJ))
    SLI = at("SLI", [1, SLOTS], F32, lo + up(20 * NJ) + up(12 * SLOTS))
    TRIS = at("TRIS", [P, P], F32, PH + 12288)
    YG = [[at(f"YG{i}{k}", [P, D], F32, PH + 8192 * i + 4096 * k) for k in range(2)] for i in range(2)]
    TC = [at(f"TC{i}", [P, 4, P], F32, PH + 16384 + 2048 * i) for i in range(4)]
    assert SLOTS * NJ * 4 <= 4096 and lo + 20 * NJ + 12 * SLOTS <= END

    XS = nc.dram_tensor("sorted_rows", [PAIRS + CAP, D], F32).ap()
    YS = nc.dram_tensor("expert_rows", [PAIRS + CAP, D], F32).ap()

    PS = es.enter_context(nc.psum_tensor("PS", [P, 8, 512], F32))

    S = {n: sem(n) for n in (
        "raw_ready0", "raw_ready1", "folded", "hi_ready", "lo_ready", "pw_ready0", "pw_ready1",
        "mm_done", "evicted", "misc_done", "misc_free", "act_req", "act_done", "split_req", "split_hi", "split_done",
        "dve_own", "act_own", "pool_own", "consts", "x_loaded", "par_loaded", "prs_loaded", "sgu_zeroed", "st_loaded", "sgu_loaded", "pbd_loaded", "pads_clear",
        "rstd_ready", "sq_ready", "sgu_weights", "v_ready", "br_a", "br_b", "br_c", "br_d", "yb_ready", "lnsq_ready", "pooled",
        "stage_full", "stage_out", "outputs0", "outputs1", "tok_ready", "p_loaded", "p_ready", "mixed_ready", "rows_ready", "rows_gone0", "rows_gone1", "tri_ready",
        "counts_ready", "items_ready", "scattered", "xg_ready", "xg_used", "xs_ready", "ys_full", "ys_out", "gathered0", "gathered1", "gather_used", "combined",
        "xnew_ready", "y_full", "v_out", "par_ready", "rw_loaded", "phase_clear", "spacer")}

    mix_l = lambda l: [("col", l)] * 4 + [("col", l)] * 4 + [("col", l)] * 3 + [("col", l)] * 4 + [("col", l)] * 1 + [("col", l)] * 8
    ffn_l = [("col", 2)] * 2 + [("col", 2), ("col", 2), ("row", None)] * (FFN_GROUPS - 1) + [("row", None)]
    kinds = mix_l(0) + [("col", None)] * 4 + ffn_l + [("col", 4)] * 4 + mix_l(1) + [("col", None)] * 4 + [("col", 5)] * 4
    item_kinds = [("col", None)] * 2 + [("col", None), ("col", None), ("row", None)] * (MOE_GROUPS - 1) + [("row", None)]
    T_MOE = 24 + 4 + len(ffn_l) + 4 + 24 + 4
    gain = lambda norm: PAR[:, 152 + norm * KC:152 + (norm + 1) * KC]
    par = lambda l, c, r: PAR[:, (l * 2 + c) * 38 + r:(l * 2 + c) * 38 + r + 1]
    R_CB, R_CA, R_BIAS, R_LG, R_LB, R_PS = 0, 31, 34, 35, 36, 37

    def raw_view(t, half, kind):
        if kind == "col":
            return WRAW[t][:].rearrange("p (k n) -> p k n", k=KC)[:, :, half * P:(half + 1) * P]
        return WRAW[t][:, half * 1024:(half + 1) * 1024].rearrange("p (k n) -> p k n", k=KC)

    def pieces(j, buf, pad):
        t0, n = BLOCKS[j]
        out = []
        if t0 < SEQ:
            m = min(n, SEQ - t0)
            out.append((0, m, buf[:, pad + t0:pad + t0 + m]))
        if t0 + n > SEQ:
            s = buf[:, pad + SEQ:].rearrange("p (s t) -> p s t", s=NSEQ)[:, :, pad:]
            out.append((SEQ - t0, n - (SEQ - t0), s))
        return out

    def shaped(ap, like):
        return ap.rearrange("p (s t) -> p s t", s=NSEQ) if len(like.shape) == 3 else ap

    def tokens(j):
        return min(P, NTOK - j * P)

    def groups(n):
        yield ("GU", 0)
        for g in range(1, n):
            yield ("GU", g)
            yield ("DN", g - 1)
        yield ("DN", n - 1)

    FFN_LOOP, MOE_LOOP = (FFN_GROUPS - 3) // 2, (MOE_GROUPS - 2) // 2
    assert FFN_GROUPS % 2 == 1 and MOE_GROUPS % 2 == 0
    Q_FFN = 6 + 12 + 48 + 18 + 48 + 6 + 48 + 48 + 24
    Q_LAST_DOWN = Q_FFN + 12 + 36 * (FFN_GROUPS - 1)
    W_FFN = 3 * KC + KC + 3 * KC
    W_MOE = W_FFN + 6 * FFN_GROUPS + 3 * KC + 3 * KC + KC + 3 * KC

    def ffn_schedule(n, loops):
        steps = list(groups(n))
        return steps[:1], steps[1:5], steps[1 + 4 * loops:]

    def spacer(eng):
        eng.sem_inc(S["spacer"], 1)

    def load_p(q, l):
        for j in range(NT):
            n = tokens(j)
            src = A["p_prompt"][l, 0, j * P:(j + 1) * P, :] if j < NT - 1 else A["p_sample"][l].rearrange("s t d -> (s t) d")
            q.dma_start(PTOK[0:n, j, :], src).then_inc(S["p_loaded"], 16)

    block = es.enter_context(nc.Block())

    @block.sync
    def _(sp):
        tile = Count()
        pw, q, pw_end = Count(), Count(), []

        def load(src):
            if tile.n >= RAW:
                sp.wait_ge(S["lo_ready"], lo_value(tile))
            s = tile.n % RAW
            k = src.shape[1]
            sp.dma_start(WRAW[s][:].rearrange("p (k n) -> p k n", k=k), src).then_inc(S[f"raw_ready{s}"], 16)
            tile.n += 1

        def lo_value(t):
            v = t.n * 2 - 2 * RAW + 2
            for reg, per in t.terms:
                v = v + reg * (2 * per)
            return v

        def load_pw(src):
            if pw.n >= 2:
                sp.wait_ge(S["mm_done"], pw_end[pw.n - 2])
            s = pw.n % 2
            sp.dma_start(PW[s][:], src).then_inc(S[f"pw_ready{s}"], 16)
            pw.n += 1

        def cols(w, c0, n=DB):
            return w.rearrange("(k p) n -> p k n", p=P)[:, :, bass.ds(c0, n)]

        for j in range(NT):
            n = tokens(j)
            src = A["x_prompt"][0, j * P:(j + 1) * P, :] if j < NT - 1 else A["x_sample"].rearrange("s t d -> (s t) d")
            sp.dma_start(XIN[0:n, j, :], src).then_inc(S["x_loaded"], 16)
        for l in range(DEPTH):
            w_in = A["w_in"][l]
            wb = A["w_branch"][l]

            def gate_project(br):
                for j in range(4):
                    load(cols(w_in, OFF_GATE + br * D + j * DB))
                    load_pw(cols(wb[br], j * DB))
                    q.n += 12
                    pw_end.append(q.at(q.n))

            load(cols(w_in, OFF_U))
            load(cols(w_in, OFF_V))
            load(cols(w_in, OFF_CFB))
            load(cols(w_in, OFF_CFA))
            q.n += 18
            gate_project(BR_D)
            for off in (OFF_AC, OFF_H, OFF_AB):
                load(cols(w_in, off))
            q.n += 18
            gate_project(BR_A)
            load(cols(w_in, OFF_POOL))
            q.n += 6
            gate_project(BR_B)
            gate_project(BR_C)
            for j in range(4):
                load(cols(A["w_out"][l], j * DB))
            q.n += 24
            if l == 0:
                wg, wu, wd = (A[n][0] for n in ("ffn_w_gate", "ffn_w_up", "ffn_w_down"))
                wdr = wd.rearrange("(f p) n -> p f n", p=P)

                def step(kind, g, i=0):
                    if kind == "GU":
                        load(cols(wg, i * 512 + g * DB))
                        load(cols(wu, i * 512 + g * DB))
                    else:
                        load(wdr[:, bass.ds(i * 4 + g * 2, 2), :])

                head, body, tail = ffn_schedule(FFN_GROUPS, FFN_LOOP)
                for s in head:
                    step(*s)
                with sp.Fori(0, FFN_LOOP) as i:
                    st = looped([tile], i, {tile: 6})
                    for s in body:
                        step(*s, i)
                leave([tile], st, {tile: 6}, FFN_LOOP)
                for s in tail:
                    step(*s)
                q.n += 36 * FFN_GROUPS
            else:
                sp.wait_ge(S["items_ready"], 1)
                n_items = sp.value_load(ITEMS[0:1, 2 * SLOTS:2 * SLOTS + 1], min_val=NE, max_val=SLOTS)
                wg = A["moe_w_gate"][0].rearrange("e (k p) n -> p (e k) n", p=P)
                wu = A["moe_w_up"][0].rearrange("e (k p) n -> p (e k) n", p=P)
                wd = A["moe_w_down"][0].rearrange("e (f p) n -> p (e f) n", p=P)
                NF = DFE // P
                with sp.Fori(0, SLOTS) as it:
                    with sp.If(it < n_items):
                        e = sp.value_load(ITEMS[0:1, bass.ds(it, 1)], min_val=0, max_val=NE - 1)
                        st = looped([tile], it, {tile: len(item_kinds)})

                        def step(kind, g, i=0):
                            if kind == "GU":
                                load(wg[:, bass.ds(e * KC, KC), bass.ds(i * 512 + g * DB, DB)])
                                load(wu[:, bass.ds(e * KC, KC), bass.ds(i * 512 + g * DB, DB)])
                            else:
                                load(wd[:, bass.ds(e * NF + i * 4 + g * 2, 2), :])

                        head, body, tail = ffn_schedule(MOE_GROUPS, MOE_LOOP)
                        for s in head:
                            step(*s)
                        with sp.Fori(0, MOE_LOOP) as i:
                            st2 = looped([tile], i, {tile: 6})
                            for s in body:
                                step(*s, i)
                        leave([tile], st2, {tile: 6}, MOE_LOOP)
                        for s in tail:
                            step(*s)
                        leave_items([tile], st, {tile: len(item_kinds)}, n_items)
                q.terms.append((n_items, 12 * MOE_GROUPS))
            for j in range(4):
                load(cols(A["ple_w_gate"][l], j * DB))
                if l == 0 and j == 0:
                    sp.wait_ge(S["evicted"], Q_LAST_DOWN + 1)
                load_pw(cols(A["ple_w_proj"][l], j * DB))
                q.n += 12
                pw_end.append(q.at(q.n))

    @block.gpsimd
    def _(g):
        pool = Engine(g, S["pool_own"])
        tile = Count()
        kp = [0]

        for j in range(7):
            src = (A["norm_mix_g"][j % 2] if j < 2 else A["norm_ffn_g"][j % 2] if j < 4 else A["norm_ple_g"][j % 2] if j < 6
                   else A["final_norm_g"])
            g.dma_start(NRS[j * KC:(j + 1) * KC, :], src.rearrange("(k p) -> k p", p=P)).then_inc(S["par_loaded"], 16)
        for l in range(DEPTH):
            for r, n, src in ((R_CB, 31, A["conv_b_w"][l]), (R_CA, 3, A["conv_a_w"][l]), (R_BIAS, 1, A["conv_b_bias"][l:l + 1]),
                              (R_LG, 1, A["conv_b_ln_g"][l:l + 1]), (R_LB, 1, A["conv_b_ln_b"][l:l + 1]), (R_PS, 1, A["pool_scale"][l:l + 1])):
                g.dma_start(PRS[r:r + n, l, :], src).then_inc(S["par_loaded"], 16)
        g.memset(IDF[:], 0.0).then_inc(S["pool_own"], 1)
        g.memset(TRIL[:], 1.0).then_inc(S["pool_own"], 1)
        g.wait_ge(S["pool_own"], 2)
        g.affine_select(out=IDF[:], in_=IDF[:], compare_op=ALU.not_equal, fill=1.0, base=0, pattern=[[-1, P]],
                        channel_multiplier=1).then_inc(S["consts"], 1)
        g.affine_select(out=TRIL[:], in_=TRIL[:], compare_op=ALU.is_ge, fill=0.0, base=0, pattern=[[1, P]],
                        channel_multiplier=-1).then_inc(S["consts"], 1)
        g.iota(FIXT[:], pattern=[[0, 2], [1, 16]], base=1, channel_multiplier=0,
               allow_small_or_imprecise_dtypes=True).then_inc(S["consts"], 1)

        def layer_params(l):
            g.wait_ge(S["sgu_zeroed"], l + 1)
            g.dma_start(SWRAW[:], A["sgu_w"][l].rearrange("g t s -> t g s")).then_inc(S["sgu_loaded"], 16)
            for b in range(NSEQ):
                g.dma_start(BDRAW[8 * b:8 * b + 8, :, 8 * b:8 * b + 8], A["sgu_w"][l][:, 0:8, 0:8].rearrange("g t s -> t g s")
                            ).then_inc(S["sgu_loaded"], 16)
            for q in range(GROUPS):
                g.dma_start(BIAS[64 * (q % 2):64 * (q % 2) + 64, q // 2, :], A["sgu_b"][l, q, :].partition_broadcast(64)
                            ).then_inc(S["sgu_loaded"], 16)
                g.dma_start(PBD[64 * (q % 2):64 * (q % 2) + 64, q // 2, 64 * (q % 2):64 * (q % 2) + 64], A["pool_w"][l, q]
                            ).then_inc(S["pbd_loaded"], 16)
            g.dma_start(LNG[:], A["sgu_ln_g"][l].partition_broadcast(P)).then_inc(S["sgu_loaded"], 16)
            g.dma_start(LNB[:], A["sgu_ln_b"][l].partition_broadcast(P)).then_inc(S["sgu_loaded"], 16)
            sb_ = A["state_conv_b"][l].rearrange("(h s) r c -> h (s r) c", h=2)
            for h in range(2):
                g.dma_start(ST[:, h, :], sb_[h]).then_inc(S["st_loaded"], 16)
            g.dma_start(ST[:, 2, :], A["state_pool"][l].rearrange("s r c -> (s r) c")).then_inc(S["st_loaded"], 16)
            g.dma_start(ST[0:16, 3, :], A["state_conv_a"][l].rearrange("s r c -> (s r) c")).then_inc(S["st_loaded"], 16)

        def fold():
            kind, norm = kinds[kp[0]]
            kp[0] += 1
            if norm is not None:
                s = tile.n % RAW
                g.wait_ge(S["par_ready"], 1)
                g.wait_ge(S[f"raw_ready{s}"], tile.at(tile.n, 16, 2) + 16)
                w = WRAW[s][:].rearrange("p (k n) -> p k n", k=KC)
                g.tensor_tensor(w, w, gain(norm).unsqueeze(2).to_broadcast([P, KC, DB]), ALU.mult).then_inc(S["folded"], 1)
            tile.n += 1

        layer_params(0)
        for _ in range(24 + 4):
            fold()
        fold(), fold()
        with g.Fori(0, FFN_LOOP) as i:
            st = looped([tile], i, {tile: 6})
            for _ in range(6):
                fold()
        leave([tile], st, {tile: 6}, FFN_LOOP)
        kp[0] = tile.n
        while tile.n < 24 + 4 + len(ffn_l):
            fold()
        g.wait_ge(S["evicted"], Q_LAST_DOWN)
        load_p(g, 0)
        for _ in range(4):
            fold()
        fold(), fold()
        layer_params(1)
        for _ in range(24 + 4 - 2):
            fold()

        g.wait_ge(S["phase_clear"], 1)
        g.dma_start(RW[:], A["router_w"][0].rearrange("(k p) e -> p k e", p=P)).then_inc(S["rw_loaded"], 16)
        g.iota(SLI[:], pattern=[[1, SLOTS]], base=0, channel_multiplier=0, allow_small_or_imprecise_dtypes=True).then_inc(S["consts"], 1)
        g.iota(IOT[:], pattern=[[1, NE]], base=0, channel_multiplier=0, allow_small_or_imprecise_dtypes=True).then_inc(S["consts"], 1)
        for j, (r0, n) in enumerate(XBLK):
            g.dma_start(XS[PAIRS + r0:PAIRS + r0 + n, :], XG[0:n, j, :]).then_inc(S["scattered"], 16)
        for j in range(NT):
            n = tokens(j)
            g.wait_ge(S["rows_ready"], j + 1)
            for k in range(2):
                g.indirect_dma_start(XS[0:PAIRS, :], bass.IndirectOffsetOnAxis(ap=POSI[0:n, k, j:j + 1], axis=0), YT[j % 2][0:n, :],
                                     None).then_inc(S[f"rows_gone{j % 2}"], 16)
        g.wait_ge(S["rows_gone0"], 32 * ((NT + 1) // 2))
        g.wait_ge(S["rows_gone1"], 32 * (NT // 2))
        g.wait_ge(S["scattered"], 48)
        g.wait_ge(S["ys_out"], 48)
        g.wait_ge(S["items_ready"], 1)
        n_items = g.value_load(ITEMS[0:1, 2 * SLOTS:2 * SLOTS + 1], min_val=NE, max_val=SLOTS)
        with g.Fori(0, SLOTS) as it:
            with g.If(it < n_items):
                row = g.value_load(ITEMS[0:1, bass.ds(it + SLOTS, 1)], min_val=0, max_val=PAIRS)
                g.wait_ge(S["xg_used"], it + 1)
                spacer(g)
                for j, (r0, n) in enumerate(XBLK):
                    g.dma_start(XG[0:n, j, :], XS[bass.ds(row + r0, n), :]).then_inc(S["xg_ready"], 16)
        g.wait_ge(S["ys_out"], n_items * 48 + 48)
        spacer(g)
        for j in range(NT):
            n = tokens(j)
            if j >= 2:
                g.wait_ge(S["gather_used"], j - 1)
            for k in range(2):
                g.indirect_dma_start(YG[j % 2][k][0:n, :], None, YS[0:PAIRS, :],
                                     bass.IndirectOffsetOnAxis(ap=POSI[0:n, k, j:j + 1], axis=0)).then_inc(S[f"gathered{j % 2}"], 16)
        load_p(g, 1)
        tile.terms.append((n_items, len(item_kinds)))
        for _ in range(4):
            fold()

    @block.tensor
    def _(pe):
        unit, q, m, pw = Count(), Count(S["mm_done"]), Count(S["misc_done"]), Count()
        split = Count()

        def use(n=1):
            pe.wait_ge(S["lo_ready"], unit.at(unit.n + n))

        def open_bank():
            wait(pe, S["evicted"], q.before(BANKS - 1))
            return q.n % BANKS

        def misc_bank():
            wait(pe, S["misc_free"], m.before(1))
            if m.terms:
                spacer(pe)
            return 6 + m.n % 2

        def product(bank, n, slot, hi, lo, ks=range(KC), last_of_unit=False, first=True, last=True):
            for x, k in enumerate(ks):
                wh, wl = WHI[slot][:, k, :], WLO[slot][:, k, :]
                pe.matmul(PS[:, bank, 0:n], wh, hi(k), start=(first and x == 0), stop=False)
                pe.matmul(PS[:, bank, 0:n], wh, lo(k), start=False, stop=False)
                ins = pe.matmul(PS[:, bank, 0:n], wl, hi(k), start=False, stop=(last and x == len(ks) - 1))
            return ins

        def column_unit(HI, LO):
            use()
            slot = unit.n % HL
            for t0, n in BLOCKS:
                b = open_bank()
                product(b, n, slot, lambda k: HI[:, k, t0:t0 + n], lambda k: LO[:, k, t0:t0 + n]).then_inc(q.next(), 1)
            unit.n += 1

        def stats():
            rs.n += 1
            pe.wait_ge(S["sq_ready"], sq.take())
            for t0, n in BLOCKS:
                b = misc_bank()
                pe.matmul(PS[:, b, 0:n], ONES[:], SQS[:, t0:t0 + n], start=True, stop=True).then_inc(m.next(), 1)

        def rstd_tokens():
            pe.wait_ge(S["rstd_ready"], rs.n)
            b = misc_bank()
            for j in range(NT):
                n = tokens(j)
                ins = pe.matmul(PS[0:n, b, j:j + 1], RSTD[:, j * P:j * P + n], IDF[:, 0:1], start=True, stop=True)
            ins.then_inc(m.next(), 1)

        sq, rs = Count(), Count()

        def gate_project(ready, count, Y):
            pe_ready = [False]
            for j in range(4):
                for h in range(2):
                    use()
                    slot = unit.n % HL
                    for t0, n in BLOCKS:
                        b = open_bank()
                        product(b, n, slot, lambda k: XHI[:, k, t0:t0 + n], lambda k: XLO[:, k, t0:t0 + n]).then_inc(q.next(), 1)
                        if not pe_ready[0]:
                            pe.wait_ge(S[ready], count)
                            pe_ready[0] = True
                        if h == 0 and t0 == 0:
                            pe.wait_ge(S[f"pw_ready{pw.n % 2}"], (pw.n // 2 + 1) * 16)
                        b = open_bank()
                        for k in range(2):
                            ins = pe.matmul(PS[:, b, 0:n], PW[pw.n % 2][:, k, h * P:(h + 1) * P], Y[:, k, t0:t0 + n], start=(k == 0), stop=(k == 1))
                        ins.then_inc(q.next(), 1)
                    unit.n += 1
                pw.n += 1

        def states_in():
            pe.wait_ge(S["st_loaded"], 64 * (l + 1))
            b = misc_bank()
            for c in range(2):
                for h in range(2):
                    x = (c * 2 + h) * 120
                    ins = pe.transpose(PS[:, b, x:x + 120], ST[:, h, c * P:(c + 1) * P], IDF[0:120, 0:120])
            ins.then_inc(m.next(), 1)
            b = misc_bank()
            for c in range(2):
                pe.transpose(PS[:, b, c * 120:c * 120 + 120], ST[:, 2, c * P:(c + 1) * P], IDF[0:120, 0:120])
                ins = pe.transpose(PS[:, b, 240 + c * 16:256 + c * 16], ST[0:16, 3, c * P:(c + 1) * P], IDF[0:16, 0:16])
            ins.then_inc(m.next(), 1)

        so = Count()

        def states_out(buf, tmp, pad):
            rows = NSEQ * pad
            lots = -(-rows // 120)
            pe.wait_ge(S["tok_ready"], so.take())
            for h in range(lots):
                n = rows // lots
                b = misc_bank()
                for c in range(2):
                    ins = pe.transpose(PS[0:n, b, c * P:(c + 1) * P], tmp[:, c, h * n:(h + 1) * n], IDF[:])
                ins.then_inc(m.next(), 1)
            b = misc_bank()
            for c in range(2):
                ins = pe.transpose(PS[0:pad, b, c * P:(c + 1) * P], buf[:, c, SEQ:SEQ + pad], IDF[:])
            ins.then_inc(m.next(), 1)

        def down(hi, lo, blocks):
            use(2)
            s0, s1 = unit.n % HL, (unit.n + 1) % HL
            for d in range(KC):
                for t0, n in blocks:
                    b = open_bank()
                    for f, s in enumerate((s0, s1)):
                        pe.matmul(PS[:, b, 0:n], WHI[s][:, d, :], hi[:, f, t0:t0 + n], start=(f == 0), stop=False)
                        pe.matmul(PS[:, b, 0:n], WHI[s][:, d, :], lo[:, f, t0:t0 + n], start=False, stop=False)
                        ins = pe.matmul(PS[:, b, 0:n], WLO[s][:, d, :], hi[:, f, t0:t0 + n], start=False, stop=(f == 1))
                    ins.then_inc(q.next(), 1)
            unit.n += 2

        pe.wait_ge(S["consts"], 3)
        pe.wait_ge(S["x_loaded"], 16 * NT)
        for c in range(KC):
            for t0, n in BLOCKS:
                b = misc_bank()
                for j in range(t0 // P, -(-(t0 + n) // P)):
                    w = tokens(j)
                    ins = pe.transpose(PS[:, b, j * P - t0:j * P - t0 + w], XIN[0:w, j, c * P:(c + 1) * P], IDF[0:w, 0:w])
                ins.then_inc(m.next(), 1)
        pe.wait_ge(S["par_loaded"], 16 * (7 + 12))
        b = misc_bank()
        for l in range(DEPTH):
            for c in range(2):
                pe.transpose(PS[:, b, (l * 2 + c) * 38:(l * 2 + c) * 38 + 38], PRS[:, l, c * P:(c + 1) * P], IDF[0:38, 0:38])
        pe.transpose(PS[:, b, 152:152 + 7 * KC], NRS[:], IDF[0:7 * KC, 0:7 * KC]).then_inc(m.next(), 1)

        for l in range(DEPTH):
            stats()
            column_unit(XHI, XLO)
            column_unit(XHI, XLO)
            rstd_tokens()
            use(2)
            for j in range(NT):
                n = tokens(j)
                b = misc_bank()
                for h in range(2):
                    s = (unit.n + h) % HL
                    for k in range(KC):
                        xh, xl = XHI[:, k, j * P:j * P + n], XLO[:, k, j * P:j * P + n]
                        pe.matmul(PS[0:n, b, h * P:(h + 1) * P], xh, WHI[s][:, k, :], start=(k == 0), stop=False)
                        pe.matmul(PS[0:n, b, h * P:(h + 1) * P], xl, WHI[s][:, k, :], start=False, stop=False)
                        ins = pe.matmul(PS[0:n, b, h * P:(h + 1) * P], xh, WLO[s][:, k, :], start=False, stop=(k == KC - 1))
                ins.then_inc(m.next(), 1)
            unit.n += 2
            pe.wait_ge(S["sgu_loaded"], 16 * (1 + NSEQ + GROUPS + 2) * (l + 1))
            b = misc_bank()
            for q4 in range(GROUPS):
                ins = pe.transpose(PS[:, b, q4 * P:(q4 + 1) * P], SWRAW[:, q4, :], IDF[:])
            ins.then_inc(m.next(), 1)
            b = misc_bank()
            for q4 in range(GROUPS):
                ins = pe.transpose(PS[0:64, b, q4 * 64:(q4 + 1) * 64], BDRAW[:, q4, :], IDF[0:64, 0:64])
            ins.then_inc(m.next(), 1)
            states_in()
            for _ in range(4):
                column_unit(XHI, XLO)
            pe.wait_ge(S["v_ready"], l + 1)
            for c in range(2):
                for jj in range(2):
                    b = misc_bank()
                    for j in range(4 * jj, 4 * jj + 4):
                        for h in range(2):
                            g4 = 2 * c + h
                            ins = pe.matmul(PS[64 * h:64 * h + 64, b, (j % 4) * P:(j % 4 + 1) * P], V[:, j, g4 * 64:g4 * 64 + 64], WT[:, g4, :],
                                            start=True, stop=True)
                    ins.then_inc(m.next(), 1)
            b = misc_bank()
            for c in range(2):
                for h in range(2):
                    g4 = 2 * c + h
                    ins = pe.matmul(PS[64 * h:64 * h + 64, b, c * 64:c * 64 + 64], V[0:64, NT - 1, g4 * 64:g4 * 64 + 64], BD[:, g4, :],
                                    start=True, stop=True)
            ins.then_inc(m.next(), 1)
            states_out(GLU, YB, PB)
            gate_project("br_d", l + 1, UB)
            for _ in range(4):
                column_unit(XHI, XLO)
            states_out(ZA, YA, PA)
            column_unit(XHI, XLO)
            column_unit(XHI, XLO)
            gate_project("br_a", l + 1, YA)
            pe.wait_ge(S["yb_ready"], l + 1)
            for t0, n in BLOCKS:
                b = misc_bank()
                for k in range(2):
                    ins = pe.matmul(PS[:, b, 0:n], ONES[:], YB[:, k, t0:t0 + n], start=(k == 0), stop=(k == 1))
                ins.then_inc(m.next(), 1)
            column_unit(XHI, XLO)
            column_unit(XHI, XLO)
            pe.wait_ge(S["lnsq_ready"], l + 1)
            for t0, n in BLOCKS:
                b = misc_bank()
                for k in range(2):
                    ins = pe.matmul(PS[:, b, 0:n], ONES[:], SQB[:, k, t0:t0 + n], start=(k == 0), stop=(k == 1))
                ins.then_inc(m.next(), 1)
            states_out(ZP, YP, PC)
            gate_project("br_b", l + 1, YB)
            pe.wait_ge(S["pooled"], l + 1)
            pe.wait_ge(S["pbd_loaded"], 64 * (l + 1))
            for c in range(2):
                for t0, n in BLOCKS:
                    b = misc_bank()
                    pe.matmul(PS[:, b, 0:n], PBD[:, c, :], YP[:, c, t0:t0 + n], start=True, stop=True).then_inc(m.next(), 1)
            gate_project("br_c", l + 1, YP)
            pe.wait_ge(S["mixed_ready"], l + 1)
            for _ in range(KC):
                column_unit(MHI, MLO)
            stats()
            if l == 0:
                hs = Count()

                def step(kind, g):
                    if kind == "GU":
                        for _ in range(4):
                            column_unit(XHI, XLO)
                    else:
                        pe.wait_ge(S["split_done"], hs.take(2 * 3))
                        down(HHI[g % 2], HLO[g % 2], BLOCKS)

                hs.n = W_FFN
                head, body, tail = ffn_schedule(FFN_GROUPS, FFN_LOOP)
                for s in head:
                    step(*s)
                with pe.Fori(0, FFN_LOOP) as i:
                    cs = [unit, q, hs]
                    per = {unit: 12, q: 2 * (12 + 24), hs: 12}
                    st = looped(cs, i, per)
                    for s in body:
                        step(*s)
                leave(cs, st, per, FFN_LOOP)
                for s in tail:
                    step(*s)
            else:
                rstd_tokens()
                pe.wait_ge(S["tri_ready"], 1)
                b = misc_bank()
                for j in range(NT):
                    n = tokens(j)
                    for k in range(KC):
                        pe.matmul(PS[0:n, b, j * NE:(j + 1) * NE], XHF[:, k, j * P:j * P + n], RW[:, k, :], start=(k == 0), stop=False)
                        ins = pe.matmul(PS[0:n, b, j * NE:(j + 1) * NE], XLF[:, k, j * P:j * P + n], RW[:, k, :], start=False, stop=(k == KC - 1))
                ins.then_inc(m.next(), 1)
                pe.wait_ge(S["counts_ready"], 1)
                b = misc_bank()
                for j in range(NT):
                    pe.matmul(PS[:, b, j * NE:(j + 1) * NE], TRIS[:], SS[:, j, :], start=True, stop=False)
                    pe.matmul(PS[:, b, j * NE:(j + 1) * NE], ONES[:], CS[:, j, :], start=False, stop=True)
                pe.matmul(PS[:, b, NT * NE:(NT + 1) * NE], ONES[:], TM[:, 0, :], start=True, stop=True).then_inc(m.next(), 1)
                for j in range(NT):
                    n = tokens(j)
                    for h in range(2):
                        b = misc_bank()
                        for k in range(4):
                            pe.matmul(PS[0:n, b, k * P:(k + 1) * P], XHI[:, 4 * h + k, j * P:j * P + n], IDR[:], start=True, stop=False)
                            ins = pe.matmul(PS[0:n, b, k * P:(k + 1) * P], XLO[:, 4 * h + k, j * P:j * P + n], IDR[:], start=False, stop=True)
                        ins.then_inc(m.next(), 1)
                pe.wait_ge(S["items_ready"], 1)
                n_items = pe.value_load(ITEMS[0:1, 2 * SLOTS:2 * SLOTS + 1], min_val=NE, max_val=SLOTS)
                hs = Count()
                hs.n = W_MOE
                cs = [unit, q, m, hs]
                per = {unit: 2 * len(item_kinds), q: MOE_GROUPS * 12, m: 14, hs: KC + 2 * MOE_GROUPS}
                with pe.Fori(0, SLOTS) as it:
                    with pe.If(it < n_items):
                        st = looped(cs, it, per)
                        pe.wait_ge(S["xg_ready"], it * 48 + 48)
                        for k in range(KC):
                            b = misc_bank()
                            for j, (r0, n) in enumerate(XBLK):
                                ins = pe.transpose(PS[:, b, r0:r0 + n], XG[0:n, j, k * P:(k + 1) * P], IDF[0:n, 0:n])
                            ins.then_inc(m.next(), 1)
                        pe.wait_ge(S["split_done"], hs.take(KC))

                        def step(kind, g):
                            if kind == "GU":
                                for _ in range(4):
                                    use()
                                    b = open_bank()
                                    product(b, CAP, unit.n % HL, lambda k: XSH[:, k, :], lambda k: XSL[:, k, :]).then_inc(q.next(), 1)
                                    unit.n += 1
                            else:
                                pe.wait_ge(S["split_done"], hs.take(2))
                                down(EHI[g % 2], ELO[g % 2], ((0, CAP),))

                        head, body, tail = ffn_schedule(MOE_GROUPS, MOE_LOOP)
                        for s in head:
                            step(*s)
                        with pe.Fori(0, MOE_LOOP) as i:
                            cs2 = [unit, q, hs]
                            per2 = {unit: 12, q: 24, hs: 4}
                            st2 = looped(cs2, i, per2)
                            for s in body:
                                step(*s)
                        leave(cs2, st2, per2, MOE_LOOP)
                        for s in tail:
                            step(*s)
                        pe.wait_ge(S["evicted"], q.at(q.n))
                        for j, (r0, n) in enumerate(XBLK):
                            for h in range(2):
                                b = misc_bank()
                                for k in range(4):
                                    ins = pe.transpose(PS[0:n, b, k * P:(k + 1) * P], EACC[:, 4 * h + k, r0:r0 + n], IDF[:])
                                ins.then_inc(m.next(), 1)
                        leave_items(cs, st, per, n_items)
                for j in range(NT):
                    n = tokens(j)
                    pe.wait_ge(S["combined"], j + 1)
                    for h in range(2):
                        b = misc_bank()
                        for k in range(4):
                            c0 = (4 * h + k) * P
                            ins = pe.transpose(PS[:, b, k * P:k * P + n], YG[j % 2][0][0:n, c0:c0 + P], IDF[0:n, 0:n])
                        ins.then_inc(m.next(), 1)
            stats()
            pe.wait_ge(S["p_loaded"], 16 * NT * (l + 1))
            for c in range(2):
                for t0, n in BLOCKS:
                    b = misc_bank()
                    for j in range(t0 // P, -(-(t0 + n) // P)):
                        w = tokens(j)
                        ins = pe.transpose(PS[:, b, j * P - t0:j * P - t0 + w], PTOK[0:w, j, c * P:(c + 1) * P], IDF[0:w, 0:w])
                    ins.then_inc(m.next(), 1)
            gate_project("p_ready", l + 1, PT)
        stats()
        rstd_tokens()
        pe.wait_ge(S["xnew_ready"], 1)
        for j in range(NT):
            n = tokens(j)
            for h in range(2):
                b = misc_bank()
                for k in range(4):
                    ins = pe.transpose(PS[0:n, b, k * P:(k + 1) * P], XNEW[:, 4 * h + k, j * P:j * P + n], IDF[:])
                ins.then_inc(m.next(), 1)

    @block.scalar
    def _(act):
        conv, q, m = Count(S["hi_ready"]), Count(), Count()
        fold, req, split = Count(), Count(S["act_done"]), Count(S["split_hi"])
        kp = [0, kinds]

        def convert(misc=False):
            kind, norm = kp[1][kp[0] // 2]
            kp[0] += 1
            half, tile = conv.n % 2, conv.n // 2
            if norm is not None:
                if half == 0:
                    fold.n += 1
                act.wait_ge(S["folded"], fold.at(fold.n))
            else:
                act.wait_ge(S[f"raw_ready{tile % RAW}"], conv.at(conv.n, 16, 4) + 16)
            if misc:
                act.wait_ge(S["misc_done"], m.at(m.n))
            elif q.n:
                act.wait_ge(S["mm_done"], q.at(q.n))
            act.activation(WHI[conv.n % HL][:], raw_view(tile % RAW, half, kind), ACT.Copy).then_inc(conv.next(), 1)

        def serve(f):
            act.wait_ge(S["act_req"], req.at(req.n + 1))
            f().then_inc(req.next(), 1)

        def split_x(src, j, dst, t0, n, square=True):
            act.wait_ge(S["split_req"], split.at(split.n + 1))
            ins = act.activation(dst, src, ACT.Copy)
            if square:
                ins = act.activation(T[2 + split.n % 2][:, 0:n], src, ACT.Square)
            ins.then_inc(split.next(), 1)

        def norm_sqrt():
            serve(lambda: act.activation(RSTD[:], RSTD[:], ACT.Sqrt, bias=EPSC[:], scale=1.0 / D))

        def sigmoid_steps(flush=0):
            for u in range(KC):
                if u < KC - flush:
                    convert()
                for j, (t0, n) in enumerate(BLOCKS):
                    serve(lambda: act.activation(T[req.n % 2][:, 0:n], T[req.n % 2][:, 0:n], ACT.Sigmoid))
                    q.n += 2

        def plain(units, flush=0):
            for u in range(units):
                if u < units - flush:
                    convert()
                q.n += 3

        def states_out_act(sample, prompt, pad, lots):
            for h in range(lots + 1):
                act.wait_ge(S["stage_full"], so.take())
                n = NSEQ * pad // lots if h < lots else pad
                dst = sample.rearrange("s r c -> (s r) c")[h * n:(h + 1) * n, :] if h < lots else prompt
                act.dma_start(dst, OUTST[0:n, :]).then_inc(S["stage_out"], 16)

        so = Count()
        act.wait_ge(S["consts"], 3)
        for c in range(KC):
            for t0, n in BLOCKS:
                split_x(T[split.n % 2][:, 0:n], 0, XHI[:, c, t0:t0 + n], t0, n)
                m.n += 1
        m.n += 1
        for _ in range(LOOK):
            convert()
        for l in range(DEPTH):
            m.n += 3
            norm_sqrt()
            plain(2)
            m.n += 1
            convert()
            m.n += NT
            serve(lambda: act.activation(VR[:], MV[:, :, 1], ACT.Sqrt, bias=EPSC[:]))
            convert(misc=True)
            act.wait_ge(S["v_ready"], l + 1)
            act.dma_start(O["v_p"][l, 0], V[:, NT - 2, :]).then_inc(S["v_out"], 16)
            act.dma_start(O["v_s"][l].rearrange("s t c -> (s t) c"), V[0:64, NT - 1, :]).then_inc(S["v_out"], 16)
            m.n += 4
            for c in range(2):
                convert()
                q.n += 3
                act.wait_ge(S["act_req"], req.at(req.n + 1))
                gp, gs = GLU[:, c, PB:PB + SEQ], GLU[:, c, PB + SEQ:].rearrange("p (s t) -> p s t", s=NSEQ)[:, :, PB:]
                act.activation(gp, gp, ACT.Sigmoid)
                act.activation(gs, gs, ACT.Sigmoid).then_inc(req.next(), 1)
            plain(2)
            m.n += 5 + 3
            states_out_act(O["b_s"][l], O["b_p"][l, 0], PB, 2)
            sigmoid_steps()
            plain(4)
            m.n += 2
            states_out_act(O["a_s"][l], O["a_p"][l, 0], PA, 1)
            plain(2)
            sigmoid_steps()
            m.n += 3
            plain(2)
            m.n += 3
            serve(lambda: act.activation(SQB[:, 0, :], SQB[:, 0, :], ACT.Sqrt, bias=EPSC[:], scale=1.0 / DB))
            act.wait_ge(S["act_req"], req.at(req.n + 1))
            act.activation(YB[:, 0, :], YB[:, 0, :], ACT.Silu, bias=par(l, 0, R_LB), scale=par(l, 0, R_LG))
            act.activation(YB[:, 1, :], YB[:, 1, :], ACT.Silu, bias=par(l, 1, R_LB), scale=par(l, 1, R_LG)).then_inc(req.next(), 1)
            m.n += 2
            states_out_act(O["c_s"][l], O["c_p"][l, 0], PC, 1)
            sigmoid_steps()
            m.n += 6
            sigmoid_steps()
            for d in range(KC):
                act.wait_ge(S["split_req"], split.at(split.n + 1))
                act.activation(MHI[:, d, :], MIXED[:, d, :], ACT.Copy).then_inc(split.next(), 1)
            for d in range(KC):
                if not (l == 1 and d >= KC - LOOK):
                    convert()
                for t0, n in BLOCKS:
                    split_x(T[split.n % 2][:, 0:n], 0, XHI[:, d, t0:t0 + n], t0, n)
                q.n += 3
            m.n += 3
            norm_sqrt()
            if l == 0:
                def step(kind, g, last=False):
                    if kind == "GU":
                        for f in range(2):
                            convert()
                            q.n += 3
                            for t0, n in BLOCKS:
                                serve(lambda: act.activation(GS[:, f, t0:t0 + n], GS[:, f, t0:t0 + n], ACT.Silu))
                        for f in range(2):
                            convert()
                            q.n += 3
                            for t0, n in BLOCKS:
                                act.wait_ge(S["split_req"], split.at(split.n + 1))
                                act.activation(HHI[g % 2][:, f, t0:t0 + n], T[split.n % 2][:, 0:n], ACT.Copy).then_inc(split.next(), 1)
                    else:
                        convert()
                        if last:
                            for d in range(KC):
                                for t0, n in BLOCKS:
                                    split_x(T[split.n % 2][:, 0:n], 0, XHI[:, d, t0:t0 + n], t0, n)
                        q.n += 24
                        convert()

                head, body, tail = ffn_schedule(FFN_GROUPS, FFN_LOOP)
                for s in head:
                    step(*s)
                cs = [conv, q, fold, req, split]
                per = {conv: 12, q: 72, fold: 4, req: 12, split: 12}
                with act.Fori(0, FFN_LOOP) as i:
                    st = looped(cs, i, per)
                    for s in body:
                        step(*s)
                leave(cs, st, per, FFN_LOOP)
                kp[0] += 12 * (FFN_LOOP - 1)
                for s in tail:
                    step(*s, last=(s == tail[-1]))
            else:
                act.wait_ge(S["phase_clear"], 1)
                for j, (r0, n) in enumerate(XBLK):
                    act.dma_start(YS[PAIRS + r0:PAIRS + r0 + n, :], XG[0:n, j, :]).then_inc(S["ys_out"], 16)
                for k in range(2):
                    serve(lambda: act.activation(TW[:, k, :], TW[:, k, :], ACT.Sigmoid))
                m.n += 1 + 2 + 2 * NT
                act.wait_ge(S["items_ready"], 1)
                n_items = act.value_load(ITEMS[0:1, 2 * SLOTS:2 * SLOTS + 1], min_val=NE, max_val=SLOTS)
                cs = [conv, q, m, req, split]
                per = {conv: 2 * len(item_kinds), q: 12 * MOE_GROUPS, m: 14, req: 2 * MOE_GROUPS, split: KC + 2 * MOE_GROUPS}
                main, kp_main = kinds, kp[0]
                with act.Fori(0, SLOTS) as it:
                    with act.If(it < n_items):
                        row = act.value_load(ITEMS[0:1, bass.ds(it + SLOTS, 1)], min_val=0, max_val=PAIRS)
                        st = looped(cs, it, per)
                        kp[0], kp[1] = 0, item_kinds
                        def conv_left():
                            if kp[0] < 2 * len(item_kinds):
                                convert()

                        for _ in range(LOOK):
                            conv_left()
                        for k in range(KC):
                            act.wait_ge(S["split_req"], split.at(split.n + 1))
                            act.activation(XSH[:, k, :], T[split.n % 2][:, 0:CAP], ACT.Copy).then_inc(split.next(), 1)

                        def step(kind, g):
                            if kind == "GU":
                                for f in range(2):
                                    conv_left()
                                    q.n += 1
                                    serve(lambda: act.activation(EG[:, f, :], EG[:, f, :], ACT.Silu))
                                for f in range(2):
                                    conv_left()
                                    q.n += 1
                                    act.wait_ge(S["split_req"], split.at(split.n + 1))
                                    act.activation(EHI[g % 2][:, f, :], T[split.n % 2][:, 0:CAP], ACT.Copy).then_inc(split.next(), 1)
                            else:
                                conv_left()
                                q.n += KC
                                conv_left()

                        head, body, tail = ffn_schedule(MOE_GROUPS, MOE_LOOP)
                        for s in head:
                            step(*s)
                        cs2 = [conv, q, req, split]
                        per2 = {conv: 12, q: 24, req: 4, split: 4}
                        with act.Fori(0, MOE_LOOP) as i:
                            st2 = looped(cs2, i, per2)
                            for s in body:
                                step(*s)
                        leave(cs2, st2, per2, MOE_LOOP)
                        kp[0] += 12 * (MOE_LOOP - 1)
                        for s in tail:
                            step(*s)
                        m.n += 14
                        for j, (r0, n) in enumerate(XBLK):
                            if j == 0:
                                act.wait_ge(S["ys_out"], it * 48 + 48)
                            act.wait_ge(S["ys_full"], it * 3 + (j + 1))
                            act.dma_start(YS[bass.ds(row + r0, n), :], YT[j % 2][0:n, :]).then_inc(S["ys_out"], 16)
                        leave_items(cs, st, per, n_items)
                kp[0], kp[1] = kp_main, kinds
                for j in range(NT):
                    n = tokens(j)
                    for h in range(2):
                        act.wait_ge(S["split_req"], split.at(split.n + 1))
                        act.activation(XHI[:, 4 * h:4 * h + 4, j * P:j * P + n], TC[h][:, :, 0:n], ACT.Copy)
                        act.activation(TC[2 + h][:, :, 0:n], TC[h][:, :, 0:n], ACT.Square).then_inc(split.next(), 1)
                m.n += 2 * NT
                for _ in range(LOOK):
                    convert()
            m.n += 3
            norm_sqrt()
            m.n += 6
            sigmoid_steps(flush=LOOK if l == 1 else 0)
            for d in range(KC):
                for t0, n in BLOCKS:
                    split_x(XNEW[:, d, t0:t0 + n], 0, XHI[:, d, t0:t0 + n], t0, n)
        norm_sqrt()
        for j in range(NT):
            n = tokens(j)
            act.wait_ge(S["y_full"], j + 1)
            dst = O["y_p"][0, j * P:(j + 1) * P, :] if j < NT - 1 else O["y_s"].rearrange("s t d -> (s t) d")
            act.dma_start(dst, YOUT[j % 2][0:n, :]).then_inc(S[f"outputs{j % 2}"], 16)
        act.wait_ge(S["outputs0"], 16 * ((NT + 1) // 2))
        act.wait_ge(S["outputs1"], 16 * (NT // 2))
        act.wait_ge(S["stage_out"], 16 * 7 * DEPTH)
        act.wait_ge(S["v_out"], 32 * DEPTH)

    @block.vector
    def _(dve):
        v = Engine(dve, S["dve_own"])
        conv, q, m = Count(S["lo_ready"]), Count(S["evicted"]), Count(S["misc_free"])
        req, split = Count(S["act_req"]), Count(S["split_done"])
        sreq = Count(S["split_req"])
        kp = [0, kinds]
        def convert():
            kind, norm = kp[1][kp[0] // 2]
            kp[0] += 1
            dve.wait_ge(S["hi_ready"], conv.at(conv.n + 1))
            s = conv.n % HL
            v.do(dve.tensor_tensor(WLO[s][:], raw_view(conv.n // 2 % RAW, conv.n % 2, kind), WHI[s][:].bitcast(F32), ALU.subtract), conv)

        def main_ready():
            dve.wait_ge(S["mm_done"], q.at(q.n + 1))
            return PS[:, q.n % BANKS, :]

        def misc_ready():
            dve.wait_ge(S["misc_done"], m.at(m.n + 1))
            return PS[:, 6 + m.n % 2, :]

        def split_x(d, j, src, in1=None):
            t0, n = BLOCKS[j]
            dve.wait_ge(S["split_hi"], sreq.at(sreq.n))
            w = sreq.n - 1
            v.do(dve.tensor_tensor(XLO[:, d, t0:t0 + n], src, XHF[:, d, t0:t0 + n], ALU.subtract))
            sq = T[2 + w % 2][:, 0:n]
            if d == 0:
                v.do(dve.tensor_copy(SQS[:, t0:t0 + n], sq), split)
            else:
                v.do(dve.tensor_tensor(SQS[:, t0:t0 + n], SQS[:, t0:t0 + n], sq, ALU.add), split)
            v.sync()

        def norm():
            for t0, n in BLOCKS:
                ps = misc_ready()
                v.do(dve.tensor_copy(RSTD[:, t0:t0 + n], ps[:, 0:n]), m)
            request()
            v.do(dve.reciprocal(RSTD[:], RSTD[:]), rst)
            v.sync()

        rst = Count(S["rstd_ready"])

        def norm_tokens():
            ps = misc_ready()
            v.do(dve.tensor_copy(RTOK[:, 0:NT - 1], ps[:, 0:NT - 1]))
            v.do(dve.tensor_copy(RTOK[0:64, NT - 1:NT], ps[0:64, NT - 1:NT]), m)
            v.sync()

        def request():
            v.sync()
            dve.sem_inc(req.next(), 1)
            dve.wait_ge(S["act_done"], req.at(req.n))

        bg = [iter(())]

        def background(k):
            for _ in range(k):
                next(bg[0], None)

        def gate_project(br_first, br_pulls):
            for d in range(KC):
                convert()
                for t0, n in BLOCKS:
                    ps = main_ready()
                    t = T[req.n % 2][:, 0:n]
                    v.do(dve.tensor_tensor(t, ps[:, 0:n], RSTD[:, t0:t0 + n], ALU.mult), q)
                    v.sync()
                    dve.sem_inc(req.next(), 1)
                    background(br_pulls)
                    ps = main_ready()
                    dve.wait_ge(S["act_done"], req.at(req.n))
                    dst = MIXED[:, d, t0:t0 + n]
                    if br_first:
                        v.do(dve.tensor_tensor(dst, ps[:, 0:n], t, ALU.mult), q)
                        v.sync()
                    else:
                        mk = v.do(dve.tensor_tensor(t, ps[:, 0:n], t, ALU.mult), q)
                        v.sync(mk)
                        v.do(dve.tensor_tensor(dst, dst, t, ALU.add))
                        v.sync()

        def padded_unit(buf, pad, c, times=False, tmp=[0]):
            convert()
            for j, (t0, n) in enumerate(BLOCKS):
                ps = main_ready()
                ps_r = ps
                if times:
                    t = T[2 + tmp[0] % 2]
                    tmp[0] += 1
                    v.do(dve.tensor_tensor(t[:, 0:n], ps[:, 0:n], RSTD[:, t0:t0 + n], ALU.mult), q)
                    v.sync()
                    for a, b, dst in pieces(j, buf[:, c, :], pad):
                        v.do(dve.tensor_tensor(dst, dst, shaped(t[:, a:a + b], dst), ALU.mult))
                    v.sync()
                else:
                    ds = pieces(j, buf[:, c, :], pad)
                    for x, (a, b, dst) in enumerate(ds):
                        v.do(dve.tensor_tensor(dst, shaped(ps[:, a:a + b], dst), shaped(RSTD[:, t0 + a:t0 + a + b], dst), ALU.mult),
                             q if x == len(ds) - 1 else None)
                background(1)
            v.sync()

        def pad_sample(buf, c, pad):
            return buf[:, c, pad + SEQ:].rearrange("p (s t) -> p s t", s=NSEQ)

        def states_out(buf, tmp, pad, lots):
            for c in range(2):
                x = pad_sample(buf, c, pad)[:, :, DSEQ:]
                v.do(dve.tensor_copy(tmp[:, c, 0:NSEQ * pad].rearrange("p (s t) -> p s t", s=NSEQ), x), tok if c == 1 else None)
            for h in range(lots + 1):
                n = NSEQ * pad // lots if h < lots else pad
                ps = misc_ready()
                if stage.n:
                    dve.wait_ge(S["stage_out"], 16 * stage.n)
                v.do(dve.tensor_copy(OUTST[0:n, :], ps[0:n, 0:DB]), stage)
                v.sync()
                dve.sem_inc(m.next(), 1)

        tok, stage = Count(S["tok_ready"]), Count(S["stage_full"])

        for t_, val in ((ONES, 1.0), (EPSC, EPS)):
            v.do(dve.memset(t_[:], val))
        v.do(dve.memset(BDRAW[:], 0.0))
        v.do(dve.memset(PBD[:], 0.0))
        for c in range(2):
            for h in range(2):
                v.do(dve.memset(WIN[64 * h:64 * h + 64, c:c + 1], float(WINDOWS[2 * c + h])))
        v.sync()
        dve.sem_inc(S["sgu_zeroed"], 1)
        v.do(dve.reciprocal(WINV[:], WIN[:]))
        dve.wait_ge(S["consts"], 3)
        v.do(dve.tensor_copy(IDR[:], IDF[:]))
        for c in range(2):
            v.do(dve.tensor_scalar(FIXT[:, c, :], FIXT[:, c, :], WIN[:, c:c + 1], None, ALU.min))
        v.sync()
        v.do(dve.reciprocal(FIXT[:], FIXT[:]))
        v.sync()
        sqc = Count(S["sq_ready"])
        for c in range(KC):
            for j, (t0, n) in enumerate(BLOCKS):
                ps = misc_ready()
                t = T[sreq.n % 2][:, 0:n]
                v.do(dve.tensor_copy(t, ps[:, 0:n]), m)
                v.sync()
                dve.sem_inc(sreq.next(), 1)
                split_x(c, j, t)
        dve.sem_inc(sqc.next(), 1)
        ps = misc_ready()
        v.do(dve.tensor_copy(PAR[:], ps[:, 0:4 * 38 + 7 * KC]), m)
        v.sync()
        dve.sem_inc(S["par_ready"], 1)
        for _ in range(LOOK):
            convert()

        for l in range(DEPTH):
            norm()
            v.do(dve.memset(MV[:], 1.0))
            for c in range(2):
                convert()
                for t0, n in BLOCKS:
                    ps = main_ready()
                    v.do(dve.tensor_tensor(UB[:, c, t0:t0 + n], ps[:, 0:n], RSTD[:, t0:t0 + n], ALU.mult), q)
            norm_tokens()
            convert()
            for j in range(NT):
                n = tokens(j)
                ps = misc_ready()
                v.do(dve.tensor_scalar(V[0:n, j, :], ps[0:n, 0:DB], RTOK[0:n, j:j + 1], None, ALU.mult), m)
                v.sync()
                v.do(dve.bn_stats(BNS[0:n, j, :], V[0:n, j, :]))
                v.sync()
                v.do(dve.bn_aggr(MV[0:n, j, :], BNS[0:n, j, :]))
            v.sync()
            dve.sem_inc(req.next(), 1)
            dve.wait_ge(S["act_done"], req.at(req.n))
            v.do(dve.reciprocal(VR[:], VR[:]))
            v.sync()
            for j in range(NT):
                n = tokens(j)
                v.do(dve.tensor_scalar(V[0:n, j, :], V[0:n, j, :], MV[0:n, j, 0:1], VR[0:n, j:j + 1], ALU.subtract, ALU.mult))
            v.sync()
            dve.wait_ge(S["sgu_loaded"], 16 * (1 + NSEQ + GROUPS + 2) * (l + 1))
            for j in range(NT):
                n = tokens(j)
                v.do(dve.tensor_tensor(V[0:n, j, :], V[0:n, j, :], LNG[0:n, :], ALU.mult))
            v.sync()
            for j in range(NT):
                n = tokens(j)
                v.do(dve.tensor_tensor(V[0:n, j, :], V[0:n, j, :], LNB[0:n, :], ALU.add))
            v.sync()
            dve.sem_inc(S["v_ready"], 1)
            convert()
            ps = misc_ready()
            v.do(dve.tensor_tensor(WT[:], ps.rearrange("p (g t) -> p g t", g=GROUPS), TRIL[:].unsqueeze(1).to_broadcast([P, GROUPS, P]),
                                   ALU.mult), m)
            ps = misc_ready()
            v.do(dve.tensor_tensor(BD[:], ps[0:64, 0:GROUPS * 64].rearrange("p (g t) -> p g t", g=GROUPS),
                                   TRIL[0:64, 0:64].unsqueeze(1).to_broadcast([64, GROUPS, 64]), ALU.mult), m)
            v.do(dve.memset(GLU[:, :, 0:PB], 0.0))
            ps = misc_ready()
            for c in range(2):
                for h in range(2):
                    x = (c * 2 + h) * 120
                    v.do(dve.tensor_copy(pad_sample(GLU, c, PB)[:, 4 * h:4 * h + 4, 0:PB], ps[:, x:x + 120].rearrange("p (s t) -> p s t", s=4)),
                         m if (c, h) == (1, 1) else None)
            ps = misc_ready()
            v.do(dve.tensor_copy(KEEP[:], ps[:, 0:272]), m)
            v.sync()
            for c in range(2):
                padded_unit(GLU, PB, c)
                dve.sem_inc(req.next(), 1)
                dve.wait_ge(S["act_done"], req.at(req.n))
            for c in range(2):
                padded_unit(GLU, PB, c, times=True)
            for c in range(2):
                for jj in range(2):
                    ps = misc_ready()
                    t4 = YB[:, c, jj * 512:jj * 512 + 512]
                    v.do(dve.tensor_tensor(t4.rearrange("p (j t) -> p j t", j=4), ps.rearrange("p (j t) -> p j t", j=4),
                                           BIAS[:, c, :].unsqueeze(1).to_broadcast([P, 4, P]), ALU.add), m)
                    v.sync()
                    u4 = UB[:, c, jj * 512:jj * 512 + 512]
                    v.do(dve.tensor_tensor(u4, u4, t4, ALU.mult))
            ps = misc_ready()
            for c in range(2):
                v.do(dve.tensor_tensor(YB[:, c, SEQ:].rearrange("p (s t) -> p s t", s=NSEQ), ps[:, c * 64:c * 64 + 64].rearrange("p (s t) -> p s t", s=NSEQ),
                                       BIAS[:, c, 0:DSEQ].unsqueeze(1).to_broadcast([P, NSEQ, DSEQ]), ALU.add), m if c else None)
            v.sync()
            v.do(dve.tensor_tensor(UB[:, :, SEQ:], UB[:, :, SEQ:], YB[:, :, SEQ:], ALU.mult))
            v.sync()
            dve.sem_inc(S["br_d"], 1)
            states_out(GLU, YB, PB, 2)

            def conv_b():
                parts = []
                for c in range(2):
                    parts.append((c, lambda k, c=c: GLU[:, c, k:k + SEQ], YB[:, c, 0:SEQ]))
                    parts.append((c, lambda k, c=c: pad_sample(GLU, c, PB)[:, :, k:k + DSEQ], YB[:, c, SEQ:].rearrange("p (s t) -> p s t", s=NSEQ)))
                marks = [None] * 4
                for k in range(PB + 1):
                    for x, (c, src, dst) in enumerate(parts):
                        w = par(l, c, R_CB + k)
                        if k == 0:
                            marks[x] = v.do(dve.tensor_scalar(dst, src(k), w, par(l, c, R_BIAS), ALU.mult, ALU.add))
                        else:
                            v.sync(marks[x])
                            marks[x] = v.do(dve.scalar_tensor_tensor(dst, src(k), w, dst, ALU.mult, ALU.add))
                        yield

            bg[0] = conv_b()
            dve.wait_ge(S["v_out"], 32 * (l + 1))
            gate_project(True, 2)
            v.do(dve.memset(ZA[:, :, 0:PA], 0.0))
            for c in range(2):
                v.do(dve.tensor_copy(pad_sample(ZA, c, PA)[:, :, 0:PA], KEEP[:, 240 + c * 16:256 + c * 16].rearrange("p (s t) -> p s t", s=NSEQ)))
            for c in range(2):
                padded_unit(ZA, PA, c)
            for c in range(2):
                padded_unit(ZA, PA, c, times=True)
            states_out(ZA, YA, PA, 1)
            for k in range(PA + 1):
                for c in range(2):
                    for src, dst in ((ZA[:, c, k:k + SEQ], YA[:, c, 0:SEQ]),
                                     (pad_sample(ZA, c, PA)[:, :, k:k + DSEQ], YA[:, c, SEQ:].rearrange("p (s t) -> p s t", s=NSEQ))):
                        w = par(l, c, R_CA + k)
                        if k == 0:
                            v.do(dve.tensor_scalar(dst, src, w, None, ALU.mult))
                        else:
                            v.do(dve.scalar_tensor_tensor(dst, src, w, dst, ALU.mult, ALU.add))
                v.sync()
            for c in range(2):
                convert()
                for t0, n in BLOCKS:
                    ps = main_ready()
                    t = T[2]
                    v.do(dve.tensor_tensor(t[:, 0:n], ps[:, 0:n], RSTD[:, t0:t0 + n], ALU.mult), q)
                    v.sync()
                    v.do(dve.tensor_tensor(YA[:, c, t0:t0 + n], YA[:, c, t0:t0 + n], t[:, 0:n], ALU.mult))
                    v.sync()
            dve.sem_inc(S["br_a"], 1)
            gate_project(False, 3)
            for _ in bg[0]:
                pass
            v.sync()
            dve.sem_inc(S["yb_ready"], 1)
            for t0, n in BLOCKS:
                ps = misc_ready()
                for c in range(2):
                    v.do(dve.scalar_tensor_tensor(YB[:, c, t0:t0 + n], ps[:, 0:n], -1.0 / DB, YB[:, c, t0:t0 + n], ALU.mult, ALU.add), m if c else None)
                v.sync()
                v.do(dve.tensor_tensor(SQB[:, :, t0:t0 + n], YB[:, :, t0:t0 + n], YB[:, :, t0:t0 + n], ALU.mult))
            v.sync()
            dve.sem_inc(S["lnsq_ready"], 1)
            v.do(dve.memset(ZP[:, :, 0:PC], 0.0))
            for c in range(2):
                v.do(dve.tensor_copy(pad_sample(ZP, c, PC)[:, :, 0:PC], KEEP[:, c * 120:c * 120 + 120].rearrange("p (s t) -> p s t", s=NSEQ)))
            for c in range(2):
                padded_unit(ZP, PC, c)
            for t0, n in BLOCKS:
                ps = misc_ready()
                v.do(dve.tensor_copy(SQB[:, 0, t0:t0 + n], ps[:, 0:n]), m)
            v.sync()
            dve.sem_inc(req.next(), 1)
            dve.wait_ge(S["act_done"], req.at(req.n))
            v.do(dve.reciprocal(SQB[:, 0, :], SQB[:, 0, :]))
            v.sync()
            for c in range(2):
                v.do(dve.tensor_tensor(YB[:, c, :], YB[:, c, :], SQB[:, 0, :], ALU.mult))
            v.sync()
            dve.sem_inc(req.next(), 1)
            dve.wait_ge(S["act_done"], req.at(req.n))
            dve.sem_inc(S["br_b"], 1)
            states_out(ZP, YP, PC, 1)

            def pool_c():
                def at_(c, s, h):
                    a, b = (64 * h if h is not None else 0), (64 * h + 64 if h is not None else P)
                    return ((ZP[a:b, c, PC - s:PC - s + SEQ], YP[a:b, c, 0:SEQ]),
                            (pad_sample(ZP, c, PC)[a:b, :, PC - s:PC - s + DSEQ], YP[a:b, c, SEQ:].rearrange("p (s t) -> p s t", s=NSEQ)))
                last = [None, None]
                for s in range(1, POOL_MAX):
                    for c in range(2):
                        w0, w1 = WINDOWS[2 * c], WINDOWS[2 * c + 1]
                        if s >= w1:
                            continue
                        h = None if s < w0 else 1
                        if last[c]:
                            v.sync(last[c])
                        for x, (src, dst) in enumerate(at_(c, s, h)):
                            first = at_(c, 0, h)[x][0] if s == 1 else dst
                            last[c] = v.do(dve.tensor_tensor(dst, first, src, ALU.add))
                            yield
                v.sync()
                for c in range(2):
                    v.do(dve.tensor_tensor(YP[:, c, 0:16], YP[:, c, 0:16], FIXT[:, c, :], ALU.mult))
                    (src, dst), (ssrc, sdst) = at_(c, 0, None)
                    v.do(dve.scalar_tensor_tensor(dst[:, 16:], dst[:, 16:], WINV[:, c:c + 1], src[:, 16:], ALU.mult, ALU.subtract))
                    v.do(dve.scalar_tensor_tensor(sdst, sdst, WINV[:, c:c + 1], ssrc, ALU.mult, ALU.subtract))
                    yield
                v.sync()
                for c in range(2):
                    v.do(dve.tensor_tensor(YP[:, c, 0:16], YP[:, c, 0:16], ZP[:, c, PC:PC + 16], ALU.subtract))
                v.sync()
                yield

            bg[0] = pool_c()
            gate_project(False, 2)
            for _ in bg[0]:
                pass
            v.sync()
            dve.sem_inc(S["pooled"], 1)
            for c in range(2):
                for t0, n in BLOCKS:
                    ps = misc_ready()
                    v.do(dve.tensor_scalar(YP[:, c, t0:t0 + n], ps[:, 0:n], par(l, c, R_PS), None, ALU.mult), m)
            v.sync()
            dve.sem_inc(S["br_c"], 1)
            gate_project(False, 0)
            for d in range(KC):
                dve.sem_inc(sreq.next(), 1)
            for d in range(KC):
                dve.wait_ge(S["split_hi"], sreq.at(sreq.n - KC + d + 1))
                v.do(dve.tensor_tensor(MLO[:, d, :], MIXED[:, d, :], MHI[:, d, :].bitcast(F32), ALU.subtract), split)
            v.sync()
            dve.sem_inc(S["mixed_ready"], 1)
            for d in range(KC):
                if not (l == 1 and d >= KC - LOOK):
                    convert()
                for j, (t0, n) in enumerate(BLOCKS):
                    ps = main_ready()
                    t = T[sreq.n % 2][:, 0:n]
                    v.do(dve.tensor_tensor(t, ps[:, 0:n], XHF[:, d, t0:t0 + n], ALU.add), q)
                    v.sync()
                    v.do(dve.tensor_tensor(t, t, XLF[:, d, t0:t0 + n], ALU.add))
                    v.sync()
                    dve.sem_inc(sreq.next(), 1)
                    split_x(d, j, t)
            dve.sem_inc(sqc.next(), 1)
            norm()
            dve.wait_ge(S["stage_out"], 16 * stage.n)
            if l == 0:
                for d in range(KC):
                    v.do(dve.tensor_tensor(ACC[:, d, :], XHF[:, d, :], XLF[:, d, :], ALU.add))
                v.sync()

                def step(kind, g, last=False):
                    if kind == "GU":
                        for f in range(2):
                            convert()
                            for t0, n in BLOCKS:
                                ps = main_ready()
                                v.do(dve.tensor_tensor(GS[:, f, t0:t0 + n], ps[:, 0:n], RSTD[:, t0:t0 + n], ALU.mult), q)
                                v.sync()
                                dve.sem_inc(req.next(), 1)
                        for f in range(2):
                            convert()
                            for j, (t0, n) in enumerate(BLOCKS):
                                ps = main_ready()
                                t = T[sreq.n % 2][:, 0:n]
                                if f == 0 and j == 0:
                                    dve.wait_ge(S["act_done"], req.at(req.n))
                                v.do(dve.tensor_tensor(t, ps[:, 0:n], RSTD[:, t0:t0 + n], ALU.mult), q)
                                v.sync()
                                v.do(dve.tensor_tensor(t, t, GS[:, f, t0:t0 + n], ALU.mult))
                                v.sync()
                                dve.sem_inc(sreq.next(), 1)
                                dve.wait_ge(S["split_hi"], sreq.at(sreq.n))
                                v.do(dve.tensor_tensor(HLO[g % 2][:, f, t0:t0 + n], t, HHI[g % 2][:, f, t0:t0 + n].bitcast(F32), ALU.subtract), split)
                                v.sync()
                    else:
                        convert()
                        for d in range(KC):
                            for j, (t0, n) in enumerate(BLOCKS):
                                ps = main_ready()
                                if last:
                                    t = T[sreq.n % 2][:, 0:n]
                                    v.do(dve.tensor_tensor(t, ps[:, 0:n], ACC[:, d, t0:t0 + n], ALU.add), q)
                                    v.sync()
                                    dve.sem_inc(sreq.next(), 1)
                                    split_x(d, j, t)
                                else:
                                    a = ACC[:, d, t0:t0 + n]
                                    v.do(dve.tensor_tensor(a, ps[:, 0:n], a, ALU.add), q)
                        v.sync()
                        convert()

                head, body, tail = ffn_schedule(FFN_GROUPS, FFN_LOOP)
                for s in head:
                    step(*s)
                cs = [conv, q, req, split, sreq, v.own]
                per = {conv: 12, q: 72, req: 12, split: 12, sreq: 12, v.own: 12}
                with dve.Fori(0, FFN_LOOP) as i:
                    st = looped(cs, i, per)
                    for s in body:
                        step(*s)
                leave(cs, st, per, FFN_LOOP)
                kp[0] += 12 * (FFN_LOOP - 1)
                for s in tail:
                    step(*s, last=(s == tail[-1]))
                dve.sem_inc(sqc.next(), 1)
            else:
                v.do(dve.memset(XG[:], 0.0))
                v.sync()
                dve.sem_inc(S["phase_clear"], 1)
                v.do(dve.tensor_tensor(TRIS[:], TRIL[:], IDF[:], ALU.subtract))
                v.do(dve.memset(LG[:], 0.0))
                dve.wait_ge(S["rw_loaded"], 16)
                v.do(dve.tensor_tensor(RW[:], RW[:], gain(3).unsqueeze(2).to_broadcast([P, KC, NE]), ALU.mult))
                norm_tokens()
                dve.sem_inc(S["tri_ready"], 1)
                ps = misc_ready()
                full, rest = NT - 1, tokens(NT - 1)
                v.do(dve.tensor_tensor(LG[:, 0:full, :], ps[:, 0:full * NE].rearrange("p (j e) -> p j e", e=NE),
                                       RTOK[:, 0:full].unsqueeze(2).to_broadcast([P, full, NE]), ALU.mult))
                v.do(dve.tensor_scalar(LG[0:rest, full, :], ps[0:rest, full * NE:NT * NE], RTOK[0:rest, full:NT], None, ALU.mult), m)
                v.sync()
                for j in range(NT):
                    v.do(dve.max(MX[:, j, :], LG[:, j, :]))
                v.sync()
                for j in range(NT):
                    v.do(dve.max_index(IX[:, j, :], MX[:, j, :], LG[:, j, :]))
                for k in range(2):
                    v.do(dve.tensor_tensor(TW[:, k, :], MX[:, :, k], MX[:, :, 1 - k], ALU.subtract))
                v.sync()
                dve.sem_inc(req.next(), 1)
                request()
                v.do(dve.tensor_copy(IXF[:], IX[:]))
                v.sync()
                dve.wait_ge(S["consts"], 5)
                for k in range(2):
                    v.do(dve.tensor_tensor(OH[k][:], IOT[:].unsqueeze(1).to_broadcast([P, NT, NE]),
                                           IXF[:, :, k:k + 1].to_broadcast([P, NT, NE]), ALU.is_equal))
                v.sync()
                v.do(dve.tensor_tensor(SS[:], OH[0][:], OH[1][:], ALU.add))
                v.do(dve.memset(CS[:, 0, :], 0.0))
                v.sync()
                v.do(dve.memset(SS[rest:P, full, :], 0.0))
                v.sync()
                for j in range(1, NT + 1):
                    v.do(dve.tensor_tensor(CS[:, j, :] if j < NT else TM[:, 0, :], CS[:, j - 1, :], SS[:, j - 1, :], ALU.add))
                    v.sync()
                dve.sem_inc(S["counts_ready"], 1)
                ps = misc_ready()
                v.do(dve.tensor_copy(CNT[:], ps[:, NT * NE:(NT + 1) * NE]))
                v.do(dve.memset(BASE[:, 0:1], 0.0))
                v.sync()
                for e in range(1, NE):
                    v.do(dve.tensor_tensor(BASE[:, e:e + 1], BASE[:, e - 1:e], CNT[:, e - 1:e], ALU.add))
                    v.sync()
                v.do(dve.tensor_tensor(TM[:], ps[:, 0:NT * NE].rearrange("p (j e) -> p j e", e=NE),
                                       BASE[:].unsqueeze(1).to_broadcast([P, NT, NE]), ALU.add), m)
                v.sync()
                for k in range(2):
                    v.do(dve.tensor_tensor(OH[k][:], OH[k][:], TM[:], ALU.mult))
                v.sync()
                for k in range(2):
                    v.do(dve.tensor_reduce(POSF[:, k, :], OH[k][:], AXX, ALU.add))
                v.sync()
                v.do(dve.tensor_copy(POSI[:], POSF[:]))
                v.sync()
                for j in range(NT):
                    n = tokens(j)
                    if j >= 2:
                        dve.wait_ge(S[f"rows_gone{j % 2}"], 32 * (j // 2))
                    for h in range(2):
                        ps = misc_ready()
                        v.do(dve.tensor_scalar(YT[j % 2][0:n, h * 512:h * 512 + 512], ps[0:n, :], RTOK[0:n, j:j + 1], None, ALU.mult), m)
                    v.sync()
                    dve.sem_inc(S["rows_ready"], 1)
                lrow = lambda r: LROW[0:1, r, :]
                further = lambda r, p_: LROW[0:1, r, 0:NE * EXTRA].rearrange("o (e x) -> o e x", x=EXTRA)[:, :, p_ - 1]
                firsts = lambda r: LROW[0:1, r, NE * EXTRA:NJ]
                ACTIVE, PLACE, EXPERT, ROW, OTHER = range(5)
                for p_ in range(1, EXTRA + 1):
                    v.do(dve.tensor_scalar(further(ACTIVE, p_), CNT[0:1, :], CAP * p_ + 0.5, None, ALU.is_ge))
                    v.do(dve.tensor_copy(further(EXPERT, p_), IOT[0:1, :]))
                    v.do(dve.tensor_scalar(further(ROW, p_), BASE[0:1, :], float(CAP * p_), None, ALU.add))
                v.do(dve.memset(firsts(ACTIVE), 1.0))
                v.do(dve.tensor_copy(firsts(EXPERT), IOT[0:1, :]))
                v.do(dve.tensor_copy(firsts(ROW), BASE[0:1, :]))
                v.sync()
                v.do(dve.tensor_copy(lrow(PLACE), lrow(ACTIVE)))
                v.sync()
                step_, a, b = 1, PLACE, OTHER
                while step_ < NJ:
                    v.do(dve.tensor_copy(LROW[0:1, b, 0:step_], LROW[0:1, a, 0:step_]))
                    v.do(dve.tensor_tensor(LROW[0:1, b, step_:], LROW[0:1, a, step_:], LROW[0:1, a, 0:NJ - step_], ALU.add))
                    v.sync()
                    a, b, step_ = b, a, step_ * 2
                v.do(dve.tensor_copy(LOUT[0:1, 2, 0:1], LROW[0:1, a, NJ - 1:NJ]))
                v.do(dve.tensor_tensor(lrow(b), lrow(a), lrow(ACTIVE), ALU.subtract))
                v.sync()
                wide = lambda ap: ap.unsqueeze(1).to_broadcast([1, SLOTS, NJ])
                for r, out in ((EXPERT, 0), (ROW, 1)):
                    v.do(dve.tensor_tensor(LSEL[:], wide(lrow(b)), SLI[:].unsqueeze(2).to_broadcast([1, SLOTS, NJ]), ALU.is_equal))
                    v.sync()
                    for r2 in (ACTIVE, r):
                        v.do(dve.tensor_tensor(LSEL[:], LSEL[:], wide(lrow(r2)), ALU.mult))
                        v.sync()
                    v.do(dve.tensor_reduce(LOUT[0:1, out, :], LSEL[:], AXX, ALU.add))
                    v.sync()
                v.do(dve.memset(ITEMS[:], 0))
                v.sync()
                v.do(dve.tensor_copy(ITEMS[0:1, 0:2 * SLOTS].rearrange("o (r s) -> o r s", r=2), LOUT[0:1, 0:2, :]))
                v.do(dve.tensor_copy(ITEMS[0:1, 2 * SLOTS:2 * SLOTS + 1], LOUT[0:1, 2, 0:1]))
                v.sync()
                dve.wait_ge(S["rows_gone0"], 32 * ((NT + 1) // 2))
                dve.wait_ge(S["rows_gone1"], 32 * (NT // 2))
                dve.sem_inc(S["items_ready"], 1)
                dve.sem_inc(S["xg_used"], 1)
                n_items = dve.value_load(ITEMS[0:1, 2 * SLOTS:2 * SLOTS + 1], min_val=NE, max_val=SLOTS)
                full_c = Count(S["ys_full"])
                cs = [conv, q, m, req, split, sreq, v.own]
                per = {conv: 2 * len(item_kinds), q: 12 * MOE_GROUPS, m: 14, req: 2 * MOE_GROUPS, split: KC + 2 * MOE_GROUPS,
                       sreq: KC + 2 * MOE_GROUPS, v.own: 1}
                kp_main = kp[0]
                with dve.Fori(0, SLOTS) as it:
                    with dve.If(it < n_items):
                        st = looped(cs, it, per)
                        kp[0], kp[1] = 0, item_kinds

                        def conv_left():
                            if kp[0] < 2 * len(item_kinds):
                                convert()

                        for _ in range(LOOK):
                            conv_left()
                        v.do(dve.memset(EACC[:], 0.0))
                        v.sync()
                        for k in range(KC):
                            ps = misc_ready()
                            t = T[sreq.n % 2][:, 0:CAP]
                            v.do(dve.tensor_scalar(t, ps[:, 0:CAP], gain(3)[:, k:k + 1], None, ALU.mult), m)
                            v.sync()
                            dve.sem_inc(sreq.next(), 1)
                            dve.wait_ge(S["split_hi"], sreq.at(sreq.n))
                            v.do(dve.tensor_tensor(XSL[:, k, :], t, XSH[:, k, :].bitcast(F32), ALU.subtract), split)
                            v.sync()
                        dve.sem_inc(S["xg_used"], 1)

                        def step(kind, g):
                            if kind == "GU":
                                for f in range(2):
                                    conv_left()
                                    ps = main_ready()
                                    v.do(dve.tensor_copy(EG[:, f, :], ps[:, 0:CAP]), q)
                                    v.sync()
                                    dve.sem_inc(req.next(), 1)
                                for f in range(2):
                                    conv_left()
                                    ps = main_ready()
                                    t = T[sreq.n % 2][:, 0:CAP]
                                    if f == 0:
                                        dve.wait_ge(S["act_done"], req.at(req.n))
                                    v.do(dve.tensor_tensor(t, ps[:, 0:CAP], EG[:, f, :], ALU.mult), q)
                                    v.sync()
                                    dve.sem_inc(sreq.next(), 1)
                                    dve.wait_ge(S["split_hi"], sreq.at(sreq.n))
                                    v.do(dve.tensor_tensor(ELO[g % 2][:, f, :], t, EHI[g % 2][:, f, :].bitcast(F32), ALU.subtract), split)
                                    v.sync()
                            else:
                                conv_left()
                                for d in range(KC):
                                    ps = main_ready()
                                    v.do(dve.tensor_tensor(EACC[:, d, :], ps[:, 0:CAP], EACC[:, d, :], ALU.add), q)
                                v.sync()
                                conv_left()

                        head, body, tail = ffn_schedule(MOE_GROUPS, MOE_LOOP)
                        for s in head:
                            step(*s)
                        cs2 = [conv, q, req, split, sreq]
                        per2 = {conv: 12, q: 24, req: 4, split: 4, sreq: 4}
                        spacer(dve)
                        with dve.Fori(0, MOE_LOOP) as i:
                            st2 = looped(cs2, i, per2)
                            for s in body:
                                step(*s)
                        leave(cs2, st2, per2, MOE_LOOP)
                        kp[0] += 12 * (MOE_LOOP - 1)
                        for s in tail:
                            step(*s)
                        for j, (r0, n) in enumerate(XBLK):
                            if j != 1:
                                dve.wait_ge(S["ys_out"], it * 48 + (48 if j == 0 else 80))
                            for h in range(2):
                                ps = misc_ready()
                                v.do(dve.tensor_copy(YT[j % 2][0:n, h * 512:h * 512 + 512], ps[0:n, :]), m)
                            v.sync()
                            dve.sem_inc(S["ys_full"], 1)
                        leave_items(cs, st, per, n_items)
                kp[0], kp[1] = kp_main, kinds
                for j in range(NT):
                    n = tokens(j)
                    dve.wait_ge(S[f"gathered{j % 2}"], 32 * (j // 2 + 1))
                    y0, y1 = YG[j % 2][0][0:n, :], YG[j % 2][1][0:n, :]
                    v.do(dve.tensor_scalar(y0, y0, TW[0:n, 0, j:j + 1], None, ALU.mult))
                    v.sync()
                    v.do(dve.scalar_tensor_tensor(y0, y1, TW[0:n, 1, j:j + 1], y0, ALU.mult, ALU.add))
                    v.sync()
                    dve.sem_inc(S["combined"], 1)
                    for h in range(2):
                        ps = misc_ready()
                        t = TC[h][:, :, 0:n]
                        xh = XHF[:, 4 * h:4 * h + 4, j * P:j * P + n]
                        xl = XLO[:, 4 * h:4 * h + 4, j * P:j * P + n]
                        v.do(dve.tensor_tensor(t, ps.rearrange("p (k t) -> p k t", k=4)[:, :, 0:n], xh, ALU.add), m)
                        v.sync()
                        v.do(dve.tensor_tensor(t, t, xl.bitcast(F32), ALU.add))
                        v.sync()
                        dve.sem_inc(sreq.next(), 1)
                        dve.wait_ge(S["split_hi"], sreq.at(sreq.n))
                        v.do(dve.tensor_tensor(xl, t, xh, ALU.subtract))
                        sq = SQS[:, j * P:j * P + n]
                        for k in range(4):
                            src = TC[2 + h][:, k, 0:n]
                            if h == 0 and k == 0:
                                v.do(dve.tensor_copy(sq, src))
                            else:
                                v.do(dve.tensor_tensor(sq, sq, src, ALU.add), split if k == 3 else None)
                            v.sync()
                    dve.sem_inc(S["gather_used"], 1)
                dve.sem_inc(sqc.next(), 1)
                for _ in range(LOOK):
                    convert()
            norm()
            for c in range(2):
                for t0, n in BLOCKS:
                    ps = misc_ready()
                    v.do(dve.tensor_copy(PT[:, c, t0:t0 + n], ps[:, 0:n]), m)
            v.sync()
            dve.sem_inc(S["p_ready"], 1)
            for d in range(KC):
                if not (l == 1 and d >= KC - LOOK):
                    convert()
                for t0, n in BLOCKS:
                    ps = main_ready()
                    t = T[req.n % 2][:, 0:n]
                    v.do(dve.tensor_tensor(t, ps[:, 0:n], RSTD[:, t0:t0 + n], ALU.mult), q)
                    v.sync()
                    dve.sem_inc(req.next(), 1)
                    ps = main_ready()
                    dve.wait_ge(S["act_done"], req.at(req.n))
                    v.do(dve.tensor_tensor(t, ps[:, 0:n], t, ALU.mult), q)
                    v.sync()
                    x = XNEW[:, d, t0:t0 + n]
                    v.do(dve.tensor_tensor(x, t, XHF[:, d, t0:t0 + n], ALU.add))
                    v.sync()
                    v.do(dve.tensor_tensor(x, x, XLF[:, d, t0:t0 + n], ALU.add))
                    v.sync()
            for d in range(KC):
                for j, (t0, n) in enumerate(BLOCKS):
                    dve.sem_inc(sreq.next(), 1)
                    split_x(d, j, XNEW[:, d, t0:t0 + n])
            dve.sem_inc(sqc.next(), 1)
            if l == 0:
                v.do(dve.memset(BDRAW[:], 0.0))
                v.sync()
                dve.sem_inc(S["sgu_zeroed"], 1)
        norm()
        norm_tokens()
        for d in range(KC):
            v.do(dve.tensor_scalar(XNEW[:, d, :], XNEW[:, d, :], gain(6)[:, d:d + 1], None, ALU.mult))
        v.sync()
        dve.sem_inc(S["xnew_ready"], 1)
        for j in range(NT):
            n = tokens(j)
            if j >= 2:
                dve.wait_ge(S[f"outputs{j % 2}"], 16 * (j // 2))
            for h in range(2):
                ps = misc_ready()
                v.do(dve.tensor_scalar(YOUT[j % 2][0:n, h * 512:h * 512 + 512], ps[0:n, :], RTOK[0:n, j:j + 1], None, ALU.mult), m)
            v.sync()
            dve.sem_inc(S["y_full"], 1)

    es.close()


_INS = ["x_prompt", "x_sample", "state_conv_a", "state_conv_b", "state_pool", "p_prompt", "p_sample", "norm_mix_g", "w_in",
        "conv_a_w", "conv_b_w", "conv_b_bias", "conv_b_ln_g", "conv_b_ln_b", "pool_w", "pool_scale", "sgu_ln_g", "sgu_ln_b",
        "sgu_w", "sgu_b", "w_branch", "w_out", "norm_ffn_g", "ffn_w_gate", "ffn_w_up", "ffn_w_down", "router_w", "moe_w_gate",
        "moe_w_up", "moe_w_down", "norm_ple_g", "ple_w_gate", "ple_w_proj", "final_norm_g"]
_OUTS = [("y_p", (1, SEQ, D)), ("y_s", (NSEQ, DSEQ, D)),
         ("a_p", (DEPTH, 1, 2, DB)), ("b_p", (DEPTH, 1, 30, DB)), ("c_p", (DEPTH, 1, 15, DB)), ("v_p", (DEPTH, 1, P, DB)),
         ("a_s", (DEPTH, NSEQ, 2, DB)), ("b_s", (DEPTH, NSEQ, 30, DB)), ("c_s", (DEPTH, NSEQ, 15, DB)), ("v_s", (DEPTH, NSEQ, DSEQ, DB))]


def kernel(**inputs):
    import numpy as _np
    import concourse.bacc as _bacc
    from concourse import mybir as _mybir
    from concourse.bass_utils import run_bass_kernel_spmd as _run

    nc = _bacc.Bacc("TRN2", target_bir_lowering=False, num_devices=1)
    arrays, a, o = {}, {}, {}
    for name in _INS:
        x = _np.ascontiguousarray(inputs[name])
        arrays[f"in_{name}"] = x
        a[name] = nc.dram_tensor(f"in_{name}", x.shape, _mybir.dt.from_np(x.dtype), kind="ExternalInput").ap()
    for name, shape in _OUTS:
        o[name] = nc.dram_tensor(f"out_{name}", shape, _mybir.dt.float32, kind="ExternalOutput").ap()
    build(nc, a, o)
    r = _run(nc, [arrays], core_ids=[0])
    return tuple(r.results[0][f"out_{name}"] for name, _ in _OUTS)
```

```python
from contextlib import ExitStack

import concourse.bass as bass
from concourse import mybir

F32 = mybir.dt.float32
F32R = mybir.dt.float32r
I32 = mybir.dt.int32
U32 = mybir.dt.uint32
ALU = mybir.AluOpType
ACT = mybir.ActivationFunctionType
AXX = mybir.AxisListType.X

P = 128
D = 1024
KC = D // P
DEPTH = 2
SEQ = 1024
NSEQ, DSEQ = 8, 8
NTOK = SEQ + NSEQ * DSEQ
NT = -(-NTOK // P)
DB = 256
DFF = 2816
NE = 8
DFE = 3584
EPS = 1e-6
BLOCKS = ((0, 384), (384, 384), (768, 320))
GROUPS = 4
WINDOWS = (2, 4, 8, 16)
POOL_MAX = max(WINDOWS)

OFF_H, OFF_AB, OFF_AC, OFF_CFA, OFF_CFB, OFF_POOL, OFF_U, OFF_V, OFF_GATE = (DB * i for i in range(9))
BR_A, BR_B, BR_C, BR_D = range(4)

CAP = 336
EXTRA = -(-NTOK // CAP) - 1
PAIRS = 2 * NTOK
SLOTS = NE + PAIRS // CAP
FFN_GROUPS = DFF // 256
MOE_GROUPS = DFE // 256
XBLK = ((0, 128), (128, 128), (256, CAP - 256))
SIZES = (256, 288, CAP)
LIST = SLOTS + 2
L_EXPERT, L_ROW, L_SIZE, L_NUM = (LIST * i for i in range(4))

RAW, HL, BANKS, LOOK = 2, 4, 6, 3


class Count:

    def __init__(self, sem=None):
        self.sem, self.n, self.terms = sem, 0, []

    def next(self):
        self.n += 1
        return self.sem

    def take(self, k=1):
        self.n += k
        return self.at(self.n)

    def at(self, n, mul=1, div=1):
        v = n // div * mul
        for reg, per in self.terms:
            assert per % div == 0
            v = v + reg * (per // div * mul)
        return v

    def before(self, back, mul=1):
        if self.n - back <= 0:
            assert not self.terms, "a wait in a loop against a value that may be zero"
            return None
        return self.at(self.n - back, mul)


def wait(eng, sem, value):
    if value is not None:
        eng.wait_ge(sem, value)


class Engine:

    def __init__(self, eng, own):
        self.eng, self.own, self.last = eng, Count(own), None

    def do(self, ins, sig=None):
        sig = sig or self.own
        ins.then_inc(sig.next(), 1)
        self.last = (sig, sig.n)
        return self.last

    def sync(self, mark=None):
        sig, n = mark or self.last
        self.eng.wait_ge(sig.sem, sig.at(n))


def looped(counts, reg, per):
    for c in counts:
        c.terms.append((reg, per[c]))
    return [c.n for c in counts]


def leave(counts, starts, per, times):
    for c, n0 in zip(counts, starts):
        assert c.n - n0 == per[c], (c.sem, c.n - n0, per[c])
        c.terms.pop()
        c.n = n0 + times * per[c]


def leave_items(counts, starts, per, reg):
    for c, n0 in zip(counts, starts):
        assert c.n - n0 == per[c], (c.sem, c.n - n0, per[c])
        c.terms.pop()
        c.n = n0
        c.terms.append((reg, per[c]))


def sized(eng, size, counts, body):
    starts = [c.n for c in counts]
    for v, n in enumerate(SIZES):
        for c, n0 in zip(counts, starts):
            c.n = n0
        with eng.If(size == v):
            body(n)


def build(nc, A, O):
    es = ExitStack()
    sem = lambda name: es.enter_context(nc.semaphore(name))
    place = [16512]
    names = {}

    def at(name, shape, dt, off):
        return nc.alloc_sbuf_tensor_at(name, list(shape), dt, offset=off)

    def sb(name, shape, dt=F32):
        size = 4
        for s in shape[1:]:
            size *= s
        off = place[0]
        place[0] += -(-size // 32) * 32
        names[name] = off
        return at(name, shape, dt, off)

    XHI = sb("XHI", [P, KC, NTOK], F32R)
    XLO = sb("XLO", [P, KC, NTOK], F32R)
    WRAW = [sb(f"WRAW{i}", [P, 2048]) for i in range(RAW)]
    WHI_RING = sb("WHI", [P, HL, KC, P], F32R)
    WLO_RING = sb("WLO", [P, HL, KC, P], F32R)
    WHI = [WHI_RING[:, i] for i in range(HL)]
    WLO = [WLO_RING[:, i] for i in range(HL)]
    RSTD = sb("RSTD", [P, NTOK])
    T = [sb(f"T{i}", [P, 384]) for i in range(4)]
    IDF = sb("IDF", [P, P])
    IDR = sb("IDR", [P, P], F32R)
    TRIL = sb("TRIL", [P, P])
    ONES = sb("ONES", [P, P])
    PAR = sb("PAR", [P, 4 * 38 + 7 * KC])
    RTOK = sb("RTOK", [P, NT])
    EPSC = sb("EPSC", [P, 1])
    WIN = sb("WIN", [P, 2])
    WINV = sb("WINV", [P, 2])
    FIXT = sb("FIXT", [P, 2, 16])
    PH = place[0]
    END = nc.sbuf_usable_end
    XHF, XLF = XHI[:].bitcast(F32), XLO[:].bitcast(F32)

    MIXED = at("MIXED", [P, KC, NTOK], F32, PH)
    MLO = at("MLO", [P, KC, NTOK], F32R, PH)
    MHI = at("MHI", [P, KC, NTOK], F32R, PH + 34816)
    o = PH
    sub = {}
    for name, shape in (("V", [P, NT, DB]), ("SWRAW", [P, GROUPS, P]), ("BDRAW", [64, GROUPS, 64]), ("WT", [P, GROUPS, P]),
                        ("BD", [64, GROUPS, 64]), ("BIAS", [P, 2, P]), ("LNG", [P, DB]), ("LNB", [P, DB]),
                        ("ST", [120, 4, DB]), ("PRS", [38, 2, DB]), ("NRS", [7 * KC, P]), ("BNS", [P, NT, 6]), ("MV", [P, NT, 2]),
                        ("VR", [P, NT])):
        size = 4
        for s in shape[1:]:
            size *= s
        sub[name] = at(name, shape, F32, o)
        o += -(-size // 32) * 32
    assert o <= PH + 32768
    V, SWRAW, BDRAW, WT, BD, BIAS, LNG, LNB, ST, PRS, NRS, BNS, MV, VR = sub.values()
    PA, PB, PC = 2, 30, 15
    WA, WB, WC = (p + SEQ + NSEQ * (p + DSEQ) for p in (PA, PB, PC))
    AR1 = PH + 34816
    GLU = at("GLU", [P, 2, WB], F32, AR1)
    SQB = at("SQB", [P, 2, NTOK], F32, AR1)
    up = lambda size: -(-size // 32) * 32
    YB = at("YB", [P, 2, NTOK], F32, AR1 + up(2 * WB * 4))
    AR2 = AR1 + up(2 * WB * 4) + 2 * NTOK * 4
    UB = at("UB", [P, 2, NTOK], F32, AR2)
    ZA = at("ZA", [P, 2, WA], F32, AR2)
    YA = at("YA", [P, 2, NTOK], F32, AR2 + up(2 * WA * 4))
    ZP = at("ZP", [P, 2, WC], F32, AR2)
    YP = at("YP", [P, 2, NTOK], F32, AR2 + up(2 * WC * 4))
    KEEP = at("KEEP", [P, 272], F32, PH + 72896)
    assert AR2 + up(2 * WC * 4) + 2 * NTOK * 4 <= PH + 72896
    XIN = at("XIN", [P, NT, D], F32, PH + 32768)
    SQS = at("SQS", [P, NTOK], F32, PH + 69632)
    PW = [at(f"PW{i}", [P, 2, DB], F32, PH + 69632 + 4352 + 2048 * i) for i in range(2)]
    OUTST = at("OUTST", [120, DB], F32, PH + 78080)
    PBD = at("PBD", [P, 2, P], F32, PH + 78080 + 1024)
    assert PH + 78080 + 2048 <= END, (PH, END)
    ACC = at("ACC", [P, KC, NTOK], F32, PH)
    HHI = [at(f"HHI{i}", [P, 2, NTOK], F32R, PH + 34816 + 17408 * i) for i in range(2)]
    HLO = [at(f"HLO{i}", [P, 2, NTOK], F32R, PH + 34816 + 17408 * i + 8704) for i in range(2)]
    GS = at("GS", [P, 2, NTOK], F32, PH + 69632)
    XNEW = at("XNEW", [P, KC, NTOK], F32, PH)
    PTOK = at("PTOK", [P, NT, DB], F32, PH + 52224)
    PT = at("PT", [P, 2, NTOK], F32, PH + 34816)
    FGAIN = at("FGAIN", [P, D], F32, PH + 61440)
    YOUT = [at(f"YOUT{i}", [P, D], F32, PH + 34816 + 4096 * i) for i in range(2)]
    o = [PH]

    def mo(name, shape, dt=F32):
        size = 4
        for s in shape[1:]:
            size *= s
        t = at(name, shape, dt, o[0])
        o[0] += -(-size // 32) * 32
        return t

    XG = mo("XG", [P, 3, D])
    XSH = mo("XSH", [P, KC, CAP], F32R)
    XSL = mo("XSL", [P, KC, CAP], F32R)
    EHI = [mo(f"EHI{i}", [P, 2, CAP], F32R) for i in range(2)]
    ELO = [mo(f"ELO{i}", [P, 2, CAP], F32R) for i in range(2)]
    EG = mo("EG", [P, 2, CAP])
    EACC = mo("EACC", [P, KC, CAP])
    YT = [mo(f"YT{i}", [P, D]) for i in range(2)]
    YT.append(at("YT2", [P, D], F32, PH + 69632))
    RW = mo("RW", [P, KC, NE])
    LG = mo("LG", [P, NT, NE])
    MX = mo("MX", [P, NT, NE])
    IX = mo("IX", [P, NT, NE], U32)
    IXF = mo("IXF", [P, NT, NE])
    OH = [mo(f"OH{i}", [P, NT, NE]) for i in range(2)]
    SS = mo("SS", [P, NT, NE])
    CS = mo("CS", [P, NT, NE])
    TM = mo("TM", [P, NT, NE])
    POSF = mo("POSF", [P, 2, NT])
    POSI = mo("POSI", [P, 2, NT], I32)
    TW = mo("TW", [P, 2, NT])
    IOT = mo("IOT", [P, NE])
    CNT = mo("CNT", [P, NE])
    BASE = at("BASE", [P, NE], F32, PH + 80000)
    ITEMS = mo("ITEMS", [1, 4 * LIST], I32)
    assert o[0] <= PH + 69632, o[0] - PH
    NJ = NE * (EXTRA + 1)
    lo = PH + 73984 + 4096
    LROW = at("LROW", [1, 6, NJ], F32, lo)
    LSEL = at("LSEL", [1, SLOTS, NJ], F32, PH + 73984)
    LOUT = at("LOUT", [1, 4, SLOTS], F32, up(lo + 24 * NJ))
    SLI = at("SLI", [1, SLOTS], F32, lo + up(24 * NJ) + up(16 * SLOTS))
    RWH = at("RWH", [P, KC, NE], F32R, PH + 12288 + 1024)
    RWL = at("RWL", [P, KC, NE], F32R, PH + 12288 + 2048)
    TRIS = at("TRIS", [P, P], F32, PH + 12288)
    YG = [[at(f"YG{i}{k}", [P, D], F32, PH + 8192 * i + 4096 * k) for k in range(2)] for i in range(3)]
    TC = [at(f"TC{i}", [P, 4, P], F32, PH + 24576 + 2048 * i) for i in range(2)]
    assert SLOTS * NJ * 4 <= 4096 and lo + up(24 * NJ) + up(16 * SLOTS) + 4 * SLOTS <= PH + 80000 <= END - 4 * NE

    XS = nc.dram_tensor("sorted_rows", [PAIRS + CAP, D], F32).ap()
    YS = nc.dram_tensor("expert_rows", [PAIRS + CAP, D], F32).ap()

    PS = es.enter_context(nc.psum_tensor("PS", [P, 8, 512], F32))

    S = {n: sem(n) for n in (
        "raw_ready0", "raw_ready1", "folded", "hi_ready", "lo_ready", "pw_ready0", "pw_ready1",
        "mm_done", "evicted", "misc_done", "misc_free", "act_req", "act_done", "split_req", "split_hi", "split_done",
        "dve_own", "act_own", "pool_own", "consts", "x_loaded0", "x_loaded1", "x_loaded2", "weighted", "gain_loaded", "par_loaded", "prs_loaded", "sgu_zeroed", "st_loaded", "sgu_loaded", "pbd_loaded", "pads_clear",
        "diag_ready", "sq_ready", "sgu_weights", "v_ready", "br_a", "br_b", "br_c", "br_d", "yb_ready", "lnsq_ready", "pooled",
        "stage_full", "stage_out", "outputs0", "outputs1", "tok_ready", "p_loaded", "p_ready", "mixed_ready", "rows_ready", "rows_gone0", "rows_gone1", "tri_ready",
        "counts_ready", "items_ready", "scattered", "xg_ready", "xg_used", "xs_ready", "ys_full", "ys_out", "gathered0", "gathered1", "gathered2", "gather_used", "combined",
        "xnew_ready", "y_full", "v_out", "par_ready", "rw_loaded", "phase_clear", "spacer")}

    mix_l = lambda l: [("col", l)] * 4 + [("col", l)] * 4 + [("col", l)] * 3 + [("col", l)] * 4 + [("col", l)] * 1 + [("col", l)] * 8
    ffn_l = [("col", 2)] * 2 + [("col", 2), ("col", 2), ("row", None)] * (FFN_GROUPS - 1) + [("row", None)]
    kinds = mix_l(0) + [("col", None)] * 4 + ffn_l + [("col", 4)] * 4 + mix_l(1) + [("col", None)] * 4 + [("col", 5)] * 4
    item_kinds = [("col", None)] * 2 + [("col", None), ("col", None), ("row", None)] * (MOE_GROUPS - 1) + [("row", None)]
    T_MOE = 24 + 4 + len(ffn_l) + 4 + 24 + 4
    gain = lambda norm: PAR[:, 152 + norm * KC:152 + (norm + 1) * KC]
    par = lambda l, c, r: PAR[:, (l * 2 + c) * 38 + r:(l * 2 + c) * 38 + r + 1]
    R_CB, R_CA, R_BIAS, R_LG, R_LB, R_PS = 0, 31, 34, 35, 36, 37

    def raw_view(t, half, kind):
        if kind == "col":
            return WRAW[t][:].rearrange("p (k n) -> p k n", k=KC)[:, :, half * P:(half + 1) * P]
        return WRAW[t][:, half * 1024:(half + 1) * 1024].rearrange("p (k n) -> p k n", k=KC)

    def pieces(j, buf, pad):
        t0, n = BLOCKS[j]
        out = []
        if t0 < SEQ:
            m = min(n, SEQ - t0)
            out.append((0, m, buf[:, pad + t0:pad + t0 + m]))
        if t0 + n > SEQ:
            s = buf[:, pad + SEQ:].rearrange("p (s t) -> p s t", s=NSEQ)[:, :, pad:]
            out.append((SEQ - t0, n - (SEQ - t0), s))
        return out

    def shaped(ap, like):
        return ap.rearrange("p (s t) -> p s t", s=NSEQ) if len(like.shape) == 3 else ap

    def tokens(j):
        return min(P, NTOK - j * P)

    def groups(n):
        yield ("GU", 0)
        for g in range(1, n):
            yield ("GU", g)
            yield ("DN", g - 1)
        yield ("DN", n - 1)

    FFN_LOOP, MOE_LOOP = (FFN_GROUPS - 3) // 2, (MOE_GROUPS - 2) // 2
    assert FFN_GROUPS % 2 == 1 and MOE_GROUPS % 2 == 0
    Q_FFN = 3 * KC + 6 + 12 + 48 + 18 + 48 + 6 + 48 + 48 + 24
    Q_LAST_DOWN = Q_FFN + 12 + 36 * (FFN_GROUPS - 1)
    W_FFN = 3 * KC + KC + 3 * KC
    W_MIX1 = W_FFN + 6 * FFN_GROUPS + 3 * KC + 3 * KC
    MERGE_EARLY = (AR2 + up(2 * WC * 4) - (PH + 34816)) // (NTOK * 4)
    W_MOE = W_MIX1 + KC + KC + 3 * KC

    def ffn_schedule(n, loops):
        steps = list(groups(n))
        return steps[:1], steps[1:5], steps[1 + 4 * loops:]

    def spacer(eng):
        eng.sem_inc(S["spacer"], 1)

    def load_p(q, l):
        for j in range(NT):
            n = tokens(j)
            src = A["p_prompt"][l, 0, j * P:(j + 1) * P, :] if j < NT - 1 else A["p_sample"][l].rearrange("s t d -> (s t) d")
            q.dma_start(PTOK[0:n, j, :], src).then_inc(S["p_loaded"], 16)

    block = es.enter_context(nc.Block())

    @block.sync
    def _(sp):
        tile = Count()
        pw, q, pw_end = Count(), Count(), []

        def load(src):
            if tile.n >= RAW:
                sp.wait_ge(S["lo_ready"], lo_value(tile))
            s = tile.n % RAW
            k = src.shape[1]
            sp.dma_start(WRAW[s][:].rearrange("p (k n) -> p k n", k=k), src).then_inc(S[f"raw_ready{s}"], 16)
            tile.n += 1

        def lo_value(t):
            v = t.n * 2 - 2 * RAW + 2
            for reg, per in t.terms:
                v = v + reg * (2 * per)
            return v

        def load_pw(src):
            if pw.n >= 2:
                sp.wait_ge(S["mm_done"], pw_end[pw.n - 2])
            s = pw.n % 2
            sp.dma_start(PW[s][:], src).then_inc(S[f"pw_ready{s}"], 16)
            pw.n += 1

        def cols(w, c0, n=DB):
            return w.rearrange("(k p) n -> p k n", p=P)[:, :, bass.ds(c0, n)]

        def load_x(block):
            t0, m = BLOCKS[block]
            for j in range(t0 // P, -(-(t0 + m) // P)):
                n = tokens(j)
                src = A["x_prompt"][0, j * P:(j + 1) * P, :] if j < NT - 1 else A["x_sample"].rearrange("s t d -> (s t) d")
                sp.dma_start(XIN[0:n, j, :], src).then_inc(S[f"x_loaded{block}"], 16)

        load_x(0)
        load_x(1)
        q.n += 3 * KC
        for l in range(DEPTH):
            w_in = A["w_in"][l]
            wb = A["w_branch"][l]

            def gate_project(br):
                for j in range(4):
                    load(cols(w_in, OFF_GATE + br * D + j * DB))
                    load_pw(cols(wb[br], j * DB))
                    q.n += 12
                    pw_end.append(q.at(q.n))

            load(cols(w_in, OFF_U))
            if l == 0:
                load_x(2)
            load(cols(w_in, OFF_V))
            load(cols(w_in, OFF_CFB))
            load(cols(w_in, OFF_CFA))
            q.n += 18
            gate_project(BR_D)
            for off in (OFF_AC, OFF_H, OFF_AB):
                load(cols(w_in, off))
            q.n += 18
            gate_project(BR_A)
            load(cols(w_in, OFF_POOL))
            q.n += 6
            gate_project(BR_B)
            gate_project(BR_C)
            for j in range(4):
                load(cols(A["w_out"][l], j * DB))
            q.n += 24
            if l == 0:
                wg, wu, wd = (A[n][0] for n in ("ffn_w_gate", "ffn_w_up", "ffn_w_down"))
                wdr = wd.rearrange("(f p) n -> p f n", p=P)

                def step(kind, g, i=0):
                    if kind == "GU":
                        load(cols(wg, i * 512 + g * DB))
                        load(cols(wu, i * 512 + g * DB))
                    else:
                        load(wdr[:, bass.ds(i * 4 + g * 2, 2), :])

                head, body, tail = ffn_schedule(FFN_GROUPS, FFN_LOOP)
                for s in head:
                    step(*s)
                with sp.Fori(0, FFN_LOOP) as i:
                    st = looped([tile], i, {tile: 6})
                    for s in body:
                        step(*s, i)
                leave([tile], st, {tile: 6}, FFN_LOOP)
                for s in tail:
                    step(*s)
                q.n += 36 * FFN_GROUPS
            else:
                q.n += 2 * NT
                sp.wait_ge(S["items_ready"], 1)
                n_items = sp.value_load(ITEMS[0:1, L_NUM:L_NUM + 1], min_val=NE, max_val=SLOTS)
                wg = A["moe_w_gate"][0].rearrange("e (k p) n -> p (e k) n", p=P)
                wu = A["moe_w_up"][0].rearrange("e (k p) n -> p (e k) n", p=P)
                wd = A["moe_w_down"][0].rearrange("e (f p) n -> p (e f) n", p=P)
                NF = DFE // P
                with sp.Fori(0, SLOTS) as it:
                    with sp.If(it < n_items):
                        e = sp.value_load(ITEMS[0:1, bass.ds(it, 1)], min_val=0, max_val=NE - 1)
                        st = looped([tile], it, {tile: len(item_kinds)})

                        def step(kind, g, i=0):
                            if kind == "GU":
                                load(wg[:, bass.ds(e * KC, KC), bass.ds(i * 512 + g * DB, DB)])
                                load(wu[:, bass.ds(e * KC, KC), bass.ds(i * 512 + g * DB, DB)])
                            else:
                                load(wd[:, bass.ds(e * NF + i * 4 + g * 2, 2), :])

                        head, body, tail = ffn_schedule(MOE_GROUPS, MOE_LOOP)
                        for s in head:
                            step(*s)
                        with sp.Fori(0, MOE_LOOP) as i:
                            st2 = looped([tile], i, {tile: 6})
                            for s in body:
                                step(*s, i)
                        leave([tile], st2, {tile: 6}, MOE_LOOP)
                        for s in tail:
                            step(*s)
                        leave_items([tile], st, {tile: len(item_kinds)}, n_items)
                q.terms.append((n_items, 12 * MOE_GROUPS))
            for j in range(4):
                load(cols(A["ple_w_gate"][l], j * DB))
                if l == 0 and j == 0:
                    sp.wait_ge(S["evicted"], Q_LAST_DOWN + 1)
                load_pw(cols(A["ple_w_proj"][l], j * DB))
                q.n += 12
                pw_end.append(q.at(q.n))

    @block.gpsimd
    def _(g):
        pool = Engine(g, S["pool_own"])
        tile = Count()
        kp = [0]

        g.memset(IDF[:], 0.0).then_inc(S["pool_own"], 1)
        g.memset(TRIL[:], 1.0).then_inc(S["pool_own"], 1)
        g.wait_ge(S["pool_own"], 2)
        g.affine_select(out=IDF[:], in_=IDF[:], compare_op=ALU.not_equal, fill=1.0, base=0, pattern=[[-1, P]],
                        channel_multiplier=1).then_inc(S["consts"], 1)
        g.affine_select(out=TRIL[:], in_=TRIL[:], compare_op=ALU.is_ge, fill=0.0, base=0, pattern=[[1, P]],
                        channel_multiplier=-1).then_inc(S["consts"], 1)
        g.iota(FIXT[:], pattern=[[0, 2], [1, 16]], base=1, channel_multiplier=0,
               allow_small_or_imprecise_dtypes=True).then_inc(S["consts"], 1)

        for j in range(7):
            src = (A["norm_mix_g"][j % 2] if j < 2 else A["norm_ffn_g"][j % 2] if j < 4 else A["norm_ple_g"][j % 2] if j < 6
                   else A["final_norm_g"])
            g.dma_start(NRS[j * KC:(j + 1) * KC, :], src.rearrange("(k p) -> k p", p=P)).then_inc(S["par_loaded"], 16)
        for l in range(DEPTH):
            for r, n, src in ((R_CB, 31, A["conv_b_w"][l]), (R_CA, 3, A["conv_a_w"][l]), (R_BIAS, 1, A["conv_b_bias"][l:l + 1]),
                              (R_LG, 1, A["conv_b_ln_g"][l:l + 1]), (R_LB, 1, A["conv_b_ln_b"][l:l + 1]), (R_PS, 1, A["pool_scale"][l:l + 1])):
                g.dma_start(PRS[r:r + n, l, :], src).then_inc(S["par_loaded"], 16)

        def layer_params(l):
            g.wait_ge(S["sgu_zeroed"], l + 1)
            g.dma_start(SWRAW[:], A["sgu_w"][l].rearrange("g t s -> t g s")).then_inc(S["sgu_loaded"], 16)
            for b in range(NSEQ):
                g.dma_start(BDRAW[8 * b:8 * b + 8, :, 8 * b:8 * b + 8], A["sgu_w"][l][:, 0:8, 0:8].rearrange("g t s -> t g s")
                            ).then_inc(S["sgu_loaded"], 16)
            for q in range(GROUPS):
                g.dma_start(BIAS[64 * (q % 2):64 * (q % 2) + 64, q // 2, :], A["sgu_b"][l, q, :].partition_broadcast(64)
                            ).then_inc(S["sgu_loaded"], 16)
                g.dma_start(PBD[64 * (q % 2):64 * (q % 2) + 64, q // 2, 64 * (q % 2):64 * (q % 2) + 64], A["pool_w"][l, q]
                            ).then_inc(S["pbd_loaded"], 16)
            g.dma_start(LNG[:], A["sgu_ln_g"][l].partition_broadcast(P)).then_inc(S["sgu_loaded"], 16)
            g.dma_start(LNB[:], A["sgu_ln_b"][l].partition_broadcast(P)).then_inc(S["sgu_loaded"], 16)
            sb_ = A["state_conv_b"][l].rearrange("(h s) r c -> h (s r) c", h=2)
            for h in range(2):
                g.dma_start(ST[:, h, :], sb_[h]).then_inc(S["st_loaded"], 16)
            g.dma_start(ST[:, 2, :], A["state_pool"][l].rearrange("s r c -> (s r) c")).then_inc(S["st_loaded"], 16)
            g.dma_start(ST[0:16, 3, :], A["state_conv_a"][l].rearrange("s r c -> (s r) c")).then_inc(S["st_loaded"], 16)

        def fold():
            kind, norm = kinds[kp[0]]
            kp[0] += 1
            if norm is not None:
                s = tile.n % RAW
                g.wait_ge(S["par_ready"], 1)
                g.wait_ge(S[f"raw_ready{s}"], tile.at(tile.n, 16, 2) + 16)
                w = WRAW[s][:].rearrange("p (k n) -> p k n", k=KC)
                g.tensor_tensor(w, w, gain(norm).unsqueeze(2).to_broadcast([P, KC, DB]), ALU.mult).then_inc(S["folded"], 1)
            tile.n += 1

        layer_params(0)
        for _ in range(24 + 4):
            fold()
        fold(), fold()
        with g.Fori(0, FFN_LOOP) as i:
            st = looped([tile], i, {tile: 6})
            for _ in range(6):
                fold()
        leave([tile], st, {tile: 6}, FFN_LOOP)
        kp[0] = tile.n
        while tile.n < 24 + 4 + len(ffn_l):
            fold()
        g.wait_ge(S["evicted"], Q_LAST_DOWN)
        load_p(g, 0)
        for _ in range(4):
            fold()
        fold(), fold()
        layer_params(1)
        for _ in range(24 + 4 - 2):
            fold()

        g.wait_ge(S["phase_clear"], 1)
        g.dma_start(RW[:], A["router_w"][0].rearrange("(k p) e -> p k e", p=P)).then_inc(S["rw_loaded"], 16)
        g.iota(SLI[:], pattern=[[1, SLOTS]], base=0, channel_multiplier=0, allow_small_or_imprecise_dtypes=True).then_inc(S["consts"], 1)
        g.iota(IOT[:], pattern=[[1, NE]], base=0, channel_multiplier=0, allow_small_or_imprecise_dtypes=True).then_inc(S["consts"], 1)
        for j, (r0, n) in enumerate(XBLK):
            g.dma_start(XS[PAIRS + r0:PAIRS + r0 + n, :], XG[0:n, j, :]).then_inc(S["scattered"], 16)
        for j in range(NT):
            n = tokens(j)
            g.wait_ge(S["rows_ready"], j + 1)
            for k in range(2):
                g.indirect_dma_start(XS[0:PAIRS, :], bass.IndirectOffsetOnAxis(ap=POSI[0:n, k, j:j + 1], axis=0), YT[j % 2][0:n, :],
                                     None).then_inc(S[f"rows_gone{j % 2}"], 16)
        g.wait_ge(S["rows_gone0"], 32 * ((NT + 1) // 2))
        g.wait_ge(S["rows_gone1"], 32 * (NT // 2))
        g.wait_ge(S["scattered"], 48)
        g.wait_ge(S["items_ready"], 1)
        n_items = g.value_load(ITEMS[0:1, L_NUM:L_NUM + 1], min_val=NE, max_val=SLOTS)
        row = g.value_load(ITEMS[0:1, L_ROW + 1:L_ROW + 2], min_val=0, max_val=PAIRS)
        for j, (r0, n) in enumerate(XBLK):
            g.dma_start(XG[0:n, j, :], XS[bass.ds(row + r0, n), :]).then_inc(S["xg_ready"], 16)
        with g.Fori(0, SLOTS) as it:
            with g.If(it < n_items):
                row = g.value_load(ITEMS[0:1, bass.ds(it + L_ROW + 2, 1)], min_val=0, max_val=PAIRS)
                g.wait_ge(S["xg_used"], it + 1)
                spacer(g)
                for j, (r0, n) in enumerate(XBLK):
                    g.dma_start(XG[0:n, j, :], XS[bass.ds(row + r0, n), :]).then_inc(S["xg_ready"], 16)
        tile.terms.append((n_items, len(item_kinds)))
        fold(), fold()
        g.wait_ge(S["ys_out"], n_items * 48 + 48)
        spacer(g)
        for j in range(NT):
            n = tokens(j)
            if j >= 3:
                g.wait_ge(S["gather_used"], j - 2)
            for k in range(2):
                g.indirect_dma_start(YG[j % 3][k][0:n, :], None, YS[0:PAIRS, :],
                                     bass.IndirectOffsetOnAxis(ap=POSI[0:n, k, j:j + 1], axis=0)).then_inc(S[f"gathered{j % 3}"], 16)
        load_p(g, 1)
        g.dma_start(FGAIN[:], A["final_norm_g"].partition_broadcast(P)).then_inc(S["gain_loaded"], 16)
        for _ in range(2):
            fold()

    @block.tensor
    def _(pe):
        unit, q, m, pw = Count(), Count(S["mm_done"]), Count(S["misc_done"]), Count()
        split = Count()

        def use(n=1):
            pe.wait_ge(S["lo_ready"], unit.at(unit.n + n))

        def open_bank():
            wait(pe, S["evicted"], q.before(BANKS - 1))
            return q.n % BANKS

        def misc_bank():
            wait(pe, S["misc_free"], m.before(1))
            if m.terms:
                spacer(pe)
            return 6 + m.n % 2

        def product(bank, n, slot, hi, lo, splits=None):
            for k in range(KC):
                if splits is not None:
                    pe.wait_ge(S["split_done"], splits + k + 1)
                wh, wl = WHI[slot][:, k, :], WLO[slot][:, k, :]
                pe.matmul(PS[:, bank, 0:n], wh, hi(k), start=(k == 0), stop=False)
                pe.matmul(PS[:, bank, 0:n], wh, lo(k), start=False, stop=False)
                ins = pe.matmul(PS[:, bank, 0:n], wl, hi(k), start=False, stop=(k == KC - 1))
            return ins

        def column_unit(HI, LO, first_use=None):
            use()
            slot = unit.n % HL
            for t0, n in BLOCKS:
                b = open_bank()
                product(b, n, slot, lambda k: HI[:, k, t0:t0 + n], lambda k: LO[:, k, t0:t0 + n],
                        first_use if t0 == 0 else None).then_inc(q.next(), 1)
            unit.n += 1

        def token_sums(*parts):
            b = misc_bank()
            for j in range(NT):
                n = tokens(j)
                for x, part in enumerate(parts):
                    ins = pe.matmul(PS[0:n, b, j:j + 1], part[:, j * P:j * P + n], ONES[:, 0:1], start=(x == 0), stop=(x == len(parts) - 1))
            ins.then_inc(m.next(), 1)

        def stats():
            pe.wait_ge(S["sq_ready"], sq.take())
            token_sums(SQS)

        def spread():
            pe.wait_ge(S["diag_ready"], diag.take())
            for j, (t0, n) in enumerate(BLOCKS):
                b = misc_bank()
                pe.matmul(PS[:, b, 0:n], ONES[:], T[j][:, 0:n], start=True, stop=True).then_inc(m.next(), 1)

        sq, diag = Count(), Count()

        def gate_project(ready, count, Y, after_first=lambda: None):
            pe_ready = [False]
            for j in range(4):
                for h in range(2):
                    use()
                    slot = unit.n % HL
                    for t0, n in BLOCKS:
                        b = open_bank()
                        product(b, n, slot, lambda k: XHI[:, k, t0:t0 + n], lambda k: XLO[:, k, t0:t0 + n]).then_inc(q.next(), 1)
                        if not pe_ready[0]:
                            after_first()
                            pe.wait_ge(S[ready], count)
                            pe_ready[0] = True
                        if h == 0 and t0 == 0:
                            pe.wait_ge(S[f"pw_ready{pw.n % 2}"], (pw.n // 2 + 1) * 16)
                        b = open_bank()
                        for k in range(2):
                            ins = pe.matmul(PS[:, b, 0:n], PW[pw.n % 2][:, k, h * P:(h + 1) * P], Y[:, k, t0:t0 + n], start=(k == 0), stop=(k == 1))
                        ins.then_inc(q.next(), 1)
                    unit.n += 1
                pw.n += 1

        def states_in():
            pe.wait_ge(S["st_loaded"], 64 * (l + 1))
            b = misc_bank()
            for c in range(2):
                for h in range(2):
                    x = (c * 2 + h) * 120
                    ins = pe.transpose(PS[:, b, x:x + 120], ST[:, h, c * P:(c + 1) * P], IDF[0:120, 0:120])
            ins.then_inc(m.next(), 1)
            b = misc_bank()
            for c in range(2):
                pe.transpose(PS[:, b, c * 120:c * 120 + 120], ST[:, 2, c * P:(c + 1) * P], IDF[0:120, 0:120])
                ins = pe.transpose(PS[:, b, 240 + c * 16:256 + c * 16], ST[0:16, 3, c * P:(c + 1) * P], IDF[0:16, 0:16])
            ins.then_inc(m.next(), 1)

        so = Count()

        def states_out(buf, tmp, pad):
            rows = NSEQ * pad
            lots = -(-rows // 120)
            pe.wait_ge(S["tok_ready"], so.take())
            for h in range(lots):
                n = rows // lots
                b = misc_bank()
                for c in range(2):
                    ins = pe.transpose(PS[0:n, b, c * P:(c + 1) * P], tmp[:, c, h * n:(h + 1) * n], IDF[:])
                ins.then_inc(m.next(), 1)
            b = misc_bank()
            for c in range(2):
                ins = pe.transpose(PS[0:pad, b, c * P:(c + 1) * P], buf[:, c, SEQ:SEQ + pad], IDF[:])
            ins.then_inc(m.next(), 1)

        def down(hi, lo, blocks, after=lambda d: None):
            use(2)
            s0, s1 = unit.n % HL, (unit.n + 1) % HL
            for d in range(KC):
                for t0, n in blocks:
                    b = open_bank()
                    for f, s in enumerate((s0, s1)):
                        pe.matmul(PS[:, b, 0:n], WHI[s][:, d, :], hi[:, f, t0:t0 + n], start=(f == 0), stop=False)
                        pe.matmul(PS[:, b, 0:n], WHI[s][:, d, :], lo[:, f, t0:t0 + n], start=False, stop=False)
                        ins = pe.matmul(PS[:, b, 0:n], WLO[s][:, d, :], hi[:, f, t0:t0 + n], start=False, stop=(f == 1))
                    ins.then_inc(q.next(), 1)
                after(d)
            unit.n += 2

        pe.wait_ge(S["consts"], 3)
        for block, (t0, n) in enumerate(BLOCKS):
            tiles = range(t0 // P, -(-(t0 + n) // P))
            pe.wait_ge(S[f"x_loaded{block}"], 16 * len(tiles))
            for c in range(KC):
                b = open_bank()
                for j in tiles:
                    w = tokens(j)
                    ins = pe.transpose(PS[:, b, j * P - t0:j * P - t0 + w], XIN[0:w, j, c * P:(c + 1) * P], IDF[0:w, 0:w])
                ins.then_inc(q.next(), 1)
            if block == 0:
                pe.wait_ge(S["par_loaded"], 16 * (7 + 12))
                b = misc_bank()
                for l in range(DEPTH):
                    for c in range(2):
                        pe.transpose(PS[:, b, (l * 2 + c) * 38:(l * 2 + c) * 38 + 38], PRS[:, l, c * P:(c + 1) * P], IDF[0:38, 0:38])
                pe.transpose(PS[:, b, 152:152 + 7 * KC], NRS[:], IDF[0:7 * KC, 0:7 * KC]).then_inc(m.next(), 1)

        for l in range(DEPTH):
            stats()
            column_unit(XHI, XLO, first_use=(W_MIX1 if l else None))
            spread()
            column_unit(XHI, XLO)
            use(2)
            for j in range(NT):
                n = tokens(j)
                b = misc_bank()
                pair = slice(unit.n % HL, unit.n % HL + 2)
                dst = PS[0:n, b, 0:DB].rearrange("p (h c) -> p h c", h=2)
                for k in range(KC):
                    xh, xl = XHI[:, k, j * P:j * P + n], XLO[:, k, j * P:j * P + n]
                    pe.matmul(dst, xh, WHI_RING[:, pair, k, :], start=(k == 0), stop=False)
                    pe.matmul(dst, xl, WHI_RING[:, pair, k, :], start=False, stop=False)
                    ins = pe.matmul(dst, xh, WLO_RING[:, pair, k, :], start=False, stop=(k == KC - 1))
                ins.then_inc(m.next(), 1)
            unit.n += 2
            pe.wait_ge(S["sgu_loaded"], 16 * (1 + NSEQ + GROUPS + 2) * (l + 1))
            b = misc_bank()
            for q4 in range(GROUPS):
                ins = pe.transpose(PS[:, b, q4 * P:(q4 + 1) * P], SWRAW[:, q4, :], IDF[:])
            ins.then_inc(m.next(), 1)
            b = misc_bank()
            for q4 in range(GROUPS):
                ins = pe.transpose(PS[0:64, b, q4 * 64:(q4 + 1) * 64], BDRAW[:, q4, :], IDF[0:64, 0:64])
            ins.then_inc(m.next(), 1)
            states_in()
            for _ in range(4):
                column_unit(XHI, XLO)
            pe.wait_ge(S["v_ready"], l + 1)
            for c in range(2):
                for jj in range(2):
                    b = misc_bank()
                    for j in range(4 * jj, 4 * jj + 4):
                        for h in range(2):
                            g4 = 2 * c + h
                            ins = pe.matmul(PS[64 * h:64 * h + 64, b, (j % 4) * P:(j % 4 + 1) * P], V[:, j, g4 * 64:g4 * 64 + 64], WT[:, g4, :],
                                            start=True, stop=True)
                    ins.then_inc(m.next(), 1)
            b = misc_bank()
            for c in range(2):
                for h in range(2):
                    g4 = 2 * c + h
                    ins = pe.matmul(PS[64 * h:64 * h + 64, b, c * 64:c * 64 + 64], V[0:64, NT - 1, g4 * 64:g4 * 64 + 64], BD[:, g4, :],
                                    start=True, stop=True)
            ins.then_inc(m.next(), 1)
            states_out(GLU, YB, PB)
            gate_project("br_d", l + 1, UB)
            for _ in range(4):
                column_unit(XHI, XLO)
            states_out(ZA, YA, PA)
            column_unit(XHI, XLO)
            column_unit(XHI, XLO)
            gate_project("br_a", l + 1, YA)
            pe.wait_ge(S["yb_ready"], l + 1)
            for t0, n in BLOCKS:
                b = misc_bank()
                for k in range(2):
                    ins = pe.matmul(PS[:, b, 0:n], ONES[:], YB[:, k, t0:t0 + n], start=(k == 0), stop=(k == 1))
                ins.then_inc(m.next(), 1)
            column_unit(XHI, XLO)
            pe.wait_ge(S["lnsq_ready"], l + 1)
            token_sums(SQB[:, 0, :], SQB[:, 1, :])
            column_unit(XHI, XLO)
            spread()
            states_out(ZP, YP, PC)
            gate_project("br_b", l + 1, YB)
            pe.wait_ge(S["pooled"], l + 1)
            pe.wait_ge(S["pbd_loaded"], 64 * (l + 1))
            for c in range(2):
                for t0, n in BLOCKS:
                    b = misc_bank()
                    pe.matmul(PS[:, b, 0:n], PBD[:, c, :], YP[:, c, t0:t0 + n], start=True, stop=True).then_inc(m.next(), 1)
            gate_project("br_c", l + 1, YP)
            for d in range(KC):
                column_unit(MHI, MLO, first_use=(W_FFN if l == 0 else W_MOE) - 3 * KC - KC if d == 0 else None)
            stats()
            if l == 0:
                hs = Count()

                def step(kind, g, first=False):
                    if kind == "GU":
                        for u in range(4):
                            column_unit(XHI, XLO)
                            if first and u == 0:
                                spread()
                    else:
                        pe.wait_ge(S["split_done"], hs.take(2 * 3))
                        down(HHI[g % 2], HLO[g % 2], BLOCKS)

                hs.n = W_FFN
                head, body, tail = ffn_schedule(FFN_GROUPS, FFN_LOOP)
                for s in head:
                    step(*s, first=True)
                with pe.Fori(0, FFN_LOOP) as i:
                    cs = [unit, q, hs]
                    per = {unit: 12, q: 2 * (12 + 24), hs: 12}
                    st = looped(cs, i, per)
                    for s in body:
                        step(*s)
                leave(cs, st, per, FFN_LOOP)
                for s in tail:
                    step(*s)
            else:
                pe.wait_ge(S["tri_ready"], 1)
                b = misc_bank()
                for j in range(NT):
                    n = tokens(j)
                    for k in range(KC):
                        xh, xl, dst = XHI[:, k, j * P:j * P + n], XLO[:, k, j * P:j * P + n], PS[0:n, b, j * NE:(j + 1) * NE]
                        pe.matmul(dst, xh, RWH[:, k, :], start=(k == 0), stop=False)
                        pe.matmul(dst, xl, RWH[:, k, :], start=False, stop=False)
                        ins = pe.matmul(dst, xh, RWL[:, k, :], start=False, stop=(k == KC - 1))
                ins.then_inc(m.next(), 1)

                def rows(j):
                    n = tokens(j)
                    for h in range(2):
                        b = open_bank()
                        for k in range(4):
                            pe.matmul(PS[0:n, b, k * P:(k + 1) * P], XHI[:, 4 * h + k, j * P:j * P + n], IDR[:], start=True, stop=False)
                            ins = pe.matmul(PS[0:n, b, k * P:(k + 1) * P], XLO[:, 4 * h + k, j * P:j * P + n], IDR[:], start=False, stop=True)
                        ins.then_inc(q.next(), 1)

                for j in range(2):
                    rows(j)
                pe.wait_ge(S["counts_ready"], 1)
                b = misc_bank()
                flat = lambda t: t[:].rearrange("p j e -> p (j e)")
                pe.matmul(PS[:, b, 0:NT * NE], TRIS[:], flat(SS), start=True, stop=False)
                pe.matmul(PS[:, b, 0:NT * NE], ONES[:], flat(CS), start=False, stop=True)
                pe.matmul(PS[:, b, NT * NE:(NT + 1) * NE], ONES[:], TM[:, 0, :], start=True, stop=True).then_inc(m.next(), 1)
                for j in range(2, NT):
                    rows(j)
                pe.wait_ge(S["items_ready"], 1)
                n_items = pe.value_load(ITEMS[0:1, L_NUM:L_NUM + 1], min_val=NE, max_val=SLOTS)
                hs = Count()
                hs.n = W_MOE
                q_item = None
                cs = [unit, q, m, hs]
                per = {unit: 2 * len(item_kinds), q: MOE_GROUPS * 12, m: 14, hs: KC + 2 * MOE_GROUPS}

                def prepare(k):
                    b = misc_bank()
                    for j, (r0, n) in enumerate(XBLK):
                        ins = pe.transpose(PS[:, b, r0:r0 + n], XG[0:n, j, k * P:(k + 1) * P], IDF[0:n, 0:n])
                    ins.then_inc(m.next(), 1)

                def item_out():
                    pe.wait_ge(S["evicted"], q_item)
                    for j, (r0, n) in enumerate(XBLK):
                        for h in range(2):
                            b = misc_bank()
                            for k in range(4):
                                ins = pe.transpose(PS[0:n, b, k * P:(k + 1) * P], EACC[:, 4 * h + k, r0:r0 + n], IDF[:])
                            ins.then_inc(m.next(), 1)

                pe.wait_ge(S["xg_ready"], 48)
                for k in range(KC):
                    prepare(k)
                with pe.Fori(0, SLOTS) as it:
                    with pe.If(it < n_items):
                        size = pe.value_load(ITEMS[0:1, bass.ds(it + L_SIZE, 1)], min_val=0, max_val=len(SIZES) - 1)
                        st = looped(cs, it, per)

                        def item(rows):
                            nonlocal q_item

                            def step(kind, g, after=lambda d: None):
                                if kind == "GU":
                                    for _ in range(4):
                                        use()
                                        b = open_bank()
                                        product(b, rows, unit.n % HL, lambda k: XSH[:, k, 0:rows], lambda k: XSL[:, k, 0:rows]).then_inc(q.next(), 1)
                                        unit.n += 1
                                else:
                                    pe.wait_ge(S["split_done"], hs.take(2))
                                    down(EHI[g % 2], ELO[g % 2], ((0, rows),), after)

                            q_item = q.at(q.n)
                            pe.wait_ge(S["split_done"], hs.take(KC))
                            head, body, tail = ffn_schedule(MOE_GROUPS, MOE_LOOP)
                            for s in head:
                                step(*s)
                            item_out()
                            with pe.Fori(0, MOE_LOOP) as i:
                                cs2 = [unit, q, hs]
                                per2 = {unit: 12, q: 24, hs: 4}
                                st2 = looped(cs2, i, per2)
                                for s in body:
                                    step(*s)
                            leave(cs2, st2, per2, MOE_LOOP)
                            step(*tail[0])
                            pe.wait_ge(S["xg_ready"], it * 48 + 96)
                            step(*tail[1], after=prepare)
                            step(*tail[2])

                        sized(pe, size, cs, item)
                        leave_items(cs, st, per, n_items)
                q_item = q.at(q.n)
                item_out()
                for j in range(NT):
                    n = tokens(j)
                    pe.wait_ge(S["combined"], j + 1)
                    for h in range(2):
                        b = misc_bank()
                        dst = PS[:, b, 0:4 * P].rearrange("p (k t) -> p k t", k=4)[:, :, 0:n]
                        pe.matmul(dst, IDR[:], XHI[:, 4 * h:4 * h + 4, j * P:j * P + n], start=True, stop=False)
                        pe.matmul(dst, IDR[:], XLO[:, 4 * h:4 * h + 4, j * P:j * P + n], start=False, stop=False)
                        for k in range(4):
                            c0 = (4 * h + k) * P
                            ins = pe.matmul(PS[:, b, k * P:k * P + n], YG[j % 3][0][0:n, c0:c0 + P], IDF[0:n, 0:n], start=False, stop=(k == 3))
                        ins.then_inc(m.next(), 1)
            pe.wait_ge(S["p_loaded"], 16 * NT * (l + 1))
            for c in range(2):
                for t0, n in BLOCKS:
                    b = misc_bank()
                    for j in range(t0 // P, -(-(t0 + n) // P)):
                        w = tokens(j)
                        ins = pe.transpose(PS[:, b, j * P - t0:j * P - t0 + w], PTOK[0:w, j, c * P:(c + 1) * P], IDF[0:w, 0:w])
                    ins.then_inc(m.next(), 1)
            stats()
            gate_project("p_ready", l + 1, PT, after_first=spread)
        stats()
        for j in range(NT):
            n = tokens(j)
            for h in range(2):
                b = open_bank()
                spacer(pe)
                for k in range(4):
                    ins = pe.transpose(PS[0:n, b, k * P:(k + 1) * P], XNEW[:, 4 * h + k, j * P:j * P + n], IDF[:])
                ins.then_inc(q.next(), 1)

    @block.scalar
    def _(act):
        halves, q, m = Count(S["hi_ready"]), Count(), Count()
        fold, req, split = Count(), Count(S["act_done"]), Count(S["split_hi"])
        kp = [0, kinds]

        def convert(misc=False):
            kind, norm = kp[1][kp[0] // 2]
            kp[0] += 1
            half, tile = halves.n % 2, halves.n // 2
            if norm is not None:
                if half == 0:
                    fold.n += 1
                act.wait_ge(S["folded"], fold.at(fold.n))
            else:
                act.wait_ge(S[f"raw_ready{tile % RAW}"], halves.at(halves.n, 16, 4) + 16)
            if misc:
                act.wait_ge(S["misc_done"], m.at(m.n))
            elif q.n:
                act.wait_ge(S["mm_done"], q.at(q.n))
            act.activation(WHI[halves.n % HL][:], raw_view(tile % RAW, half, kind), ACT.Copy).then_inc(halves.next(), 1)

        def serve(f):
            act.wait_ge(S["act_req"], req.at(req.n + 1))
            f().then_inc(req.next(), 1)

        def split_x(src, j, dst, t0, n, square=True):
            act.wait_ge(S["split_req"], split.at(split.n + 1))
            ins = act.activation(dst, src, ACT.Copy)
            if square:
                ins = act.activation(T[2 + split.n % 2][:, 0:n], src, ACT.Square)
            ins.then_inc(split.next(), 1)

        def norm_sqrt(count=D):
            serve(lambda: act.activation(RTOK[:], RTOK[:], ACT.Sqrt, bias=EPSC[:], scale=1.0 / count))

        def sigmoid_steps(after=lambda d: None):
            for u in range(KC):
                convert()
                for j, (t0, n) in enumerate(BLOCKS):
                    serve(lambda: act.activation(T[req.n % 2][:, 0:n], T[req.n % 2][:, 0:n], ACT.Sigmoid))
                    q.n += 2
                after(u)

        def plain(units, flush=0):
            for u in range(units):
                if u < units - flush:
                    convert()
                q.n += 3

        def states_out_act(sample, prompt, pad, lots):
            for h in range(lots + 1):
                act.wait_ge(S["stage_full"], so.take())
                n = NSEQ * pad // lots if h < lots else pad
                dst = sample.rearrange("s r c -> (s r) c")[h * n:(h + 1) * n, :] if h < lots else prompt
                act.dma_start(dst, OUTST[0:n, :]).then_inc(S["stage_out"], 16)

        so = Count()
        act.wait_ge(S["consts"], 3)
        for t0, n in BLOCKS:
            for c in range(KC):
                act.wait_ge(S["mm_done"], q.n + 1)
                src = PS[:, q.n % BANKS, 0:n]
                act.activation(XHI[:, c, t0:t0 + n], src, ACT.Copy)
                if split.n >= 2:
                    act.wait_ge(S["split_done"], split.n - 1)
                act.activation(T[2 + split.n % 2][:, 0:n], src, ACT.Square).then_inc(split.next(), 1)
                q.n += 1
        m.n += 1
        for _ in range(LOOK):
            convert()
        for l in range(DEPTH):
            m.n += 3
            norm_sqrt()
            plain(2)
            m.n += 1
            convert()
            m.n += NT
            serve(lambda: act.activation(VR[:], MV[:, :, 1], ACT.Sqrt, bias=EPSC[:]))
            convert(misc=True)
            act.wait_ge(S["v_ready"], l + 1)
            act.dma_start(O["v_p"][l, 0], V[:, NT - 2, :]).then_inc(S["v_out"], 16)
            act.dma_start(O["v_s"][l].rearrange("s t c -> (s t) c"), V[0:64, NT - 1, :]).then_inc(S["v_out"], 16)
            m.n += 4
            for c in range(2):
                convert()
                q.n += 3
                act.wait_ge(S["act_req"], req.at(req.n + 1))
                gp, gs = GLU[:, c, PB:PB + SEQ], GLU[:, c, PB + SEQ:].rearrange("p (s t) -> p s t", s=NSEQ)[:, :, PB:]
                act.activation(gp, gp, ACT.Sigmoid)
                act.activation(gs, gs, ACT.Sigmoid).then_inc(req.next(), 1)
            plain(2)
            m.n += 5 + 3
            states_out_act(O["b_s"][l], O["b_p"][l, 0], PB, 2)
            sigmoid_steps()
            plain(4)
            m.n += 2
            states_out_act(O["a_s"][l], O["a_p"][l, 0], PA, 1)
            plain(2)
            sigmoid_steps()
            m.n += 3
            plain(1)
            norm_sqrt(DB)
            plain(1)
            m.n += 1 + 3
            act.wait_ge(S["act_req"], req.at(req.n + 1))
            act.activation(YB[:, 0, :], YB[:, 0, :], ACT.Silu, bias=par(l, 0, R_LB), scale=par(l, 0, R_LG))
            act.activation(YB[:, 1, :], YB[:, 1, :], ACT.Silu, bias=par(l, 1, R_LB), scale=par(l, 1, R_LG)).then_inc(req.next(), 1)
            m.n += 2
            states_out_act(O["c_s"][l], O["c_p"][l, 0], PC, 1)
            sigmoid_steps()
            m.n += 6

            def merge_high(d):
                act.wait_ge(S["split_req"], split.at(split.n + 1))
                act.activation(MHI[:, d, :], MIXED[:, d, :], ACT.Copy).then_inc(split.next(), 1)

            sigmoid_steps(after=lambda d: merge_high(d) if d < MERGE_EARLY else None)
            for d in range(MERGE_EARLY, KC):
                merge_high(d)
            for d in range(KC):
                if not (l == 1 and d >= KC - LOOK):
                    convert()
                for t0, n in BLOCKS:
                    split_x(T[split.n % 2][:, 0:n], 0, XHI[:, d, t0:t0 + n], t0, n)
                q.n += 3
            m.n += 1
            norm_sqrt()
            if l == 0:
                m.n += 3
                def step(kind, g, last=False):
                    if kind == "GU":
                        for f in range(2):
                            convert()
                            q.n += 3
                            for t0, n in BLOCKS:
                                serve(lambda: act.activation(GS[:, f, t0:t0 + n], GS[:, f, t0:t0 + n], ACT.Silu))
                        for f in range(2):
                            convert()
                            q.n += 3
                            for t0, n in BLOCKS:
                                act.wait_ge(S["split_req"], split.at(split.n + 1))
                                act.activation(HHI[g % 2][:, f, t0:t0 + n], T[split.n % 2][:, 0:n], ACT.Copy).then_inc(split.next(), 1)
                    else:
                        convert()
                        if last:
                            for d in range(KC):
                                for t0, n in BLOCKS:
                                    split_x(T[split.n % 2][:, 0:n], 0, XHI[:, d, t0:t0 + n], t0, n)
                        q.n += 24
                        convert()

                head, body, tail = ffn_schedule(FFN_GROUPS, FFN_LOOP)
                for s in head:
                    step(*s)
                cs = [halves, q, fold, req, split]
                per = {halves: 12, q: 72, fold: 4, req: 12, split: 12}
                with act.Fori(0, FFN_LOOP) as i:
                    st = looped(cs, i, per)
                    for s in body:
                        step(*s)
                leave(cs, st, per, FFN_LOOP)
                kp[0] += 12 * (FFN_LOOP - 1)
                for s in tail:
                    step(*s, last=(s == tail[-1]))
            else:
                for k in range(2):
                    serve(lambda: act.activation(TW[:, k, :], TW[:, k, :], ACT.Sigmoid))
                m.n += 2
                q.n += 2 * NT
                act.wait_ge(S["items_ready"], 1)
                n_items = act.value_load(ITEMS[0:1, L_NUM:L_NUM + 1], min_val=NE, max_val=SLOTS)
                cs = [halves, q, m, req, split]
                per = {halves: 2 * len(item_kinds), q: 12 * MOE_GROUPS, m: 14, req: 2 * MOE_GROUPS, split: KC + 2 * MOE_GROUPS}
                main, kp_main = kinds, kp[0]
                kp[0], kp[1] = 0, item_kinds * 2
                for _ in range(LOOK):
                    convert()

                def prepare(k):
                    act.wait_ge(S["split_req"], split.at(split.n + 1))
                    act.activation(XSH[:, k, :], T[split.n % 2][:, 0:CAP], ACT.Copy).then_inc(split.next(), 1)

                def item_out(number, row):
                    act.wait_ge(S["ys_out"], number * 48)
                    for j, (r0, n) in enumerate(XBLK):
                        act.wait_ge(S["ys_full"], number * 3 + (j + 1))
                        act.dma_start(YS[bass.ds(row + r0, n), :], YT[j][0:n, :]).then_inc(S["ys_out"], 16)

                for k in range(KC):
                    prepare(k)
                m.n += KC
                with act.Fori(0, SLOTS) as it:
                    with act.If(it < n_items):
                        size = act.value_load(ITEMS[0:1, bass.ds(it + L_SIZE, 1)], min_val=0, max_val=len(SIZES) - 1)
                        row = act.value_load(ITEMS[0:1, bass.ds(it + L_ROW, 1)], min_val=0, max_val=PAIRS)
                        st = looped(cs, it, per)

                        def conv():
                            ahead = kp[0] - 2 * len(item_kinds)
                            if ahead >= 0:
                                with act.If(n_items < it + 2):
                                    act.wait_ge(S["folded"], fold.at(fold.n + 1 + ahead // 2))
                                    act.sem_inc(S["spacer"], 1)
                            convert()

                        def item(rows):
                            kp[0] = LOOK

                            def step(kind, g, between=lambda: None):
                                if kind == "GU":
                                    for f in range(2):
                                        conv()
                                        q.n += 1
                                        serve(lambda: act.activation(EG[:, f, 0:rows], EG[:, f, 0:rows], ACT.Silu))
                                    for f in range(2):
                                        conv()
                                        q.n += 1
                                        act.wait_ge(S["split_req"], split.at(split.n + 1))
                                        act.activation(EHI[g % 2][:, f, 0:rows], T[split.n % 2][:, 0:rows], ACT.Copy).then_inc(split.next(), 1)
                                else:
                                    conv()
                                    between()
                                    q.n += KC
                                    conv()

                            head, body, tail = ffn_schedule(MOE_GROUPS, MOE_LOOP)
                            for s in head:
                                step(*s)
                            item_out(it, row)
                            m.n += 6
                            cs2 = [halves, q, req, split]
                            per2 = {halves: 12, q: 24, req: 4, split: 4}
                            with act.Fori(0, MOE_LOOP) as i:
                                st2 = looped(cs2, i, per2)
                                for s in body:
                                    step(*s)
                            leave(cs2, st2, per2, MOE_LOOP)
                            kp[0] += 12 * (MOE_LOOP - 1)
                            step(*tail[0])
                            step(*tail[1], between=lambda: [prepare(k) for k in range(KC)])
                            m.n += KC
                            step(*tail[2])

                        sized(act, size, cs, item)
                        leave_items(cs, st, per, n_items)
                row = act.value_load(ITEMS[0:1, bass.ds(n_items + L_ROW, 1)], min_val=0, max_val=PAIRS)
                item_out(n_items, row)
                m.n += 6
                kp[0], kp[1] = kp_main + LOOK, kinds
                fold.n += (LOOK + 1) // 2

                def weigh(j):
                    n = tokens(j)
                    act.wait_ge(S[f"gathered{j % 3}"], 32 * (j // 3 + 1))
                    y0 = YG[j % 3][0][0:n, :]
                    act.activation(y0, y0, ACT.Copy, scale=TW[0:n, 0, j:j + 1]).then_inc(S["weighted"], 1)

                weigh(0)
                for j in range(NT):
                    n = tokens(j)
                    if j + 1 < NT:
                        weigh(j + 1)
                    for h in range(2):
                        act.wait_ge(S["misc_done"], m.at(m.n + 1))
                        act.sem_inc(S["spacer"], 1)
                        src = PS[:, 6 + m.n % 2, 0:4 * P].rearrange("p (k t) -> p k t", k=4)[:, :, 0:n]
                        act.activation(XHI[:, 4 * h:4 * h + 4, j * P:j * P + n], src, ACT.Copy)
                        if j or h:
                            act.wait_ge(S["split_done"], split.at(split.n - 1))
                            act.sem_inc(S["spacer"], 1)
                        act.activation(TC[h][:, :, 0:n], src, ACT.Square).then_inc(split.next(), 1)
                        m.n += 1
            m.n += 6 + 1
            norm_sqrt()
            m.n += 3
            for d in range(KC):
                if not (l == 1 and d >= KC - LOOK):
                    convert()
                for t0, n in BLOCKS:
                    serve(lambda: act.activation(T[req.n % 2][:, 0:n], T[req.n % 2][:, 0:n], ACT.Sigmoid))
                    q.n += 2
                    act.wait_ge(S["split_req"], split.at(split.n + 1))
                    act.activation(T[2 + split.n % 2][:, 0:n], XNEW[:, d, t0:t0 + n], ACT.Square).then_inc(split.next(), 1)
            if l == 0:
                for d in range(KC):
                    act.wait_ge(S["split_req"], split.at(split.n + 1))
                    act.activation(XHI[:, d, :], XNEW[:, d, :], ACT.Copy).then_inc(split.next(), 1)
        norm_sqrt()
        for j in range(NT):
            n = tokens(j)
            act.wait_ge(S["y_full"], j + 1)
            dst = O["y_p"][0, j * P:(j + 1) * P, :] if j < NT - 1 else O["y_s"].rearrange("s t d -> (s t) d")
            act.dma_start(dst, YOUT[j % 2][0:n, :]).then_inc(S[f"outputs{j % 2}"], 16)
        act.wait_ge(S["outputs0"], 16 * ((NT + 1) // 2))
        act.wait_ge(S["outputs1"], 16 * (NT // 2))
        act.wait_ge(S["stage_out"], 16 * 7 * DEPTH)
        act.wait_ge(S["v_out"], 32 * DEPTH)

    @block.vector
    def _(dve):
        v = Engine(dve, S["dve_own"])
        conv, q, m = Count(S["lo_ready"]), Count(S["evicted"]), Count(S["misc_free"])
        req, split = Count(S["act_req"]), Count(S["split_done"])
        sreq = Count(S["split_req"])
        kp = [0, kinds]
        def convert():
            kind, norm = kp[1][kp[0] // 2]
            kp[0] += 1
            dve.wait_ge(S["hi_ready"], conv.at(conv.n + 1))
            s = conv.n % HL
            v.do(dve.tensor_tensor(WLO[s][:], raw_view(conv.n // 2 % RAW, conv.n % 2, kind), WHI[s][:].bitcast(F32), ALU.subtract), conv)

        def main_ready():
            dve.wait_ge(S["mm_done"], q.at(q.n + 1))
            return PS[:, q.n % BANKS, :]

        def misc_ready():
            dve.wait_ge(S["misc_done"], m.at(m.n + 1))
            return PS[:, 6 + m.n % 2, :]

        pending = []

        def finish_x():
            if not pending:
                return
            d, j, src, n_req, low = pending.pop()
            t0, n = BLOCKS[j]
            dve.wait_ge(S["split_hi"], sreq.at(n_req))
            if low:
                v.do(dve.tensor_tensor(XLO[:, d, t0:t0 + n], src, XHF[:, d, t0:t0 + n], ALU.subtract))
            sq = T[2 + (n_req - 1) % 2][:, 0:n]
            if d == 0:
                v.do(dve.tensor_copy(SQS[:, t0:t0 + n], sq), split)
            else:
                v.do(dve.tensor_tensor(SQS[:, t0:t0 + n], SQS[:, t0:t0 + n], sq, ALU.add), split)
            v.sync()

        def split_x(d, j, src, low=True):
            dve.sem_inc(sreq.next(), 1)
            finish_x()
            pending.append((d, j, src, sreq.n, low))

        def norm_tokens():
            ps = misc_ready()
            v.do(dve.tensor_copy(RTOK[:, 0:NT - 1], ps[:, 0:NT - 1]))
            v.do(dve.tensor_copy(RTOK[0:64, NT - 1:NT], ps[0:64, NT - 1:NT]), m)
            request()
            v.do(dve.reciprocal(RTOK[:], RTOK[:]))
            v.sync()

        def diagonals():
            for j, (t0, n) in enumerate(BLOCKS):
                whole = n // P
                dst = T[j][:, 0:whole * P].rearrange("p (j t) -> p j t", t=P)
                c0 = t0 // P
                v.do(dve.tensor_tensor(dst, IDF[:].unsqueeze(1).to_broadcast([P, whole, P]),
                                       RTOK[:, c0:c0 + whole].unsqueeze(2).to_broadcast([P, whole, P]), ALU.mult))
                if n % P:
                    v.do(dve.tensor_scalar(T[j][:, whole * P:n], IDF[:, 0:n % P], RTOK[:, c0 + whole:c0 + whole + 1], None, ALU.mult))
            v.sync()
            dve.sem_inc(S["diag_ready"], 1)

        def spread_rstd():
            for t0, n in BLOCKS:
                ps = misc_ready()
                v.do(dve.tensor_copy(RSTD[:, t0:t0 + n], ps[:, 0:n]), m)
            v.sync()

        def norm():
            norm_tokens()
            diagonals()
            spread_rstd()

        def request():
            v.sync()
            dve.sem_inc(req.next(), 1)
            dve.wait_ge(S["act_done"], req.at(req.n))

        bg = [iter(())]

        def background(k):
            for _ in range(k):
                next(bg[0], None)

        def merge_low(d):
            dve.wait_ge(S["split_hi"], split.at(split.n + 1))
            v.do(dve.tensor_tensor(MLO[:, d, :], MIXED[:, d, :], MHI[:, d, :].bitcast(F32), ALU.subtract), split)

        def gate_project(br_first, br_pulls, merge=False):
            for d in range(KC):
                convert()
                if merge and 1 <= d <= MERGE_EARLY:
                    merge_low(d - 1)
                for t0, n in BLOCKS:
                    ps = main_ready()
                    t = T[req.n % 2][:, 0:n]
                    v.do(dve.tensor_tensor(t, ps[:, 0:n], RSTD[:, t0:t0 + n], ALU.mult), q)
                    v.sync()
                    dve.sem_inc(req.next(), 1)
                    background(br_pulls)
                    ps = main_ready()
                    dve.wait_ge(S["act_done"], req.at(req.n))
                    dst = MIXED[:, d, t0:t0 + n]
                    if br_first:
                        v.do(dve.tensor_tensor(dst, ps[:, 0:n], t, ALU.mult), q)
                        v.sync()
                    else:
                        mk = v.do(dve.tensor_tensor(t, ps[:, 0:n], t, ALU.mult), q)
                        v.sync(mk)
                        v.do(dve.tensor_tensor(dst, dst, t, ALU.add))
                        v.sync()
                if merge:
                    dve.sem_inc(sreq.next(), 1)

        def padded_unit(buf, pad, c, times=False, tmp=[0]):
            convert()
            for j, (t0, n) in enumerate(BLOCKS):
                ps = main_ready()
                ps_r = ps
                if times:
                    t = T[2 + tmp[0] % 2]
                    tmp[0] += 1
                    v.do(dve.tensor_tensor(t[:, 0:n], ps[:, 0:n], RSTD[:, t0:t0 + n], ALU.mult), q)
                    v.sync()
                    for a, b, dst in pieces(j, buf[:, c, :], pad):
                        v.do(dve.tensor_tensor(dst, dst, shaped(t[:, a:a + b], dst), ALU.mult))
                    v.sync()
                else:
                    ds = pieces(j, buf[:, c, :], pad)
                    for x, (a, b, dst) in enumerate(ds):
                        v.do(dve.tensor_tensor(dst, shaped(ps[:, a:a + b], dst), shaped(RSTD[:, t0 + a:t0 + a + b], dst), ALU.mult),
                             q if x == len(ds) - 1 else None)
                background(1)
            v.sync()

        def pad_sample(buf, c, pad):
            return buf[:, c, pad + SEQ:].rearrange("p (s t) -> p s t", s=NSEQ)

        def states_out(buf, tmp, pad, lots):
            for c in range(2):
                x = pad_sample(buf, c, pad)[:, :, DSEQ:]
                v.do(dve.tensor_copy(tmp[:, c, 0:NSEQ * pad].rearrange("p (s t) -> p s t", s=NSEQ), x), tok if c == 1 else None)
            for h in range(lots + 1):
                n = NSEQ * pad // lots if h < lots else pad
                ps = misc_ready()
                if stage.n:
                    dve.wait_ge(S["stage_out"], 16 * stage.n)
                v.do(dve.tensor_copy(OUTST[0:n, :], ps[0:n, 0:DB]), stage)
                v.sync()
                dve.sem_inc(m.next(), 1)

        tok, stage = Count(S["tok_ready"]), Count(S["stage_full"])

        for t_, val in ((ONES, 1.0), (EPSC, EPS)):
            v.do(dve.memset(t_[:], val))
        v.do(dve.memset(BDRAW[:], 0.0))
        v.do(dve.memset(PBD[:], 0.0))
        for c in range(2):
            for h in range(2):
                v.do(dve.memset(WIN[64 * h:64 * h + 64, c:c + 1], float(WINDOWS[2 * c + h])))
        v.sync()
        dve.sem_inc(S["sgu_zeroed"], 1)
        v.do(dve.reciprocal(WINV[:], WIN[:]))
        dve.wait_ge(S["consts"], 3)
        v.do(dve.tensor_copy(IDR[:], IDF[:]))
        for c in range(2):
            v.do(dve.tensor_scalar(FIXT[:, c, :], FIXT[:, c, :], WIN[:, c:c + 1], None, ALU.min))
        v.sync()
        v.do(dve.reciprocal(FIXT[:], FIXT[:]))
        v.sync()
        sqc = Count(S["sq_ready"])
        v.do(dve.memset(RTOK[:], 1.0))
        for j, (t0, n) in enumerate(BLOCKS):
            for c in range(KC):
                ps = main_ready()
                dve.wait_ge(S["split_hi"], split.n + 1)
                sreq.n += 1
                v.do(dve.tensor_tensor(XLO[:, c, t0:t0 + n], ps[:, 0:n], XHF[:, c, t0:t0 + n], ALU.subtract), q)
                sq = T[2 + split.n % 2][:, 0:n]
                if c == 0:
                    v.do(dve.tensor_copy(SQS[:, t0:t0 + n], sq), split)
                else:
                    v.do(dve.tensor_tensor(SQS[:, t0:t0 + n], SQS[:, t0:t0 + n], sq, ALU.add), split)
                v.sync()
            if j == 0:
                ps = misc_ready()
                v.do(dve.tensor_copy(PAR[:], ps[:, 0:4 * 38 + 7 * KC]), m)
                v.sync()
                dve.sem_inc(S["par_ready"], 1)
        dve.sem_inc(S["split_req"], sreq.n)
        dve.sem_inc(sqc.next(), 1)
        for _ in range(LOOK):
            convert()

        for l in range(DEPTH):
            if l:
                for d in range(KC):
                    dve.wait_ge(S["split_hi"], sreq.at(sreq.n - KC + d + 1))
                    v.do(dve.tensor_tensor(XLO[:, d, :], XNEW[:, d, :], XHF[:, d, :], ALU.subtract), split)
                v.sync()
                v.do(dve.memset(BDRAW[:], 0.0))
                v.sync()
                dve.sem_inc(S["sgu_zeroed"], 1)
            norm()
            v.do(dve.memset(MV[:], 1.0))
            for c in range(2):
                convert()
                for t0, n in BLOCKS:
                    ps = main_ready()
                    v.do(dve.tensor_tensor(UB[:, c, t0:t0 + n], ps[:, 0:n], RSTD[:, t0:t0 + n], ALU.mult), q)
            convert()
            for j in range(NT):
                n = tokens(j)
                ps = misc_ready()
                v.do(dve.tensor_scalar(V[0:n, j, :], ps[0:n, 0:DB], RTOK[0:n, j:j + 1], None, ALU.mult), m)
                v.sync()
                v.do(dve.bn_stats(BNS[0:n, j, :], V[0:n, j, :]))
                v.sync()
                v.do(dve.bn_aggr(MV[0:n, j, :], BNS[0:n, j, :]))
            ps = misc_ready()
            v.do(dve.tensor_tensor(WT[:], ps.rearrange("p (g t) -> p g t", g=GROUPS), TRIL[:].unsqueeze(1).to_broadcast([P, GROUPS, P]),
                                   ALU.mult), m)
            ps = misc_ready()
            v.do(dve.tensor_tensor(BD[:], ps[0:64, 0:GROUPS * 64].rearrange("p (g t) -> p g t", g=GROUPS),
                                   TRIL[0:64, 0:64].unsqueeze(1).to_broadcast([64, GROUPS, 64]), ALU.mult), m)
            v.do(dve.memset(GLU[:, :, 0:PB], 0.0))
            ps = misc_ready()
            for c in range(2):
                for h in range(2):
                    x = (c * 2 + h) * 120
                    v.do(dve.tensor_copy(pad_sample(GLU, c, PB)[:, 4 * h:4 * h + 4, 0:PB], ps[:, x:x + 120].rearrange("p (s t) -> p s t", s=4)),
                         m if (c, h) == (1, 1) else None)
            ps = misc_ready()
            v.do(dve.tensor_copy(KEEP[:], ps[:, 0:272]), m)
            v.sync()
            v.sync()
            dve.sem_inc(req.next(), 1)
            dve.wait_ge(S["act_done"], req.at(req.n))
            v.do(dve.reciprocal(VR[:], VR[:]))
            v.sync()
            for j in range(NT):
                n = tokens(j)
                v.do(dve.tensor_scalar(V[0:n, j, :], V[0:n, j, :], MV[0:n, j, 0:1], VR[0:n, j:j + 1], ALU.subtract, ALU.mult))
            v.sync()
            dve.wait_ge(S["sgu_loaded"], 16 * (1 + NSEQ + GROUPS + 2) * (l + 1))
            for j in range(NT):
                n = tokens(j)
                v.do(dve.tensor_tensor(V[0:n, j, :], V[0:n, j, :], LNG[0:n, :], ALU.mult))
            v.sync()
            for j in range(NT):
                n = tokens(j)
                v.do(dve.tensor_tensor(V[0:n, j, :], V[0:n, j, :], LNB[0:n, :], ALU.add))
            v.sync()
            dve.sem_inc(S["v_ready"], 1)
            convert()
            for c in range(2):
                padded_unit(GLU, PB, c)
                dve.sem_inc(req.next(), 1)
                dve.wait_ge(S["act_done"], req.at(req.n))
            for c in range(2):
                padded_unit(GLU, PB, c, times=True)
            for c in range(2):
                for jj in range(2):
                    ps = misc_ready()
                    t4 = YB[:, c, jj * 512:jj * 512 + 512]
                    v.do(dve.tensor_tensor(t4.rearrange("p (j t) -> p j t", j=4), ps.rearrange("p (j t) -> p j t", j=4),
                                           BIAS[:, c, :].unsqueeze(1).to_broadcast([P, 4, P]), ALU.add), m)
                    v.sync()
                    u4 = UB[:, c, jj * 512:jj * 512 + 512]
                    v.do(dve.tensor_tensor(u4, u4, t4, ALU.mult))
            ps = misc_ready()
            for c in range(2):
                v.do(dve.tensor_tensor(YB[:, c, SEQ:].rearrange("p (s t) -> p s t", s=NSEQ), ps[:, c * 64:c * 64 + 64].rearrange("p (s t) -> p s t", s=NSEQ),
                                       BIAS[:, c, 0:DSEQ].unsqueeze(1).to_broadcast([P, NSEQ, DSEQ]), ALU.add), m if c else None)
            v.sync()
            v.do(dve.tensor_tensor(UB[:, :, SEQ:], UB[:, :, SEQ:], YB[:, :, SEQ:], ALU.mult))
            v.sync()
            dve.sem_inc(S["br_d"], 1)
            states_out(GLU, YB, PB, 2)

            def conv_b():
                parts = []
                for c in range(2):
                    parts.append((c, lambda k, c=c: GLU[:, c, k:k + SEQ], YB[:, c, 0:SEQ]))
                    parts.append((c, lambda k, c=c: pad_sample(GLU, c, PB)[:, :, k:k + DSEQ], YB[:, c, SEQ:].rearrange("p (s t) -> p s t", s=NSEQ)))
                marks = [None] * 4
                for k in range(PB + 1):
                    for x, (c, src, dst) in enumerate(parts):
                        w = par(l, c, R_CB + k)
                        if k == 0:
                            marks[x] = v.do(dve.tensor_scalar(dst, src(k), w, par(l, c, R_BIAS), ALU.mult, ALU.add))
                        else:
                            v.sync(marks[x])
                            marks[x] = v.do(dve.scalar_tensor_tensor(dst, src(k), w, dst, ALU.mult, ALU.add))
                        yield

            bg[0] = conv_b()
            dve.wait_ge(S["v_out"], 32 * (l + 1))
            gate_project(True, 2)
            v.do(dve.memset(ZA[:, :, 0:PA], 0.0))
            for c in range(2):
                v.do(dve.tensor_copy(pad_sample(ZA, c, PA)[:, :, 0:PA], KEEP[:, 240 + c * 16:256 + c * 16].rearrange("p (s t) -> p s t", s=NSEQ)))
            for c in range(2):
                padded_unit(ZA, PA, c)
            for c in range(2):
                padded_unit(ZA, PA, c, times=True)
            states_out(ZA, YA, PA, 1)
            for k in range(PA + 1):
                for c in range(2):
                    for src, dst in ((ZA[:, c, k:k + SEQ], YA[:, c, 0:SEQ]),
                                     (pad_sample(ZA, c, PA)[:, :, k:k + DSEQ], YA[:, c, SEQ:].rearrange("p (s t) -> p s t", s=NSEQ))):
                        w = par(l, c, R_CA + k)
                        if k == 0:
                            v.do(dve.tensor_scalar(dst, src, w, None, ALU.mult))
                        else:
                            v.do(dve.scalar_tensor_tensor(dst, src, w, dst, ALU.mult, ALU.add))
                v.sync()
            for c in range(2):
                convert()
                for t0, n in BLOCKS:
                    ps = main_ready()
                    t = T[2]
                    v.do(dve.tensor_tensor(t[:, 0:n], ps[:, 0:n], RSTD[:, t0:t0 + n], ALU.mult), q)
                    v.sync()
                    v.do(dve.tensor_tensor(YA[:, c, t0:t0 + n], YA[:, c, t0:t0 + n], t[:, 0:n], ALU.mult))
                    v.sync()
            dve.sem_inc(S["br_a"], 1)
            gate_project(False, 3)
            for _ in bg[0]:
                pass
            v.sync()
            dve.sem_inc(S["yb_ready"], 1)
            for t0, n in BLOCKS:
                ps = misc_ready()
                for c in range(2):
                    v.do(dve.scalar_tensor_tensor(YB[:, c, t0:t0 + n], ps[:, 0:n], -1.0 / DB, YB[:, c, t0:t0 + n], ALU.mult, ALU.add), m if c else None)
                v.sync()
                v.do(dve.tensor_tensor(SQB[:, :, t0:t0 + n], YB[:, :, t0:t0 + n], YB[:, :, t0:t0 + n], ALU.mult))
            v.sync()
            dve.sem_inc(S["lnsq_ready"], 1)
            v.do(dve.memset(ZP[:, :, 0:PC], 0.0))
            for c in range(2):
                v.do(dve.tensor_copy(pad_sample(ZP, c, PC)[:, :, 0:PC], KEEP[:, c * 120:c * 120 + 120].rearrange("p (s t) -> p s t", s=NSEQ)))
            padded_unit(ZP, PC, 0)
            norm_tokens()
            diagonals()
            padded_unit(ZP, PC, 1)
            for t0, n in BLOCKS:
                ps = misc_ready()
                for c in range(2):
                    y = YB[:, c, t0:t0 + n]
                    v.do(dve.tensor_tensor(y, y, ps[:, 0:n], ALU.mult), m if c else None)
            v.sync()
            dve.sem_inc(req.next(), 1)
            dve.wait_ge(S["act_done"], req.at(req.n))
            dve.sem_inc(S["br_b"], 1)
            states_out(ZP, YP, PC, 1)

            def pool_c():
                def at_(c, s, h):
                    a, b = (64 * h if h is not None else 0), (64 * h + 64 if h is not None else P)
                    return ((ZP[a:b, c, PC - s:PC - s + SEQ], YP[a:b, c, 0:SEQ]),
                            (pad_sample(ZP, c, PC)[a:b, :, PC - s:PC - s + DSEQ], YP[a:b, c, SEQ:].rearrange("p (s t) -> p s t", s=NSEQ)))
                last = [None, None]
                for s in range(1, POOL_MAX):
                    for c in range(2):
                        w0, w1 = WINDOWS[2 * c], WINDOWS[2 * c + 1]
                        if s >= w1:
                            continue
                        h = None if s < w0 else 1
                        if last[c]:
                            v.sync(last[c])
                        for x, (src, dst) in enumerate(at_(c, s, h)):
                            first = at_(c, 0, h)[x][0] if s == 1 else dst
                            last[c] = v.do(dve.tensor_tensor(dst, first, src, ALU.add))
                            yield
                v.sync()
                for c in range(2):
                    v.do(dve.tensor_tensor(YP[:, c, 0:16], YP[:, c, 0:16], FIXT[:, c, :], ALU.mult))
                    (src, dst), (ssrc, sdst) = at_(c, 0, None)
                    v.do(dve.scalar_tensor_tensor(dst[:, 16:], dst[:, 16:], WINV[:, c:c + 1], src[:, 16:], ALU.mult, ALU.subtract))
                    v.do(dve.scalar_tensor_tensor(sdst, sdst, WINV[:, c:c + 1], ssrc, ALU.mult, ALU.subtract))
                    yield
                v.sync()
                for c in range(2):
                    v.do(dve.tensor_tensor(YP[:, c, 0:16], YP[:, c, 0:16], ZP[:, c, PC:PC + 16], ALU.subtract))
                v.sync()
                yield

            bg[0] = pool_c()
            gate_project(False, 2)
            for _ in bg[0]:
                pass
            v.sync()
            dve.sem_inc(S["pooled"], 1)
            for c in range(2):
                for t0, n in BLOCKS:
                    ps = misc_ready()
                    v.do(dve.tensor_scalar(YP[:, c, t0:t0 + n], ps[:, 0:n], par(l, c, R_PS), None, ALU.mult), m)
            v.sync()
            dve.sem_inc(S["br_c"], 1)
            gate_project(False, 0, merge=True)
            for d in range(MERGE_EARLY, KC):
                merge_low(d)
            v.sync()
            for d in range(KC):
                if not (l == 1 and d >= KC - LOOK):
                    convert()
                for j, (t0, n) in enumerate(BLOCKS):
                    ps = main_ready()
                    t = T[sreq.n % 2][:, 0:n]
                    v.do(dve.tensor_tensor(t, ps[:, 0:n], XHF[:, d, t0:t0 + n], ALU.add), q)
                    v.sync()
                    v.do(dve.tensor_tensor(t, t, XLF[:, d, t0:t0 + n], ALU.add))
                    v.sync()
                    split_x(d, j, t)
            finish_x()
            dve.sem_inc(sqc.next(), 1)
            dve.wait_ge(S["stage_out"], 16 * stage.n)
            if l == 0:
                norm()
                for d in range(KC):
                    v.do(dve.tensor_tensor(ACC[:, d, :], XHF[:, d, :], XLF[:, d, :], ALU.add))
                v.sync()

                def step(kind, g, last=False):
                    if kind == "GU":
                        for f in range(2):
                            convert()
                            for t0, n in BLOCKS:
                                ps = main_ready()
                                v.do(dve.tensor_tensor(GS[:, f, t0:t0 + n], ps[:, 0:n], RSTD[:, t0:t0 + n], ALU.mult), q)
                                v.sync()
                                dve.sem_inc(req.next(), 1)
                        for f in range(2):
                            convert()
                            for j, (t0, n) in enumerate(BLOCKS):
                                ps = main_ready()
                                t = T[sreq.n % 2][:, 0:n]
                                if f == 0 and j == 0:
                                    dve.wait_ge(S["act_done"], req.at(req.n))
                                v.do(dve.tensor_tensor(t, ps[:, 0:n], RSTD[:, t0:t0 + n], ALU.mult), q)
                                v.sync()
                                v.do(dve.tensor_tensor(t, t, GS[:, f, t0:t0 + n], ALU.mult))
                                v.sync()
                                dve.sem_inc(sreq.next(), 1)
                                dve.wait_ge(S["split_hi"], sreq.at(sreq.n))
                                v.do(dve.tensor_tensor(HLO[g % 2][:, f, t0:t0 + n], t, HHI[g % 2][:, f, t0:t0 + n].bitcast(F32), ALU.subtract), split)
                                v.sync()
                    else:
                        convert()
                        for d in range(KC):
                            for j, (t0, n) in enumerate(BLOCKS):
                                ps = main_ready()
                                if last:
                                    t = T[sreq.n % 2][:, 0:n]
                                    v.do(dve.tensor_tensor(t, ps[:, 0:n], ACC[:, d, t0:t0 + n], ALU.add), q)
                                    v.sync()
                                    split_x(d, j, t)
                                else:
                                    a = ACC[:, d, t0:t0 + n]
                                    v.do(dve.tensor_tensor(a, ps[:, 0:n], a, ALU.add), q)
                        finish_x()
                        v.sync()
                        convert()

                head, body, tail = ffn_schedule(FFN_GROUPS, FFN_LOOP)
                for s in head:
                    step(*s)
                cs = [conv, q, req, split, sreq, v.own]
                per = {conv: 12, q: 72, req: 12, split: 12, sreq: 12, v.own: 12}
                with dve.Fori(0, FFN_LOOP) as i:
                    st = looped(cs, i, per)
                    for s in body:
                        step(*s)
                leave(cs, st, per, FFN_LOOP)
                kp[0] += 12 * (FFN_LOOP - 1)
                for s in tail:
                    step(*s, last=(s == tail[-1]))
                dve.sem_inc(sqc.next(), 1)
            else:
                v.do(dve.memset(XG[:], 0.0))
                v.sync()
                dve.sem_inc(S["phase_clear"], 1)
                v.do(dve.tensor_tensor(TRIS[:], TRIL[:], IDF[:], ALU.subtract))
                v.do(dve.memset(LG[:], 0.0))
                dve.wait_ge(S["rw_loaded"], 16)
                v.do(dve.tensor_tensor(RW[:], RW[:], gain(3).unsqueeze(2).to_broadcast([P, KC, NE]), ALU.mult))
                v.sync()
                v.do(dve.tensor_copy(RWH[:], RW[:]))
                v.sync()
                v.do(dve.tensor_tensor(RWL[:], RW[:], RWH[:].bitcast(F32), ALU.subtract))
                v.sync()
                dve.sem_inc(S["tri_ready"], 1)
                norm_tokens()
                ps = misc_ready()
                full, rest = NT - 1, tokens(NT - 1)
                v.do(dve.tensor_tensor(LG[:, 0:full, :], ps[:, 0:full * NE].rearrange("p (j e) -> p j e", e=NE),
                                       RTOK[:, 0:full].unsqueeze(2).to_broadcast([P, full, NE]), ALU.mult))
                v.do(dve.tensor_scalar(LG[0:rest, full, :], ps[0:rest, full * NE:NT * NE], RTOK[0:rest, full:NT], None, ALU.mult), m)
                v.sync()
                for j in range(NT):
                    v.do(dve.max(MX[:, j, :], LG[:, j, :]))
                v.sync()
                for j in range(NT):
                    v.do(dve.max_index(IX[:, j, :], MX[:, j, :], LG[:, j, :]))
                for k in range(2):
                    v.do(dve.tensor_tensor(TW[:, k, :], MX[:, :, k], MX[:, :, 1 - k], ALU.subtract))
                v.sync()
                dve.sem_inc(req.next(), 1)
                request()
                v.do(dve.tensor_copy(IXF[:], IX[:]))
                v.sync()
                dve.wait_ge(S["consts"], 5)
                for k in range(2):
                    v.do(dve.tensor_tensor(OH[k][:], IOT[:].unsqueeze(1).to_broadcast([P, NT, NE]),
                                           IXF[:, :, k:k + 1].to_broadcast([P, NT, NE]), ALU.is_equal))
                v.sync()
                v.do(dve.tensor_tensor(SS[:], OH[0][:], OH[1][:], ALU.add))
                v.do(dve.memset(CS[:, 0, :], 0.0))
                v.sync()
                v.do(dve.memset(SS[rest:P, full, :], 0.0))
                v.sync()
                for j in range(1, NT + 1):
                    v.do(dve.tensor_tensor(CS[:, j, :] if j < NT else TM[:, 0, :], CS[:, j - 1, :], SS[:, j - 1, :], ALU.add))
                    v.sync()
                dve.sem_inc(S["counts_ready"], 1)
                ps = misc_ready()
                v.do(dve.tensor_copy(CNT[:], ps[:, NT * NE:(NT + 1) * NE]))
                v.do(dve.memset(BASE[:, 0:1], 0.0))
                v.sync()
                for e in range(1, NE):
                    v.do(dve.tensor_tensor(BASE[:, e:e + 1], BASE[:, e - 1:e], CNT[:, e - 1:e], ALU.add))
                    v.sync()
                v.do(dve.tensor_tensor(TM[:], ps[:, 0:NT * NE].rearrange("p (j e) -> p j e", e=NE),
                                       BASE[:].unsqueeze(1).to_broadcast([P, NT, NE]), ALU.add), m)
                v.sync()
                for k in range(2):
                    v.do(dve.tensor_tensor(OH[k][:], OH[k][:], TM[:], ALU.mult))
                v.sync()
                for k in range(2):
                    v.do(dve.tensor_reduce(POSF[:, k, :], OH[k][:], AXX, ALU.add))
                v.sync()
                v.do(dve.tensor_copy(POSI[:], POSF[:]))
                v.sync()
                lrow = lambda r: LROW[0:1, r, :]
                further = lambda r, p_: LROW[0:1, r, 0:NE * EXTRA].rearrange("o (e x) -> o e x", x=EXTRA)[:, :, p_ - 1]
                firsts = lambda r: LROW[0:1, r, NE * EXTRA:NJ]
                ACTIVE, PLACE, EXPERT, ROW, OTHER, SIZE = range(6)
                for p_ in range(EXTRA + 1):
                    dst = further(SIZE, p_) if p_ else firsts(SIZE)
                    v.do(dve.tensor_scalar(dst, CNT[0:1, :], float(-CAP * p_), None, ALU.add))
                for p_ in range(1, EXTRA + 1):
                    v.do(dve.tensor_scalar(further(ACTIVE, p_), CNT[0:1, :], CAP * p_ + 0.5, None, ALU.is_ge))
                    v.do(dve.tensor_copy(further(EXPERT, p_), IOT[0:1, :]))
                    v.do(dve.tensor_scalar(further(ROW, p_), BASE[0:1, :], float(CAP * p_), None, ALU.add))
                v.do(dve.memset(firsts(ACTIVE), 1.0))
                v.do(dve.tensor_copy(firsts(EXPERT), IOT[0:1, :]))
                v.do(dve.tensor_copy(firsts(ROW), BASE[0:1, :]))
                v.sync()
                assert len(SIZES) == 3
                v.do(dve.tensor_scalar(lrow(OTHER), lrow(SIZE), SIZES[0] + 0.5, None, ALU.is_ge))
                v.do(dve.tensor_scalar(lrow(PLACE), lrow(SIZE), SIZES[1] + 0.5, None, ALU.is_ge))
                v.sync()
                v.do(dve.tensor_tensor(lrow(SIZE), lrow(OTHER), lrow(PLACE), ALU.add))
                v.sync()
                v.do(dve.tensor_copy(lrow(PLACE), lrow(ACTIVE)))
                v.sync()
                step_, a, b = 1, PLACE, OTHER
                while step_ < NJ:
                    v.do(dve.tensor_copy(LROW[0:1, b, 0:step_], LROW[0:1, a, 0:step_]))
                    v.do(dve.tensor_tensor(LROW[0:1, b, step_:], LROW[0:1, a, step_:], LROW[0:1, a, 0:NJ - step_], ALU.add))
                    v.sync()
                    a, b, step_ = b, a, step_ * 2
                v.do(dve.tensor_copy(LOUT[0:1, 3, 0:1], LROW[0:1, a, NJ - 1:NJ]))
                v.do(dve.tensor_tensor(lrow(b), lrow(a), lrow(ACTIVE), ALU.subtract))
                v.sync()
                wide = lambda ap: ap.unsqueeze(1).to_broadcast([1, SLOTS, NJ])
                for r, out in ((EXPERT, 0), (ROW, 1), (SIZE, 2)):
                    v.do(dve.tensor_tensor(LSEL[:], wide(lrow(b)), SLI[:].unsqueeze(2).to_broadcast([1, SLOTS, NJ]), ALU.is_equal))
                    v.sync()
                    for r2 in (ACTIVE, r):
                        v.do(dve.tensor_tensor(LSEL[:], LSEL[:], wide(lrow(r2)), ALU.mult))
                        v.sync()
                    v.do(dve.tensor_reduce(LOUT[0:1, out, :], LSEL[:], AXX, ALU.add))
                    v.sync()
                v.do(dve.memset(ITEMS[:], 0))
                v.sync()
                v.do(dve.memset(ITEMS[0:1, L_ROW:L_ROW + 1], PAIRS))
                for r, l0 in ((0, L_EXPERT), (1, L_ROW + 1), (2, L_SIZE)):
                    v.do(dve.tensor_copy(ITEMS[0:1, l0:l0 + SLOTS], LOUT[0:1, r, :]))
                v.do(dve.tensor_copy(ITEMS[0:1, L_NUM:L_NUM + 1], LOUT[0:1, 3, 0:1]))
                v.sync()
                dve.sem_inc(S["items_ready"], 1)
                for j in range(NT):
                    n = tokens(j)
                    if j >= 2:
                        dve.wait_ge(S[f"rows_gone{j % 2}"], 32 * (j // 2))
                    for h in range(2):
                        ps = main_ready()
                        v.do(dve.tensor_scalar(YT[j % 2][0:n, h * 512:h * 512 + 512], ps[0:n, :], RTOK[0:n, j:j + 1], None, ALU.mult), q)
                    v.sync()
                    dve.sem_inc(S["rows_ready"], 1)
                n_items = dve.value_load(ITEMS[0:1, L_NUM:L_NUM + 1], min_val=NE, max_val=SLOTS)
                cs = [conv, q, m, req, split, sreq, v.own]
                per = {conv: 2 * len(item_kinds), q: 12 * MOE_GROUPS, m: 14, req: 2 * MOE_GROUPS, split: KC + 2 * MOE_GROUPS,
                       sreq: KC + 2 * MOE_GROUPS, v.own: 1}
                kp_main = kp[0]
                kp[0], kp[1] = 0, item_kinds * 2
                for _ in range(LOOK):
                    convert()
                v.do(dve.memset(EACC[:], 0.0))
                dve.wait_ge(S["rows_gone0"], 32 * ((NT + 1) // 2))
                dve.wait_ge(S["rows_gone1"], 32 * (NT // 2))

                def low(k):
                    dve.wait_ge(S["split_hi"], split.at(split.n + 1))
                    v.do(dve.tensor_tensor(XSL[:, k, :], T[split.n % 2][:, 0:CAP], XSH[:, k, :].bitcast(F32), ALU.subtract), split)

                def prepare(k):
                    ps = misc_ready()
                    v.sync()
                    v.do(dve.tensor_scalar(T[sreq.n % 2][:, 0:CAP], ps[:, 0:CAP], gain(3)[:, k:k + 1], None, ALU.mult), m)
                    v.sync()
                    dve.sem_inc(sreq.next(), 1)
                    if k:
                        low(k - 1)
                    if k == KC - 1:
                        low(k)
                        v.sync()
                        dve.sem_inc(S["xg_used"], 1)

                def item_out(number):
                    dve.wait_ge(S["ys_out"], number * 48)
                    for j, (r0, n) in enumerate(XBLK):
                        for h in range(2):
                            ps = misc_ready()
                            v.do(dve.tensor_copy(YT[j][0:n, h * 512:h * 512 + 512], ps[0:n, :]), m)
                        v.sync()
                        dve.sem_inc(S["ys_full"], 1)

                for k in range(KC):
                    prepare(k)
                with dve.Fori(0, SLOTS) as it:
                    with dve.If(it < n_items):
                        size = dve.value_load(ITEMS[0:1, bass.ds(it + L_SIZE, 1)], min_val=0, max_val=len(SIZES) - 1)
                        st = looped(cs, it, per)

                        def item(rows):
                            kp[0] = LOOK

                            def step(kind, g, between=lambda d: None):
                                if kind == "GU":
                                    for f in range(2):
                                        ps = main_ready()
                                        v.do(dve.tensor_copy(EG[:, f, 0:rows], ps[:, 0:rows]), q)
                                        v.sync()
                                        dve.sem_inc(req.next(), 1)
                                        convert()
                                    for f in range(2):
                                        ps = main_ready()
                                        t = T[sreq.n % 2][:, 0:rows]
                                        if f == 0:
                                            dve.wait_ge(S["act_done"], req.at(req.n))
                                        v.do(dve.tensor_tensor(t, ps[:, 0:rows], EG[:, f, 0:rows], ALU.mult), q)
                                        v.sync()
                                        dve.sem_inc(sreq.next(), 1)
                                        convert()
                                        dve.wait_ge(S["split_hi"], sreq.at(sreq.n))
                                        v.do(dve.tensor_tensor(ELO[g % 2][:, f, 0:rows], t, EHI[g % 2][:, f, 0:rows].bitcast(F32), ALU.subtract), split)
                                        v.sync()
                                else:
                                    convert()
                                    for d in range(KC):
                                        ps = main_ready()
                                        a = EACC[:, d, 0:rows]
                                        v.do(dve.tensor_tensor(a, ps[:, 0:rows], a, ALU.add), q)
                                        between(d)
                                    v.sync()
                                    convert()

                            head, body, tail = ffn_schedule(MOE_GROUPS, MOE_LOOP)
                            for s in head:
                                step(*s)
                            item_out(it)
                            v.do(dve.memset(EACC[:], 0.0))
                            v.sync()
                            cs2 = [conv, q, req, split, sreq]
                            per2 = {conv: 12, q: 24, req: 4, split: 4, sreq: 4}
                            spacer(dve)
                            with dve.Fori(0, MOE_LOOP) as i:
                                st2 = looped(cs2, i, per2)
                                for s in body:
                                    step(*s)
                            leave(cs2, st2, per2, MOE_LOOP)
                            kp[0] += 12 * (MOE_LOOP - 1)
                            step(*tail[0])
                            step(*tail[1], between=prepare)
                            step(*tail[2])

                        sized(dve, size, cs, item)
                        leave_items(cs, st, per, n_items)
                kp[0], kp[1] = kp_main + LOOK, kinds
                item_out(n_items)
                def combine(j):
                    n = tokens(j)
                    y0, y1 = YG[j % 3][0][0:n, :], YG[j % 3][1][0:n, :]
                    dve.wait_ge(S["weighted"], j + 1)
                    v.do(dve.scalar_tensor_tensor(y0, y1, TW[0:n, 1, j:j + 1], y0, ALU.mult, ALU.add))
                    v.sync()
                    dve.sem_inc(S["combined"], 1)

                combine(0)
                for j in range(NT):
                    n = tokens(j)
                    if j + 1 < NT:
                        combine(j + 1)
                    for h in range(2):
                        dve.wait_ge(S["split_hi"], split.at(split.n + 1))
                        spacer(dve)
                        ps = PS[:, 6 + m.n % 2, 0:4 * P].rearrange("p (k t) -> p k t", k=4)[:, :, 0:n]
                        x0 = XLO[:, 4 * h:4 * h + 4, j * P:j * P + n]
                        v.do(dve.tensor_tensor(x0, ps, XHF[:, 4 * h:4 * h + 4, j * P:j * P + n], ALU.subtract), m)
                        sq = SQS[:, j * P:j * P + n]
                        squares = TC[h][:, :, 0:n].rearrange("p k t -> p t k")
                        if h == 0:
                            v.do(dve.tensor_reduce(sq, squares, AXX, ALU.add), split)
                        else:
                            v.do(dve.tensor_reduce(T[2][:, 0:n], squares, AXX, ALU.add), split)
                            v.sync()
                            v.do(dve.tensor_tensor(sq, sq, T[2][:, 0:n], ALU.add))
                            v.sync()
                    dve.sem_inc(S["gather_used"], 1)
                sreq.n += 2 * NT
                dve.sem_inc(S["split_req"], 2 * NT)
                dve.sem_inc(sqc.next(), 1)
            for c in range(2):
                for t0, n in BLOCKS:
                    ps = misc_ready()
                    v.do(dve.tensor_copy(PT[:, c, t0:t0 + n], ps[:, 0:n]), m)
            v.sync()
            dve.sem_inc(S["p_ready"], 1)
            norm()
            for d in range(KC):
                if not (l == 1 and d >= KC - LOOK):
                    convert()
                for j, (t0, n) in enumerate(BLOCKS):
                    ps = main_ready()
                    t = T[req.n % 2][:, 0:n]
                    v.do(dve.tensor_tensor(t, ps[:, 0:n], RSTD[:, t0:t0 + n], ALU.mult), q)
                    v.sync()
                    dve.sem_inc(req.next(), 1)
                    finish_x()
                    ps = main_ready()
                    dve.wait_ge(S["act_done"], req.at(req.n))
                    v.do(dve.tensor_tensor(t, ps[:, 0:n], t, ALU.mult), q)
                    v.sync()
                    x = XNEW[:, d, t0:t0 + n]
                    v.do(dve.tensor_tensor(x, t, XHF[:, d, t0:t0 + n], ALU.add))
                    v.sync()
                    v.do(dve.tensor_tensor(x, x, XLF[:, d, t0:t0 + n], ALU.add))
                    v.sync()
                    split_x(d, j, x, low=False)
            finish_x()
            dve.sem_inc(sqc.next(), 1)
            if l == 0:
                sreq.n += KC
                dve.sem_inc(S["split_req"], KC)
        norm_tokens()
        dve.wait_ge(S["gain_loaded"], 16)
        for j in range(NT):
            n = tokens(j)
            if j >= 2:
                dve.wait_ge(S[f"outputs{j % 2}"], 16 * (j // 2))
            for h in range(2):
                ps = main_ready()
                v.do(dve.scalar_tensor_tensor(YOUT[j % 2][0:n, h * 512:h * 512 + 512], ps[0:n, :], RTOK[0:n, j:j + 1],
                                              FGAIN[0:n, h * 512:h * 512 + 512], ALU.mult, ALU.mult), q)
            v.sync()
            dve.sem_inc(S["y_full"], 1)

    es.close()


_INS = ["x_prompt", "x_sample", "state_conv_a", "state_conv_b", "state_pool", "p_prompt", "p_sample", "norm_mix_g", "w_in",
        "conv_a_w", "conv_b_w", "conv_b_bias", "conv_b_ln_g", "conv_b_ln_b", "pool_w", "pool_scale", "sgu_ln_g", "sgu_ln_b",
        "sgu_w", "sgu_b", "w_branch", "w_out", "norm_ffn_g", "ffn_w_gate", "ffn_w_up", "ffn_w_down", "router_w", "moe_w_gate",
        "moe_w_up", "moe_w_down", "norm_ple_g", "ple_w_gate", "ple_w_proj", "final_norm_g"]
_OUTS = [("y_p", (1, SEQ, D)), ("y_s", (NSEQ, DSEQ, D)),
         ("a_p", (DEPTH, 1, 2, DB)), ("b_p", (DEPTH, 1, 30, DB)), ("c_p", (DEPTH, 1, 15, DB)), ("v_p", (DEPTH, 1, P, DB)),
         ("a_s", (DEPTH, NSEQ, 2, DB)), ("b_s", (DEPTH, NSEQ, 30, DB)), ("c_s", (DEPTH, NSEQ, 15, DB)), ("v_s", (DEPTH, NSEQ, DSEQ, DB))]


def kernel(**inputs):
    import numpy as _np
    import concourse.bacc as _bacc
    from concourse import mybir as _mybir
    from concourse.bass_utils import run_bass_kernel_spmd as _run

    nc = _bacc.Bacc("TRN2", target_bir_lowering=False, num_devices=1)
    arrays, a, o = {}, {}, {}
    for name in _INS:
        x = _np.ascontiguousarray(inputs[name])
        arrays[f"in_{name}"] = x
        a[name] = nc.dram_tensor(f"in_{name}", x.shape, _mybir.dt.from_np(x.dtype), kind="ExternalInput").ap()
    for name, shape in _OUTS:
        o[name] = nc.dram_tensor(f"out_{name}", shape, _mybir.dt.float32, kind="ExternalOutput").ap()
    build(nc, a, o)
    r = _run(nc, [arrays], core_ids=[0])
    return tuple(r.results[0][f"out_{name}"] for name, _ in _OUTS)
```

```python
from contextlib import ExitStack

import concourse.bass as bass
from concourse import mybir

F32 = mybir.dt.float32
F32R = mybir.dt.float32r
I32 = mybir.dt.int32
U32 = mybir.dt.uint32
ALU = mybir.AluOpType
ACT = mybir.ActivationFunctionType
AXX = mybir.AxisListType.X

P = 128
D = 1024
KC = D // P
DEPTH = 2
SEQ = 1024
NSEQ, DSEQ = 8, 8
NTOK = SEQ + NSEQ * DSEQ
NT = -(-NTOK // P)
DB = 256
DFF = 2816
NE = 8
DFE = 3584
EPS = 1e-6
BLOCKS = ((0, 384), (384, 384), (768, 320))
GROUPS = 4
WINDOWS = (2, 4, 8, 16)
POOL_MAX = max(WINDOWS)

OFF_H, OFF_AB, OFF_AC, OFF_CFA, OFF_CFB, OFF_POOL, OFF_U, OFF_V, OFF_GATE = (DB * i for i in range(9))
BR_A, BR_B, BR_C, BR_D = range(4)

CAP = 336
EXTRA = -(-NTOK // CAP) - 1
PAIRS = 2 * NTOK
SLOTS = NE + PAIRS // CAP
FFN_GROUPS = DFF // 256
MOE_GROUPS = DFE // 256
XBLK = ((0, 128), (128, 128), (256, CAP - 256))
SIZES = tuple(range(256, CAP + 1, 8))
LIST = SLOTS + 2
L_EXPERT, L_ROW, L_SIZE, L_NUM = (LIST * i for i in range(4))

RAW, HL, BANKS, LOOK = 2, 4, 6, 3
OUTS = 6
GATHERS = 5


class Count:

    def __init__(self, sem=None):
        self.sem, self.n, self.terms = sem, 0, []

    def next(self):
        self.n += 1
        return self.sem

    def take(self, k=1):
        self.n += k
        return self.at(self.n)

    def at(self, n, mul=1, div=1):
        v = n // div * mul
        for reg, per in self.terms:
            assert per % div == 0
            v = v + reg * (per // div * mul)
        return v

    def before(self, back, mul=1):
        if self.n - back <= 0:
            assert not self.terms, "a wait in a loop against a value that may be zero"
            return None
        return self.at(self.n - back, mul)


def wait(eng, sem, value):
    if value is not None:
        eng.wait_ge(sem, value)


class Engine:

    def __init__(self, eng, own):
        self.eng, self.own, self.last = eng, Count(own), None

    def do(self, ins, sig=None):
        sig = sig or self.own
        ins.then_inc(sig.next(), 1)
        self.last = (sig, sig.n)
        return self.last

    def sync(self, mark=None):
        sig, n = mark or self.last
        self.eng.wait_ge(sig.sem, sig.at(n))


def looped(counts, reg, per):
    for c in counts:
        c.terms.append((reg, per[c]))
    return [c.n for c in counts]


def leave(counts, starts, per, times):
    for c, n0 in zip(counts, starts):
        assert c.n - n0 == per[c], (c.sem, c.n - n0, per[c])
        c.terms.pop()
        c.n = n0 + times * per[c]


def leave_items(counts, starts, per, reg):
    for c, n0 in zip(counts, starts):
        assert c.n - n0 == per[c], (c.sem, c.n - n0, per[c])
        c.terms.pop()
        c.n = n0
        c.terms.append((reg, per[c]))


def sized(eng, size, counts, body):
    starts = [c.n for c in counts]

    def choose(low, high):
        if high - low == 1:
            for c, n0 in zip(counts, starts):
                c.n = n0
            body(SIZES[low])
            return
        middle = (low + high) // 2
        with eng.If(size < middle):
            choose(low, middle)
        with eng.If(size > middle - 1):
            choose(middle, high)

    choose(0, len(SIZES))


def build(nc, A, O):
    es = ExitStack()
    sem = lambda name: es.enter_context(nc.semaphore(name))
    place = [16512]

    def at(name, shape, dt, off):
        return nc.alloc_sbuf_tensor_at(name, list(shape), dt, offset=off)

    def sb(name, shape, dt=F32):
        size = 4
        for s in shape[1:]:
            size *= s
        off = place[0]
        place[0] += -(-size // 32) * 32
        return at(name, shape, dt, off)

    XHI = sb("XHI", [P, KC, NTOK], F32R)
    XLO = sb("XLO", [P, KC, NTOK], F32R)
    WRAW = [sb(f"WRAW{i}", [P, 2048]) for i in range(RAW)]
    WHI_RING = sb("WHI", [P, HL, KC, P], F32R)
    WLO_RING = sb("WLO", [P, HL, KC, P], F32R)
    WHI = [WHI_RING[:, i] for i in range(HL)]
    WLO = [WLO_RING[:, i] for i in range(HL)]
    RSTD = sb("RSTD", [P, NTOK])
    T = [sb(f"T{i}", [P, 384]) for i in range(4)]
    IDF = sb("IDF", [P, P])
    IDR = sb("IDR", [P, P], F32R)
    TRIL = sb("TRIL", [P, P])
    ONES = sb("ONES", [P, P])
    PAR = sb("PAR", [P, 4 * 38 + 7 * KC])
    RTOK = sb("RTOK", [P, NT])
    EPSC = sb("EPSC", [P, 1])
    WIN = sb("WIN", [P, 2])
    WINV = sb("WINV", [P, 2])
    FIXT = sb("FIXT", [P, 2, 16])
    PH = place[0]
    END = nc.sbuf_usable_end
    XHF, XLF = XHI[:].bitcast(F32), XLO[:].bitcast(F32)

    MIXED = at("MIXED", [P, KC, NTOK], F32, PH)
    MLO = at("MLO", [P, KC, NTOK], F32R, PH)
    MHI = at("MHI", [P, KC, NTOK], F32R, PH + 34816)
    o = PH
    sub = {}
    for name, shape in (("V", [P, NT, DB]), ("SWRAW", [P, GROUPS, P]), ("BDRAW", [64, GROUPS, 64]), ("WT", [P, GROUPS, P]),
                        ("BD", [64, GROUPS, 64]), ("BIAS", [P, 2, P]), ("LNG", [P, DB]), ("LNB", [P, DB]),
                        ("ST", [120, 4, DB]), ("PRS", [38, 2, DB]), ("NRS", [7 * KC, P]), ("BNS", [P, NT, 6]), ("MV", [P, NT, 2]),
                        ("VR", [P, NT])):
        size = 4
        for s in shape[1:]:
            size *= s
        sub[name] = at(name, shape, F32, o)
        o += -(-size // 32) * 32
    assert o <= PH + 32768
    V, SWRAW, BDRAW, WT, BD, BIAS, LNG, LNB, ST, PRS, NRS, BNS, MV, VR = sub.values()
    PA, PB, PC = 2, 30, 15
    WA, WB, WC = (p + SEQ + NSEQ * (p + DSEQ) for p in (PA, PB, PC))
    AR1 = PH + 34816
    GLU = at("GLU", [P, 2, WB], F32, AR1)
    SQB = at("SQB", [P, 2, NTOK], F32, AR1)
    up = lambda size: -(-size // 32) * 32
    YB = at("YB", [P, 2, NTOK], F32, AR1 + up(2 * WB * 4))
    AR2 = AR1 + up(2 * WB * 4) + 2 * NTOK * 4
    UB = at("UB", [P, 2, NTOK], F32, AR2)
    ZA = at("ZA", [P, 2, WA], F32, AR2)
    YA = at("YA", [P, 2, NTOK], F32, AR2 + up(2 * WA * 4))
    ZP = at("ZP", [P, 2, WC], F32, AR2)
    YP = at("YP", [P, 2, NTOK], F32, AR2 + up(2 * WC * 4))
    KEEP = at("KEEP", [P, 272], F32, PH + 72896)
    assert AR2 + up(2 * WC * 4) + 2 * NTOK * 4 <= PH + 72896
    XIN = at("XIN", [P, NT, D], F32, PH + 32768)
    SQS = at("SQS", [P, NTOK], F32, PH + 69632)
    PWR = [at(f"PWR{i}", [P, 2, P], F32, PH + 73984 + 1024 * i) for i in range(2)]
    PWL = [at(f"PWL{i}", [P, 2, P], F32R, PH + 73984 + 1024 * i) for i in range(2)]
    PWH = [at(f"PWH{i}", [P, 2, P], F32R, PH + 76032 + 1024 * i) for i in range(2)]
    halves_at = lambda name, low, high: tuple(at(name + x, [P, 2, NTOK], F32R, off) for x, off in (("HI", high), ("LO", low)))
    U_SPLIT = halves_at("U", AR2, AR2 + 2 * NTOK * 4)
    YA_SPLIT = halves_at("YA", AR2 + up(2 * WA * 4), AR2)
    YB_SPLIT = halves_at("YB", AR1 + up(2 * WB * 4), AR1)
    YP_SPLIT = halves_at("YP", AR2 + up(2 * WC * 4), AR2)
    assert AR2 + 4 * NTOK * 4 <= PH + 72896
    OUTST = at("OUTST", [120, DB], F32, PH + 78080)
    PBD = at("PBD", [P, 2, P], F32, PH + 78080 + 1024)
    assert PH + 78080 + 2048 <= END, (PH, END)
    ACC = at("ACC", [P, KC, NTOK], F32, PH)
    HHI = [at(f"HHI{i}", [P, 2, NTOK], F32R, PH + 34816 + 17408 * i) for i in range(2)]
    HLO = [at(f"HLO{i}", [P, 2, NTOK], F32R, PH + 34816 + 17408 * i + 8704) for i in range(2)]
    GS = at("GS", [P, 2, NTOK], F32, PH + 69632)
    XNEW = at("XNEW", [P, KC, NTOK], F32, PH)
    PTOK = at("PTOK", [P, NT, DB], F32, PH + 52224)
    PT = at("PT", [P, 2, NTOK], F32, PH + 34816)
    P_SPLIT = halves_at("PT", PH + 34816, PH + 43520)
    YOUT = [at(f"YOUT{i}", [P, D], F32, PH + 34816 + 4096 * i) for i in range(OUTS)]
    o = [PH]

    def mo(name, shape, dt=F32):
        size = 4
        for s in shape[1:]:
            size *= s
        t = at(name, shape, dt, o[0])
        o[0] += -(-size // 32) * 32
        return t

    XG = mo("XG", [P, 3, D])
    XSH = mo("XSH", [P, KC, CAP], F32R)
    XSL = mo("XSL", [P, KC, CAP], F32R)
    EHI = [mo(f"EHI{i}", [P, 2, CAP], F32R) for i in range(2)]
    ELO = [mo(f"ELO{i}", [P, 2, CAP], F32R) for i in range(2)]
    EG = mo("EG", [P, 2, CAP])
    EACC = mo("EACC", [P, KC, CAP])
    YT = [mo(f"YT{i}", [P, D]) for i in range(2)]
    YT.append(at("YT2", [P, D], F32, PH + 69632))
    RW = mo("RW", [P, KC, NE])
    LG = mo("LG", [P, NT, NE])
    MX = mo("MX", [P, NT, NE])
    IX = mo("IX", [P, NT, NE], U32)
    IXF = mo("IXF", [P, NT, NE])
    OH = [mo(f"OH{i}", [P, NT, NE]) for i in range(2)]
    SS = mo("SS", [P, NT, NE])
    CS = mo("CS", [P, NT, NE])
    TM = mo("TM", [P, NT, NE])
    POSF = mo("POSF", [P, 2, NT])
    POSI = mo("POSI", [P, 2, NT], I32)
    TW = mo("TW", [P, 2, NT])
    IOT = mo("IOT", [P, NE])
    CNT = mo("CNT", [P, NE])
    BASE = at("BASE", [P, NE], F32, PH + 80000)
    ITEMS = mo("ITEMS", [1, 4 * LIST], I32)
    assert o[0] <= PH + 69632, o[0] - PH
    NJ = NE * (EXTRA + 1)
    lo = PH + 73984 + 4096
    LROW = at("LROW", [1, 6, NJ], F32, lo)
    LSEL = at("LSEL", [1, SLOTS, NJ], F32, PH + 73984)
    LOUT = at("LOUT", [1, 4, SLOTS], F32, up(lo + 24 * NJ))
    SLI = at("SLI", [1, SLOTS], F32, lo + up(24 * NJ) + up(16 * SLOTS))
    XF = at("XF", [P, KC, NTOK], F32, PH + 16384)
    LGT = at("LGT", [NE, NTOK], F32, PH + 51200)
    RWH = at("RWH", [P, KC, NE], F32R, PH + 12288 + 1024)
    RWL = at("RWL", [P, KC, NE], F32R, PH + 12288 + 2048)
    TRIS = at("TRIS", [P, P], F32, PH + 12288)
    YG = [[at(f"YG{i}{k}", [P, D], F32, PH + 8192 * i + 4096 * k) for k in range(2)] for i in range(GATHERS)]
    TC = [at(f"TC{i}", [P, 4, P], F32, PH + 8192 * GATHERS + 2048 * i) for i in range(2)]
    assert SLOTS * NJ * 4 <= 4096 and lo + up(24 * NJ) + up(16 * SLOTS) + 4 * SLOTS <= PH + 80000 <= END - 4 * NE

    XS = nc.dram_tensor("sorted_rows", [PAIRS + CAP, D], F32).ap()
    YS = nc.dram_tensor("expert_rows", [PAIRS + CAP, D], F32).ap()

    PS = es.enter_context(nc.psum_tensor("PS", [P, 8, 512], F32))

    S = {n: sem(n) for n in (
        "raw_ready0", "raw_ready1", "folded", "hi_ready", "lo_ready", "pw_ready0", "pw_ready1", "pw_hi", "pw_lo",
        "mm_done", "evicted", "misc_done", "misc_free", "act_req", "act_done", "split_req", "split_hi", "split_done",
        "dve_own", "pool_own", "consts", "x_loaded0", "x_loaded1", "x_loaded2", "weighted", "sums_clear", "logits_ready", "x_whole", "places_ready", "rtok_ready", "squares_added", "par_loaded", "sgu_zeroed", "st_loaded", "sgu_loaded", "pbd_loaded", "diag_ready", "sq_ready", "v_ready", "br_a", "br_b", "br_c", "br_d", "yb_ready", "lnsq_ready", "pooled",
        "stage_full", "stage_out", *(f"outputs{i}" for i in range(OUTS)), "tok_ready", "p_loaded", "p_ready", "rows_ready", "rows_gone0", "rows_gone1", "rows_gone2", "tri_ready",
        "counts_ready", "items_ready", "scattered", "xg_ready", "xg_used", "ys_full", "ys_out", *(f"gathered{i}" for i in range(GATHERS)), "gather_used", "combined",
        "xnew_ready", "y_full", "v_out", "par_ready", "rw_loaded", "phase_clear", "spacer")}

    mix_l = lambda l: [("col", l)] * 4 + [("col", l)] * 4 + [("col", l)] * 3 + [("col", l)] * 4 + [("col", l)] * 1 + [("col", l)] * 8
    ffn_l = [("col", 2)] * 2 + [("col", 2), ("col", 2), ("row", None)] * (FFN_GROUPS - 1) + [("row", None)]
    kinds = mix_l(0) + [("col", None)] * 4 + ffn_l + [("col", 4)] * 4 + mix_l(1) + [("col", None)] * 4 + [("col", 5)] * 4
    item_kinds = [("col", None)] * 2 + [("col", None), ("col", None), ("row", None)] * (MOE_GROUPS - 1) + [("row", None)]
    T_MOE = 24 + 4 + len(ffn_l) + 4 + 24 + 4
    gain = lambda norm: PAR[:, 152 + norm * KC:152 + (norm + 1) * KC]
    par = lambda l, c, r: PAR[:, (l * 2 + c) * 38 + r:(l * 2 + c) * 38 + r + 1]
    R_CB, R_CA, R_BIAS, R_LG, R_LB, R_PS = 0, 31, 34, 35, 36, 37

    def raw_view(t, half, kind):
        if kind == "col":
            return WRAW[t][:].rearrange("p (k n) -> p k n", k=KC)[:, :, half * P:(half + 1) * P]
        return WRAW[t][:, half * 1024:(half + 1) * 1024].rearrange("p (k n) -> p k n", k=KC)

    def pieces(j, buf, pad):
        t0, n = BLOCKS[j]
        out = []
        if t0 < SEQ:
            m = min(n, SEQ - t0)
            out.append((0, m, buf[:, pad + t0:pad + t0 + m]))
        if t0 + n > SEQ:
            s = buf[:, pad + SEQ:].rearrange("p (s t) -> p s t", s=NSEQ)[:, :, pad:]
            out.append((SEQ - t0, n - (SEQ - t0), s))
        return out

    def shaped(ap, like):
        return ap.rearrange("p (s t) -> p s t", s=NSEQ) if len(like.shape) == 3 else ap

    def tokens(j):
        return min(P, NTOK - j * P)

    def groups(n):
        yield ("GU", 0)
        for g in range(1, n):
            yield ("GU", g)
            yield ("DN", g - 1)
        yield ("DN", n - 1)

    FFN_LOOP, MOE_LOOP = (FFN_GROUPS - 3) // 2, (MOE_GROUPS - 2) // 2
    assert FFN_GROUPS % 2 == 1 and MOE_GROUPS % 2 == 0
    Q_FFN = 3 * KC + 6 + 12 + 48 + 18 + 48 + 6 + 48 + 48 + 24
    Q_LAST_DOWN = Q_FFN + 12 + 36 * (FFN_GROUPS - 1)
    W_FFN = 3 * KC + KC + 3 * KC
    W_LAST_DOWN = W_FFN + 6 * FFN_GROUPS
    W_MIX1 = W_FFN + 6 * FFN_GROUPS + 3 * KC + 3 * KC
    MERGE_EARLY = (AR2 - (PH + 34816)) // (NTOK * 4)
    W_MOE = W_MIX1 + KC + KC + 3 * KC

    def ffn_schedule(n, loops):
        steps = list(groups(n))
        return steps[:1], steps[1:5], steps[1 + 4 * loops:]

    def spacer(eng):
        eng.sem_inc(S["spacer"], 1)

    def load_p(q, l):
        for j in range(NT):
            n = tokens(j)
            src = A["p_prompt"][l, 0, j * P:(j + 1) * P, :] if j < NT - 1 else A["p_sample"][l].rearrange("s t d -> (s t) d")
            q.dma_start(PTOK[0:n, j, :], src).then_inc(S["p_loaded"], 16)

    block = es.enter_context(nc.Block())

    @block.sync
    def _(sp):
        tile = Count()
        def load(src):
            if tile.n >= RAW:
                sp.wait_ge(S["lo_ready"], lo_value(tile))
            s = tile.n % RAW
            k = src.shape[1]
            sp.dma_start(WRAW[s][:].rearrange("p (k n) -> p k n", k=k), src).then_inc(S[f"raw_ready{s}"], 16)
            tile.n += 1

        def lo_value(t):
            v = t.n * 2 - 2 * RAW + 2
            for reg, per in t.terms:
                v = v + reg * (2 * per)
            return v

        def cols(w, c0, n=DB):
            return w.rearrange("(k p) n -> p k n", p=P)[:, :, bass.ds(c0, n)]

        def load_x(block):
            t0, m = BLOCKS[block]
            for j in range(t0 // P, -(-(t0 + m) // P)):
                n = tokens(j)
                src = A["x_prompt"][0, j * P:(j + 1) * P, :] if j < NT - 1 else A["x_sample"].rearrange("s t d -> (s t) d")
                sp.dma_start(XIN[0:n, j, :], src).then_inc(S[f"x_loaded{block}"], 16)

        load_x(0)
        load_x(1)
        for l in range(DEPTH):
            w_in = A["w_in"][l]

            def gate_project(br):
                for j in range(4):
                    load(cols(w_in, OFF_GATE + br * D + j * DB))

            load(cols(w_in, OFF_U))
            if l == 0:
                load_x(2)
            load(cols(w_in, OFF_V))
            load(cols(w_in, OFF_CFB))
            load(cols(w_in, OFF_CFA))
            gate_project(BR_D)
            for off in (OFF_AC, OFF_H, OFF_AB):
                load(cols(w_in, off))
            gate_project(BR_A)
            load(cols(w_in, OFF_POOL))
            gate_project(BR_B)
            gate_project(BR_C)
            for j in range(4):
                load(cols(A["w_out"][l], j * DB))
            if l == 0:
                wg, wu, wd = (A[n][0] for n in ("ffn_w_gate", "ffn_w_up", "ffn_w_down"))
                wdr = wd.rearrange("(f p) n -> p f n", p=P)

                def step(kind, g, i=0):
                    if kind == "GU":
                        load(cols(wg, i * 512 + g * DB))
                        load(cols(wu, i * 512 + g * DB))
                    else:
                        load(wdr[:, bass.ds(i * 4 + g * 2, 2), :])

                head, body, tail = ffn_schedule(FFN_GROUPS, FFN_LOOP)
                for s in head:
                    step(*s)
                with sp.Fori(0, FFN_LOOP) as i:
                    st = looped([tile], i, {tile: 6})
                    for s in body:
                        step(*s, i)
                leave([tile], st, {tile: 6}, FFN_LOOP)
                for s in tail:
                    step(*s)
            else:
                sp.wait_ge(S["items_ready"], 1)
                n_items = sp.value_load(ITEMS[0:1, L_NUM:L_NUM + 1], min_val=NE, max_val=SLOTS)
                wg = A["moe_w_gate"][0].rearrange("e (k p) n -> p (e k) n", p=P)
                wu = A["moe_w_up"][0].rearrange("e (k p) n -> p (e k) n", p=P)
                wd = A["moe_w_down"][0].rearrange("e (f p) n -> p (e f) n", p=P)
                NF = DFE // P
                with sp.Fori(0, SLOTS) as it:
                    with sp.If(it < n_items):
                        e = sp.value_load(ITEMS[0:1, bass.ds(it, 1)], min_val=0, max_val=NE - 1)
                        st = looped([tile], it, {tile: len(item_kinds)})

                        def step(kind, g, i=0):
                            if kind == "GU":
                                load(wg[:, bass.ds(e * KC, KC), bass.ds(i * 512 + g * DB, DB)])
                                load(wu[:, bass.ds(e * KC, KC), bass.ds(i * 512 + g * DB, DB)])
                            else:
                                load(wd[:, bass.ds(e * NF + i * 4 + g * 2, 2), :])

                        head, body, tail = ffn_schedule(MOE_GROUPS, MOE_LOOP)
                        for s in head:
                            step(*s)
                        with sp.Fori(0, MOE_LOOP) as i:
                            st2 = looped([tile], i, {tile: 6})
                            for s in body:
                                step(*s, i)
                        leave([tile], st2, {tile: 6}, MOE_LOOP)
                        for s in tail:
                            step(*s)
                        leave_items([tile], st, {tile: len(item_kinds)}, n_items)
            for j in range(4):
                load(cols(A["ple_w_gate"][l], j * DB))
                if j == 1:
                    if l == 0:
                        sp.wait_ge(S["evicted"], Q_LAST_DOWN)
                    else:
                        sp.wait_ge(S["ys_out"], n_items * 48 + 48)
                        spacer(sp)
                    load_p(sp, l)

    @block.gpsimd
    def _(g):
        pool = Engine(g, S["pool_own"])
        tile = Count()
        kp = [0]

        g.memset(IDF[:], 0.0).then_inc(S["pool_own"], 1)
        g.memset(TRIL[:], 1.0).then_inc(S["pool_own"], 1)
        g.wait_ge(S["pool_own"], 2)
        g.affine_select(out=IDF[:], in_=IDF[:], compare_op=ALU.not_equal, fill=1.0, base=0, pattern=[[-1, P]],
                        channel_multiplier=1).then_inc(S["consts"], 1)
        g.affine_select(out=TRIL[:], in_=TRIL[:], compare_op=ALU.is_ge, fill=0.0, base=0, pattern=[[1, P]],
                        channel_multiplier=-1).then_inc(S["consts"], 1)
        g.iota(FIXT[:], pattern=[[0, 2], [1, 16]], base=1, channel_multiplier=0,
               allow_small_or_imprecise_dtypes=True).then_inc(S["consts"], 1)

        for j in range(7):
            src = (A["norm_mix_g"][j % 2] if j < 2 else A["norm_ffn_g"][j % 2] if j < 4 else A["norm_ple_g"][j % 2] if j < 6
                   else A["final_norm_g"])
            g.dma_start(NRS[j * KC:(j + 1) * KC, :], src.rearrange("(k p) -> k p", p=P)).then_inc(S["par_loaded"], 16)
        for l in range(DEPTH):
            for r, n, src in ((R_CB, 31, A["conv_b_w"][l]), (R_CA, 3, A["conv_a_w"][l]), (R_BIAS, 1, A["conv_b_bias"][l:l + 1]),
                              (R_LG, 1, A["conv_b_ln_g"][l:l + 1]), (R_LB, 1, A["conv_b_ln_b"][l:l + 1]), (R_PS, 1, A["pool_scale"][l:l + 1])):
                g.dma_start(PRS[r:r + n, l, :], src).then_inc(S["par_loaded"], 16)

        def layer_params(l):
            g.wait_ge(S["sgu_zeroed"], l + 1)
            g.dma_start(SWRAW[:], A["sgu_w"][l].rearrange("g t s -> t g s")).then_inc(S["sgu_loaded"], 16)
            for b in range(NSEQ):
                g.dma_start(BDRAW[8 * b:8 * b + 8, :, 8 * b:8 * b + 8], A["sgu_w"][l][:, 0:8, 0:8].rearrange("g t s -> t g s")
                            ).then_inc(S["sgu_loaded"], 16)
            for q in range(GROUPS):
                g.dma_start(BIAS[64 * (q % 2):64 * (q % 2) + 64, q // 2, :], A["sgu_b"][l, q, :].partition_broadcast(64)
                            ).then_inc(S["sgu_loaded"], 16)
                g.dma_start(PBD[64 * (q % 2):64 * (q % 2) + 64, q // 2, 64 * (q % 2):64 * (q % 2) + 64], A["pool_w"][l, q]
                            ).then_inc(S["pbd_loaded"], 16)
            g.dma_start(LNG[:], A["sgu_ln_g"][l].partition_broadcast(P)).then_inc(S["sgu_loaded"], 16)
            g.dma_start(LNB[:], A["sgu_ln_b"][l].partition_broadcast(P)).then_inc(S["sgu_loaded"], 16)
            sb_ = A["state_conv_b"][l].rearrange("(h s) r c -> h (s r) c", h=2)
            for h in range(2):
                g.dma_start(ST[:, h, :], sb_[h]).then_inc(S["st_loaded"], 16)
            g.dma_start(ST[:, 2, :], A["state_pool"][l].rearrange("s r c -> (s r) c")).then_inc(S["st_loaded"], 16)
            g.dma_start(ST[0:16, 3, :], A["state_conv_a"][l].rearrange("s r c -> (s r) c")).then_inc(S["st_loaded"], 16)

        def fold():
            kind, norm = kinds[kp[0]]
            kp[0] += 1
            if norm is not None:
                s = tile.n % RAW
                g.wait_ge(S["par_ready"], 1)
                g.wait_ge(S[f"raw_ready{s}"], tile.at(tile.n, 16, 2) + 16)
                w = WRAW[s][:].rearrange("p (k n) -> p k n", k=KC)
                g.tensor_tensor(w, w, gain(norm).unsqueeze(2).to_broadcast([P, KC, DB]), ALU.mult).then_inc(S["folded"], 1)
            tile.n += 1

        fold(), fold()
        layer_params(0)
        for _ in range(24 + 4 - 2):
            fold()
        fold(), fold()
        with g.Fori(0, FFN_LOOP) as i:
            st = looped([tile], i, {tile: 6})
            for _ in range(6):
                fold()
        leave([tile], st, {tile: 6}, FFN_LOOP)
        kp[0] = tile.n
        while tile.n < 24 + 4 + len(ffn_l):
            fold()
        fold(), fold()
        for d in range(KC):
            for j, (t0, n) in enumerate(BLOCKS):
                w = W_LAST_DOWN + 3 * d + j
                g.wait_ge(S["split_hi"], w + 1)
                square, total = T[2 + w % 2][:, 0:n], SQS[:, t0:t0 + n]
                if d:
                    if j == 0:
                        g.wait_ge(S["squares_added"], 3 * d)
                    g.tensor_tensor(total, total, square, ALU.add).then_inc(S["squares_added"], 1)
                else:
                    g.tensor_copy(total, square).then_inc(S["squares_added"], 1)
        for _ in range(2):
            fold()
        fold(), fold()
        layer_params(1)
        for _ in range(24 + 4 - 2):
            fold()

        g.wait_ge(S["phase_clear"], 1)
        g.dma_start(RW[:], A["router_w"][0].rearrange("(k p) e -> p k e", p=P)).then_inc(S["rw_loaded"], 16)
        g.iota(SLI[:], pattern=[[1, SLOTS]], base=0, channel_multiplier=0, allow_small_or_imprecise_dtypes=True).then_inc(S["consts"], 1)
        g.iota(IOT[:], pattern=[[1, NE]], base=0, channel_multiplier=0, allow_small_or_imprecise_dtypes=True).then_inc(S["consts"], 1)
        for j, (r0, n) in enumerate(XBLK):
            g.dma_start(XS[PAIRS + r0:PAIRS + r0 + n, :], XG[0:n, j, :]).then_inc(S["scattered"], 16)
        for j in range(NT):
            n = tokens(j)
            if j == 0:
                g.wait_ge(S["places_ready"], 1)
            g.wait_ge(S["rows_ready"], j + 1)
            for k in range(2):
                g.indirect_dma_start(XS[0:PAIRS, :], bass.IndirectOffsetOnAxis(ap=POSI[0:n, k, j:j + 1], axis=0), YT[j % 3][0:n, :],
                                     None).then_inc(S[f"rows_gone{j % 3}"], 16)
        assert NT % 3 == 0
        for i in range(3):
            g.wait_ge(S[f"rows_gone{i}"], 32 * (NT // 3))
        g.wait_ge(S["scattered"], 48)
        g.wait_ge(S["items_ready"], 1)
        n_items = g.value_load(ITEMS[0:1, L_NUM:L_NUM + 1], min_val=NE, max_val=SLOTS)
        row = g.value_load(ITEMS[0:1, L_ROW + 1:L_ROW + 2], min_val=0, max_val=PAIRS)
        for j, (r0, n) in enumerate(XBLK):
            g.dma_start(XG[0:n, j, :], XS[bass.ds(row + r0, n), :]).then_inc(S["xg_ready"], 16)
        with g.Fori(0, SLOTS) as it:
            with g.If(it < n_items):
                g.wait_ge(S["ys_full"], it * 3 + 3)
                spacer(g)
                g.memset(EACC[:], 0.0).then_inc(S["sums_clear"], 1)
                row = g.value_load(ITEMS[0:1, bass.ds(it + L_ROW + 2, 1)], min_val=0, max_val=PAIRS)
                g.wait_ge(S["xg_used"], it + 1)
                spacer(g)
                for j, (r0, n) in enumerate(XBLK):
                    g.dma_start(XG[0:n, j, :], XS[bass.ds(row + r0, n), :]).then_inc(S["xg_ready"], 16)
        tile.terms.append((n_items, len(item_kinds)))
        fold(), fold()
        g.wait_ge(S["ys_out"], n_items * 48 + 48)
        spacer(g)
        for j in range(NT):
            n = tokens(j)
            if j >= GATHERS:
                g.wait_ge(S["gather_used"], j - GATHERS + 1)
            for k in range(2):
                g.indirect_dma_start(YG[j % GATHERS][k][0:n, :], None, YS[0:PAIRS, :],
                                     bass.IndirectOffsetOnAxis(ap=POSI[0:n, k, j:j + 1], axis=0)).then_inc(S[f"gathered{j % GATHERS}"], 16)
        for _ in range(2):
            fold()

    @block.tensor
    def _(pe):
        unit, q, m, pw = Count(), Count(S["mm_done"]), Count(S["misc_done"]), Count()
        split = Count()

        def use(n=1):
            pe.wait_ge(S["lo_ready"], unit.at(unit.n + n))

        def open_bank():
            wait(pe, S["evicted"], q.before(BANKS - 1))
            return q.n % BANKS

        def misc_bank():
            wait(pe, S["misc_free"], m.before(1))
            if m.terms:
                spacer(pe)
            return 6 + m.n % 2

        def product(bank, n, slot, hi, lo, splits=None):
            for k in range(KC):
                if splits is not None:
                    pe.wait_ge(S["split_done"], splits + k + 1)
                wh, wl = WHI[slot][:, k, :], WLO[slot][:, k, :]
                pe.matmul(PS[:, bank, 0:n], wh, hi(k), start=(k == 0), stop=False)
                pe.matmul(PS[:, bank, 0:n], wh, lo(k), start=False, stop=False)
                ins = pe.matmul(PS[:, bank, 0:n], wl, hi(k), start=False, stop=(k == KC - 1))
            return ins

        def column_unit(HI, LO, first_use=None, after_first=lambda: None):
            use()
            slot = unit.n % HL
            for t0, n in BLOCKS:
                b = open_bank()
                product(b, n, slot, lambda k: HI[:, k, t0:t0 + n], lambda k: LO[:, k, t0:t0 + n],
                        first_use if t0 == 0 else None).then_inc(q.next(), 1)
                if t0 == 0:
                    after_first()
            unit.n += 1

        def token_sums(*parts):
            b = misc_bank()
            for j in range(NT):
                n = tokens(j)
                for x, part in enumerate(parts):
                    ins = pe.matmul(PS[0:n, b, j:j + 1], part[:, j * P:j * P + n], ONES[:, 0:1], start=(x == 0), stop=(x == len(parts) - 1))
            ins.then_inc(m.next(), 1)

        def stats():
            pe.wait_ge(S["sq_ready"], sq.take())
            token_sums(SQS)

        def spread():
            pe.wait_ge(S["diag_ready"], diag.take())
            for j, (t0, n) in enumerate(BLOCKS):
                b = misc_bank()
                pe.matmul(PS[:, b, 0:n], ONES[:], T[j][:, 0:n], start=True, stop=True).then_inc(m.next(), 1)

        sq, diag = Count(), Count()

        def gate_project(ready, count, Y, after_first=lambda: None):
            pe_ready = [False]
            for j in range(4):
                for h in range(2):
                    use()
                    slot = unit.n % HL
                    for t0, n in BLOCKS:
                        b = open_bank()
                        product(b, n, slot, lambda k: XHI[:, k, t0:t0 + n], lambda k: XLO[:, k, t0:t0 + n]).then_inc(q.next(), 1)
                        if not pe_ready[0]:
                            after_first()
                            pe.wait_ge(S[ready], count)
                            pe_ready[0] = True
                        if t0 == 0:
                            pe.wait_ge(S["pw_lo"], pw.n + 1)
                        b = open_bank()
                        wh, wl = PWH[pw.n % 2], PWL[pw.n % 2]
                        for k in range(2):
                            pe.matmul(PS[:, b, 0:n], wh[:, k, :], Y[0][:, k, t0:t0 + n], start=(k == 0), stop=False)
                            pe.matmul(PS[:, b, 0:n], wh[:, k, :], Y[1][:, k, t0:t0 + n], start=False, stop=False)
                            ins = pe.matmul(PS[:, b, 0:n], wl[:, k, :], Y[0][:, k, t0:t0 + n], start=False, stop=(k == 1))
                        ins.then_inc(q.next(), 1)
                    unit.n += 1
                    pw.n += 1

        def states_in():
            pe.wait_ge(S["st_loaded"], 64 * (l + 1))
            b = misc_bank()
            for c in range(2):
                for h in range(2):
                    x = (c * 2 + h) * 120
                    ins = pe.transpose(PS[:, b, x:x + 120], ST[:, h, c * P:(c + 1) * P], IDF[0:120, 0:120])
            ins.then_inc(m.next(), 1)
            b = misc_bank()
            for c in range(2):
                pe.transpose(PS[:, b, c * 120:c * 120 + 120], ST[:, 2, c * P:(c + 1) * P], IDF[0:120, 0:120])
                ins = pe.transpose(PS[:, b, 240 + c * 16:256 + c * 16], ST[0:16, 3, c * P:(c + 1) * P], IDF[0:16, 0:16])
            ins.then_inc(m.next(), 1)

        so = Count()

        def states_out(buf, tmp, pad):
            rows = NSEQ * pad
            lots = -(-rows // 120)
            pe.wait_ge(S["tok_ready"], so.take())
            for h in range(lots):
                n = rows // lots
                b = misc_bank()
                for c in range(2):
                    ins = pe.transpose(PS[0:n, b, c * P:(c + 1) * P], tmp[:, c, h * n:(h + 1) * n], IDF[:])
                ins.then_inc(m.next(), 1)
            b = misc_bank()
            for c in range(2):
                ins = pe.transpose(PS[0:pad, b, c * P:(c + 1) * P], buf[:, c, SEQ:SEQ + pad], IDF[:])
            ins.then_inc(m.next(), 1)

        def down(hi, lo, blocks, after=lambda d: None):
            use(2)
            s0, s1 = unit.n % HL, (unit.n + 1) % HL
            for d in range(KC):
                for t0, n in blocks:
                    b = open_bank()
                    for f, s in enumerate((s0, s1)):
                        pe.matmul(PS[:, b, 0:n], WHI[s][:, d, :], hi[:, f, t0:t0 + n], start=(f == 0), stop=False)
                        pe.matmul(PS[:, b, 0:n], WHI[s][:, d, :], lo[:, f, t0:t0 + n], start=False, stop=False)
                        ins = pe.matmul(PS[:, b, 0:n], WLO[s][:, d, :], hi[:, f, t0:t0 + n], start=False, stop=(f == 1))
                    ins.then_inc(q.next(), 1)
                after(d)
            unit.n += 2

        pe.wait_ge(S["consts"], 3)
        for block, (t0, n) in enumerate(BLOCKS):
            tiles = range(t0 // P, -(-(t0 + n) // P))
            pe.wait_ge(S[f"x_loaded{block}"], 16 * len(tiles))
            for c in range(KC):
                b = open_bank()
                for j in tiles:
                    w = tokens(j)
                    ins = pe.transpose(PS[:, b, j * P - t0:j * P - t0 + w], XIN[0:w, j, c * P:(c + 1) * P], IDF[0:w, 0:w])
                ins.then_inc(q.next(), 1)
            if block == 1:
                pe.wait_ge(S["par_loaded"], 16 * (7 + 12))
                b = misc_bank()
                for l in range(DEPTH):
                    for c in range(2):
                        pe.transpose(PS[:, b, (l * 2 + c) * 38:(l * 2 + c) * 38 + 38], PRS[:, l, c * P:(c + 1) * P], IDF[0:38, 0:38])
                pe.transpose(PS[:, b, 152:152 + 7 * KC], NRS[:], IDF[0:7 * KC, 0:7 * KC]).then_inc(m.next(), 1)

        for l in range(DEPTH):
            stats()
            column_unit(XHI, XLO, first_use=(W_MIX1 if l else None))
            spread()
            column_unit(XHI, XLO)
            use(2)
            for j in range(NT):
                n = tokens(j)
                b = misc_bank()
                pair = slice(unit.n % HL, unit.n % HL + 2)
                dst = PS[0:n, b, 0:DB].rearrange("p (h c) -> p h c", h=2)
                for k in range(KC):
                    xh, xl = XHI[:, k, j * P:j * P + n], XLO[:, k, j * P:j * P + n]
                    pe.matmul(dst, xh, WHI_RING[:, pair, k, :], start=(k == 0), stop=False)
                    pe.matmul(dst, xl, WHI_RING[:, pair, k, :], start=False, stop=False)
                    ins = pe.matmul(dst, xh, WLO_RING[:, pair, k, :], start=False, stop=(k == KC - 1))
                ins.then_inc(m.next(), 1)
            unit.n += 2
            pe.wait_ge(S["sgu_loaded"], 16 * (1 + NSEQ + GROUPS + 2) * (l + 1))
            b = misc_bank()
            for q4 in range(GROUPS):
                ins = pe.transpose(PS[:, b, q4 * P:(q4 + 1) * P], SWRAW[:, q4, :], IDF[:])
            ins.then_inc(m.next(), 1)
            b = misc_bank()
            for q4 in range(GROUPS):
                ins = pe.transpose(PS[0:64, b, q4 * 64:(q4 + 1) * 64], BDRAW[:, q4, :], IDF[0:64, 0:64])
            ins.then_inc(m.next(), 1)
            states_in()
            for _ in range(3):
                column_unit(XHI, XLO)
            pe.wait_ge(S["v_ready"], l + 1)
            for c in range(2):
                for jj in range(2):
                    b = misc_bank()
                    for j in range(4 * jj, 4 * jj + 4):
                        for h in range(2):
                            g4 = 2 * c + h
                            ins = pe.matmul(PS[64 * h:64 * h + 64, b, (j % 4) * P:(j % 4 + 1) * P], V[:, j, g4 * 64:g4 * 64 + 64], WT[:, g4, :],
                                            start=True, stop=True)
                    ins.then_inc(m.next(), 1)
            b = misc_bank()
            for c in range(2):
                for h in range(2):
                    g4 = 2 * c + h
                    ins = pe.matmul(PS[64 * h:64 * h + 64, b, c * 64:c * 64 + 64], V[0:64, NT - 1, g4 * 64:g4 * 64 + 64], BD[:, g4, :],
                                    start=True, stop=True)
            ins.then_inc(m.next(), 1)
            column_unit(XHI, XLO)
            states_out(GLU, YB, PB)
            gate_project("br_d", l + 1, U_SPLIT)
            for _ in range(4):
                column_unit(XHI, XLO)
            states_out(ZA, YA, PA)
            column_unit(XHI, XLO)
            column_unit(XHI, XLO)
            gate_project("br_a", l + 1, YA_SPLIT)
            pe.wait_ge(S["yb_ready"], l + 1)
            for t0, n in BLOCKS:
                b = misc_bank()
                for k in range(2):
                    ins = pe.matmul(PS[:, b, 0:n], ONES[:], YB[:, k, t0:t0 + n], start=(k == 0), stop=(k == 1))
                ins.then_inc(m.next(), 1)
            column_unit(XHI, XLO)
            pe.wait_ge(S["lnsq_ready"], l + 1)
            token_sums(SQB[:, 0, :], SQB[:, 1, :])
            column_unit(XHI, XLO, after_first=spread)
            states_out(ZP, YP, PC)
            gate_project("br_b", l + 1, YB_SPLIT)
            pe.wait_ge(S["pooled"], l + 1)
            pe.wait_ge(S["pbd_loaded"], 64 * (l + 1))
            for c in range(2):
                for t0, n in BLOCKS:
                    b = misc_bank()
                    pe.matmul(PS[:, b, 0:n], PBD[:, c, :], YP[:, c, t0:t0 + n], start=True, stop=True).then_inc(m.next(), 1)
            gate_project("br_c", l + 1, YP_SPLIT)
            for d in range(KC):
                column_unit(MHI, MLO, first_use=(W_FFN if l == 0 else W_MOE) - 3 * KC - KC if d == 0 else None)
            stats()
            if l == 0:
                hs = Count()

                def step(kind, g, first=False):
                    if kind == "GU":
                        for u in range(4):
                            column_unit(XHI, XLO)
                            if first and u == 0:
                                spread()
                    else:
                        pe.wait_ge(S["split_done"], hs.take(2 * 3))
                        down(HHI[g % 2], HLO[g % 2], BLOCKS)

                hs.n = W_FFN
                head, body, tail = ffn_schedule(FFN_GROUPS, FFN_LOOP)
                for s in head:
                    step(*s, first=True)
                with pe.Fori(0, FFN_LOOP) as i:
                    cs = [unit, q, hs]
                    per = {unit: 12, q: 2 * (12 + 24), hs: 12}
                    st = looped(cs, i, per)
                    for s in body:
                        step(*s)
                leave(cs, st, per, FFN_LOOP)
                for s in tail:
                    step(*s)
            else:
                pe.wait_ge(S["tri_ready"], 1)
                for t0, n in BLOCKS:
                    b = misc_bank()
                    for k in range(KC):
                        xh, xl, dst = XHI[:, k, t0:t0 + n], XLO[:, k, t0:t0 + n], PS[0:NE, b, 0:n]
                        pe.matmul(dst, RWH[:, k, :], xh, start=(k == 0), stop=False)
                        pe.matmul(dst, RWH[:, k, :], xl, start=False, stop=False)
                        ins = pe.matmul(dst, RWL[:, k, :], xh, start=False, stop=(k == KC - 1))
                    ins.then_inc(m.next(), 1)
                pe.wait_ge(S["logits_ready"], 1)
                b = misc_bank()
                for j in range(NT):
                    n = tokens(j)
                    ins = pe.transpose(PS[0:n, b, j * NE:(j + 1) * NE], LGT[:, j * P:j * P + n], IDF[0:NE, 0:NE])
                ins.then_inc(m.next(), 1)

                def rows(j):
                    n = tokens(j)
                    for h in range(2):
                        b = open_bank()
                        for k in range(4):
                            ins = pe.transpose(PS[0:n, b, k * P:(k + 1) * P], XF[:, 4 * h + k, j * P:j * P + n], IDF[:])
                        ins.then_inc(q.next(), 1)

                pe.wait_ge(S["x_whole"], 1)
                for j in range(2):
                    rows(j)
                pe.wait_ge(S["counts_ready"], 1)
                b = misc_bank()
                flat = lambda t: t[:].rearrange("p j e -> p (j e)")
                pe.matmul(PS[:, b, 0:NT * NE], TRIS[:], flat(SS), start=True, stop=False)
                pe.matmul(PS[:, b, 0:NT * NE], ONES[:], flat(CS), start=False, stop=True)
                pe.matmul(PS[:, b, NT * NE:(NT + 1) * NE], ONES[:], TM[:, 0, :], start=True, stop=True).then_inc(m.next(), 1)
                for j in range(2, NT):
                    rows(j)
                pe.wait_ge(S["items_ready"], 1)
                n_items = pe.value_load(ITEMS[0:1, L_NUM:L_NUM + 1], min_val=NE, max_val=SLOTS)
                hs = Count()
                hs.n = W_MOE
                q_item = None
                cs = [unit, q, m, hs]
                per = {unit: 2 * len(item_kinds), q: MOE_GROUPS * 12, m: 14, hs: KC + 2 * MOE_GROUPS}

                def prepare(k):
                    b = misc_bank()
                    for j, (r0, n) in enumerate(XBLK):
                        ins = pe.transpose(PS[:, b, r0:r0 + n], XG[0:n, j, k * P:(k + 1) * P], IDF[0:n, 0:n])
                    ins.then_inc(m.next(), 1)

                def item_out(j):
                    r0, n = XBLK[j]
                    if j == 0:
                        pe.wait_ge(S["evicted"], q_item)
                    for h in range(2):
                        b = misc_bank()
                        for k in range(4):
                            ins = pe.transpose(PS[0:n, b, k * P:(k + 1) * P], EACC[:, 4 * h + k, r0:r0 + n], IDF[:])
                        ins.then_inc(m.next(), 1)

                pe.wait_ge(S["xg_ready"], 48)
                for k in range(KC):
                    prepare(k)
                with pe.Fori(0, SLOTS) as it:
                    with pe.If(it < n_items):
                        size = pe.value_load(ITEMS[0:1, bass.ds(it + L_SIZE, 1)], min_val=0, max_val=len(SIZES) - 1)
                        st = looped(cs, it, per)

                        def item(rows):
                            nonlocal q_item

                            def step(kind, g, after=lambda d: None):
                                if kind == "GU":
                                    for u in range(4):
                                        use()
                                        b = open_bank()
                                        product(b, rows, unit.n % HL, lambda k: XSH[:, k, 0:rows], lambda k: XSL[:, k, 0:rows]).then_inc(q.next(), 1)
                                        unit.n += 1
                                        after(u)
                                else:
                                    pe.wait_ge(S["split_done"], hs.take(2))
                                    down(EHI[g % 2], ELO[g % 2], ((0, rows),), after)

                            q_item = q.at(q.n)
                            pe.wait_ge(S["split_done"], hs.take(KC))
                            head, body, tail = ffn_schedule(MOE_GROUPS, MOE_LOOP)
                            for s in head:
                                step(*s, after=lambda u: item_out(u) if u < len(XBLK) else None)
                            with pe.Fori(0, MOE_LOOP) as i:
                                cs2 = [unit, q, hs]
                                per2 = {unit: 12, q: 24, hs: 4}
                                st2 = looped(cs2, i, per2)
                                for s in body:
                                    step(*s)
                            leave(cs2, st2, per2, MOE_LOOP)
                            step(*tail[0])
                            pe.wait_ge(S["xg_ready"], it * 48 + 96)
                            step(*tail[1], after=prepare)
                            step(*tail[2])

                        sized(pe, size, cs, item)
                        leave_items(cs, st, per, n_items)
                q_item = q.at(q.n)
                for j in range(len(XBLK)):
                    item_out(j)
                for j in range(NT):
                    n = tokens(j)
                    pe.wait_ge(S["combined"], j + 1)
                    for h in range(2):
                        b = misc_bank()
                        dst = PS[:, b, 0:4 * P].rearrange("p (k t) -> p k t", k=4)[:, :, 0:n]
                        pe.matmul(dst, IDR[:], XHI[:, 4 * h:4 * h + 4, j * P:j * P + n], start=True, stop=False)
                        pe.matmul(dst, IDR[:], XLO[:, 4 * h:4 * h + 4, j * P:j * P + n], start=False, stop=False)
                        for k in range(4):
                            c0 = (4 * h + k) * P
                            ins = pe.matmul(PS[:, b, k * P:k * P + n], YG[j % GATHERS][0][0:n, c0:c0 + P], IDF[0:n, 0:n], start=False, stop=(k == 3))
                        ins.then_inc(m.next(), 1)
            pe.wait_ge(S["p_loaded"], 16 * NT * (l + 1))
            for c in range(2):
                for t0, n in BLOCKS:
                    b = misc_bank()
                    for j in range(t0 // P, -(-(t0 + n) // P)):
                        w = tokens(j)
                        ins = pe.transpose(PS[:, b, j * P - t0:j * P - t0 + w], PTOK[0:w, j, c * P:(c + 1) * P], IDF[0:w, 0:w])
                    ins.then_inc(m.next(), 1)
            stats()
            gate_project("p_ready", l + 1, P_SPLIT, after_first=spread)
        stats()
        pe.wait_ge(S["xnew_ready"], 3 * KC)
        for j in range(NT):
            n = tokens(j)
            for h in range(2):
                b = misc_bank() if h else open_bank()
                spacer(pe)
                for k in range(4):
                    ins = pe.transpose(PS[0:n, b, k * P:(k + 1) * P], XNEW[:, 4 * h + k, j * P:j * P + n], IDF[:])
                ins.then_inc((m if h else q).next(), 1)

    @block.scalar
    def _(act):
        halves, q, m = Count(S["hi_ready"]), Count(), Count()
        fold, req, split = Count(), Count(S["act_done"]), Count(S["split_hi"])
        kp = [0, kinds]

        def convert(misc=False):
            kind, norm = kp[1][kp[0] // 2]
            kp[0] += 1
            half, tile = halves.n % 2, halves.n // 2
            if norm is not None:
                if half == 0:
                    fold.n += 1
                act.wait_ge(S["folded"], fold.at(fold.n))
            else:
                act.wait_ge(S[f"raw_ready{tile % RAW}"], halves.at(halves.n, 16, 4) + 16)
            if misc:
                act.wait_ge(S["misc_done"], m.at(m.n))
            elif q.n:
                act.wait_ge(S["mm_done"], q.at(q.n))
            act.activation(WHI[halves.n % HL][:], raw_view(tile % RAW, half, kind), ACT.Copy).then_inc(halves.next(), 1)

        def serve(f):
            act.wait_ge(S["act_req"], req.at(req.n + 1))
            f().then_inc(req.next(), 1)

        def split_x(src, dst, n, added=None):
            act.wait_ge(S["split_req"], split.at(split.n + 1))
            act.activation(dst, src, ACT.Copy)
            if added is not None and added > 0:
                act.wait_ge(S["squares_added"], added)
            act.activation(T[2 + split.n % 2][:, 0:n], src, ACT.Square).then_inc(split.next(), 1)

        def norm_sqrt(count=D):
            serve(lambda: act.activation(RTOK[:], RTOK[:], ACT.Sqrt, bias=EPSC[:], scale=1.0 / count))

        def load_pw(w, u):
            if q.n:
                act.wait_ge(S["mm_done"], q.at(q.n))
                if q.terms:
                    act.sem_inc(S["spacer"], 1)
            act.dma_start(PWR[pw_loads.n % 2][:], w.rearrange("(k p) n -> p k n", p=P)[:, :, u * P:(u + 1) * P]
                          ).then_inc(S[f"pw_ready{pw_loads.n % 2}"], 16)
            pw_loads.n += 1

        def split_pw():
            act.wait_ge(S[f"pw_ready{pw.n % 2}"], 16 * (pw.n // 2 + 1))
            act.activation(PWH[pw.n % 2][:], PWR[pw.n % 2][:], ACT.Copy).then_inc(S["pw_hi"], 1)
            pw.n += 1

        pw_loads, pw = Count(), Count()

        def split_branch(Y, parts):
            for c in range(2):
                serve(lambda: act.activation(parts[0][:, c, :], Y[:, c, :], ACT.Copy))

        def sigmoid_steps(w, following, after=lambda d: None):
            split_pw()
            for u in range(KC):
                if u < KC - 1:
                    load_pw(w, u + 1)
                elif following is not None:
                    load_pw(following, 0)
                convert()
                for j, (t0, n) in enumerate(BLOCKS):
                    if j == 2 and u < KC - 1:
                        split_pw()
                    serve(lambda: act.activation(T[req.n % 2][:, 0:n], T[req.n % 2][:, 0:n], ACT.Sigmoid))
                    q.n += 2
                after(u)

        def plain(units, flush=0):
            for u in range(units):
                if u < units - flush:
                    convert()
                q.n += 3

        def states_out_act(sample, prompt, pad, lots):
            for h in range(lots + 1):
                act.wait_ge(S["stage_full"], so.take())
                n = NSEQ * pad // lots if h < lots else pad
                dst = sample.rearrange("s r c -> (s r) c")[h * n:(h + 1) * n, :] if h < lots else prompt
                act.dma_start(dst, OUTST[0:n, :]).then_inc(S["stage_out"], 16)

        so = Count()
        act.wait_ge(S["consts"], 3)
        for t0, n in BLOCKS:
            for c in range(KC):
                act.wait_ge(S["mm_done"], q.n + 1)
                src = PS[:, q.n % BANKS, 0:n]
                act.activation(XHI[:, c, t0:t0 + n], src, ACT.Copy)
                if split.n >= 2:
                    act.wait_ge(S["split_done"], split.n - 1)
                act.activation(T[2 + split.n % 2][:, 0:n], src, ACT.Square).then_inc(split.next(), 1)
                q.n += 1
        m.n += 1
        for _ in range(LOOK):
            convert()
        load_pw(A["w_branch"][0, BR_D], 0)
        for l in range(DEPTH):
            m.n += 3
            norm_sqrt()
            plain(2)
            m.n += 1
            convert()
            m.n += NT
            serve(lambda: act.activation(VR[:], MV[:, :, 1], ACT.Sqrt, bias=EPSC[:]))
            convert(misc=True)
            act.wait_ge(S["v_ready"], l + 1)
            act.dma_start(O["v_p"][l, 0], V[:, NT - 2, :]).then_inc(S["v_out"], 16)
            act.dma_start(O["v_s"][l].rearrange("s t c -> (s t) c"), V[0:64, NT - 1, :]).then_inc(S["v_out"], 16)
            m.n += 4
            for c in range(2):
                convert()
                q.n += 3
                act.wait_ge(S["act_req"], req.at(req.n + 1))
                gp, gs = GLU[:, c, PB:PB + SEQ], GLU[:, c, PB + SEQ:].rearrange("p (s t) -> p s t", s=NSEQ)[:, :, PB:]
                act.activation(gp, gp, ACT.Sigmoid)
                act.activation(gs, gs, ACT.Sigmoid).then_inc(req.next(), 1)
            plain(1)
            split_branch(UB, U_SPLIT)
            plain(1)
            m.n += 5 + 3
            states_out_act(O["b_s"][l], O["b_p"][l, 0], PB, 2)
            wb = A["w_branch"][l]
            sigmoid_steps(wb[BR_D], wb[BR_A])
            plain(4)
            m.n += 2
            states_out_act(O["a_s"][l], O["a_p"][l, 0], PA, 1)
            plain(2)
            split_branch(YA, YA_SPLIT)
            sigmoid_steps(wb[BR_A], wb[BR_B])
            m.n += 3
            plain(1)
            norm_sqrt(DB)
            plain(1)
            m.n += 1 + 3
            act.wait_ge(S["act_req"], req.at(req.n + 1))
            act.activation(YB[:, 0, :], YB[:, 0, :], ACT.Silu, bias=par(l, 0, R_LB), scale=par(l, 0, R_LG))
            act.activation(YB[:, 1, :], YB[:, 1, :], ACT.Silu, bias=par(l, 1, R_LB), scale=par(l, 1, R_LG)).then_inc(req.next(), 1)
            split_branch(YB, YB_SPLIT)
            m.n += 2
            states_out_act(O["c_s"][l], O["c_p"][l, 0], PC, 1)
            sigmoid_steps(wb[BR_B], wb[BR_C])
            m.n += 6
            split_branch(YP, YP_SPLIT)

            def merge_high(d):
                act.wait_ge(S["split_req"], split.at(split.n + 1))
                act.activation(MHI[:, d, :], MIXED[:, d, :], ACT.Copy).then_inc(split.next(), 1)

            sigmoid_steps(wb[BR_C], None, after=lambda d: merge_high(d) if d < MERGE_EARLY else None)
            act.wait_ge(S["mm_done"], q.at(q.n))
            for d in range(MERGE_EARLY, KC):
                merge_high(d)
            for d in range(KC):
                if not (l == 1 and d >= KC - LOOK):
                    convert()
                for t0, n in BLOCKS:
                    split_x(T[split.n % 2][:, 0:n], XHI[:, d, t0:t0 + n], n)
                q.n += 3
            m.n += 1
            norm_sqrt()
            if l == 0:
                m.n += 3
                def step(kind, g, last=False):
                    if kind == "GU":
                        for f in range(2):
                            convert()
                            q.n += 3
                            for t0, n in BLOCKS:
                                serve(lambda: act.activation(GS[:, f, t0:t0 + n], GS[:, f, t0:t0 + n], ACT.Silu))
                        for f in range(2):
                            convert()
                            q.n += 3
                            for t0, n in BLOCKS:
                                act.wait_ge(S["split_req"], split.at(split.n + 1))
                                act.activation(HHI[g % 2][:, f, t0:t0 + n], T[split.n % 2][:, 0:n], ACT.Copy).then_inc(split.next(), 1)
                    else:
                        convert()
                        if last:
                            load_pw(A["ple_w_proj"][0], 0)
                            for d in range(KC):
                                for j, (t0, n) in enumerate(BLOCKS):
                                    split_x(T[split.n % 2][:, 0:n], XHI[:, d, t0:t0 + n], n, added=3 * d + j - 1)
                        q.n += 24
                        convert()

                head, body, tail = ffn_schedule(FFN_GROUPS, FFN_LOOP)
                for s in head:
                    step(*s)
                cs = [halves, q, fold, req, split]
                per = {halves: 12, q: 72, fold: 4, req: 12, split: 12}
                with act.Fori(0, FFN_LOOP) as i:
                    st = looped(cs, i, per)
                    for s in body:
                        step(*s)
                leave(cs, st, per, FFN_LOOP)
                kp[0] += 12 * (FFN_LOOP - 1)
                for s in tail:
                    step(*s, last=(s == tail[-1]))
            else:
                for j in range(NT):
                    n = tokens(j)
                    if j == 0:
                        act.wait_ge(S["counts_ready"], 1)
                    if j >= 3:
                        act.wait_ge(S[f"rows_gone{j % 3}"], 32 * (j // 3))
                    for h in range(2):
                        act.wait_ge(S["mm_done"], q.n + 1)
                        src = PS[0:n, q.n % BANKS, :]
                        act.activation(YT[j % 3][0:n, h * 512:h * 512 + 512], src, ACT.Copy, scale=RTOK[0:n, j:j + 1]).then_inc(S["evicted"], 1)
                        q.n += 1
                    act.wait_ge(S["evicted"], q.n)
                    act.sem_inc(S["rows_ready"], 1)
                serve(lambda: act.activation(TW[:], TW[:], ACT.Sigmoid))
                m.n += 5
                act.wait_ge(S["items_ready"], 1)
                n_items = act.value_load(ITEMS[0:1, L_NUM:L_NUM + 1], min_val=NE, max_val=SLOTS)
                cs = [halves, q, m, req, split]
                per = {halves: 2 * len(item_kinds), q: 12 * MOE_GROUPS, m: 14, req: 2 * MOE_GROUPS, split: KC + 2 * MOE_GROUPS}
                kp_main = kp[0]
                kp[0], kp[1] = 0, item_kinds * 2
                for _ in range(LOOK):
                    convert()

                def prepare(k):
                    act.wait_ge(S["misc_done"], m.at(m.n + 1))
                    act.sem_inc(S["spacer"], 1)
                    act.activation(XSH[:, k, :], PS[:, 6 + m.n % 2, 0:CAP], ACT.Copy, scale=gain(3)[:, k:k + 1]).then_inc(split.next(), 1)
                    m.n += 1

                def item_out(number, row):
                    act.wait_ge(S["ys_out"], number * 48)
                    for j, (r0, n) in enumerate(XBLK):
                        act.wait_ge(S["ys_full"], number * 3 + (j + 1))
                        act.dma_start(YS[bass.ds(row + r0, n), :], YT[j][0:n, :]).then_inc(S["ys_out"], 16)

                for k in range(KC):
                    prepare(k)
                with act.Fori(0, SLOTS) as it:
                    with act.If(it < n_items):
                        size = act.value_load(ITEMS[0:1, bass.ds(it + L_SIZE, 1)], min_val=0, max_val=len(SIZES) - 1)
                        row = act.value_load(ITEMS[0:1, bass.ds(it + L_ROW, 1)], min_val=0, max_val=PAIRS)
                        st = looped(cs, it, per)

                        def conv():
                            ahead = kp[0] - 2 * len(item_kinds)
                            if ahead >= 0:
                                with act.If(n_items < it + 2):
                                    act.wait_ge(S["folded"], fold.at(fold.n + 1 + ahead // 2))
                                    act.sem_inc(S["spacer"], 1)
                            convert()

                        def item(rows):
                            kp[0] = LOOK

                            def step(kind, g, between=lambda: None):
                                if kind == "GU":
                                    for f in range(2):
                                        conv()
                                        q.n += 1
                                        serve(lambda: act.activation(EG[:, f, 0:rows], EG[:, f, 0:rows], ACT.Silu))
                                    for f in range(2):
                                        conv()
                                        q.n += 1
                                        act.wait_ge(S["split_req"], split.at(split.n + 1))
                                        act.activation(EHI[g % 2][:, f, 0:rows], T[split.n % 2][:, 0:rows], ACT.Copy).then_inc(split.next(), 1)
                                else:
                                    conv()
                                    between()
                                    q.n += KC
                                    conv()

                            head, body, tail = ffn_schedule(MOE_GROUPS, MOE_LOOP)
                            for s in head:
                                step(*s)
                            item_out(it, row)
                            m.n += 6
                            cs2 = [halves, q, req, split]
                            per2 = {halves: 12, q: 24, req: 4, split: 4}
                            with act.Fori(0, MOE_LOOP) as i:
                                st2 = looped(cs2, i, per2)
                                for s in body:
                                    step(*s)
                            leave(cs2, st2, per2, MOE_LOOP)
                            kp[0] += 12 * (MOE_LOOP - 1)
                            step(*tail[0])
                            step(*tail[1], between=lambda: [prepare(k) for k in range(KC)])
                            step(*tail[2])

                        sized(act, size, cs, item)
                        leave_items(cs, st, per, n_items)
                row = act.value_load(ITEMS[0:1, bass.ds(n_items + L_ROW, 1)], min_val=0, max_val=PAIRS)
                item_out(n_items, row)
                m.n += 6
                kp[0], kp[1] = kp_main + LOOK, kinds
                fold.n += (LOOK + 1) // 2

                def weigh(j):
                    n = tokens(j)
                    act.wait_ge(S[f"gathered{j % GATHERS}"], 32 * (j // GATHERS + 1))
                    y0 = YG[j % GATHERS][0][0:n, :]
                    act.activation(y0, y0, ACT.Copy, scale=TW[0:n, 0, j:j + 1]).then_inc(S["weighted"], 1)

                load_pw(A["ple_w_proj"][1], 0)
                weigh(0)
                for j in range(NT):
                    n = tokens(j)
                    if j + 1 < NT:
                        weigh(j + 1)
                    for h in range(2):
                        act.wait_ge(S["misc_done"], m.at(m.n + 1))
                        act.sem_inc(S["spacer"], 1)
                        src = PS[:, 6 + m.n % 2, 0:4 * P].rearrange("p (k t) -> p k t", k=4)[:, :, 0:n]
                        act.activation(XHI[:, 4 * h:4 * h + 4, j * P:j * P + n], src, ACT.Copy)
                        if j or h:
                            act.wait_ge(S["split_done"], split.at(split.n - 1))
                            act.sem_inc(S["spacer"], 1)
                        act.activation(TC[h][:, :, 0:n], src, ACT.Square).then_inc(split.next(), 1)
                        m.n += 1
            split_branch(PT, P_SPLIT)
            m.n += 6 + 1
            norm_sqrt()
            m.n += 3
            split_pw()
            for d in range(KC):
                if d < KC - 1:
                    load_pw(A["ple_w_proj"][l], d + 1)
                elif l == 0:
                    load_pw(A["w_branch"][1, BR_D], 0)
                if not (l == 1 and d >= KC - LOOK):
                    convert()
                for j, (t0, n) in enumerate(BLOCKS):
                    if j == 2 and d < KC - 1:
                        split_pw()
                    serve(lambda: act.activation(T[req.n % 2][:, 0:n], T[req.n % 2][:, 0:n], ACT.Sigmoid))
                    q.n += 2
                    act.wait_ge(S["split_req"], split.at(split.n + 1))
                    x = XNEW[:, d, t0:t0 + n]
                    act.activation(T[2 + split.n % 2][:, 0:n], x, ACT.Square).then_inc(split.next(), 1)
                    if l == 1:
                        act.wait_ge(S["split_hi"], split.at(split.n))
                        act.sem_inc(S["spacer"], 1)
                        act.activation(x, x, ACT.Copy, scale=gain(6)[:, d:d + 1]).then_inc(S["xnew_ready"], 1)
            if l == 0:
                for d in range(KC):
                    act.wait_ge(S["split_req"], split.at(split.n + 1))
                    act.activation(XHI[:, d, :], XNEW[:, d, :], ACT.Copy).then_inc(split.next(), 1)
        norm_sqrt()
        m.n += 1
        act.wait_ge(S["rtok_ready"], 1)
        for j in range(NT):
            n = tokens(j)
            if j >= OUTS:
                act.wait_ge(S[f"outputs{j % OUTS}"], 16 * (j // OUTS))
            act.wait_ge(S["misc_done"], m.at(m.n + 1))
            act.sem_inc(S["spacer"], 1)
            act.activation(YOUT[j % OUTS][0:n, 512:D], PS[0:n, 6 + m.n % 2, :], ACT.Copy, scale=RTOK[0:n, j:j + 1]).then_inc(S["misc_free"], 1)
            m.n += 1
            act.wait_ge(S["misc_free"], m.at(m.n))
            act.wait_ge(S["y_full"], j + 1)
            dst = O["y_p"][0, j * P:(j + 1) * P, :] if j < NT - 1 else O["y_s"].rearrange("s t d -> (s t) d")
            act.sem_inc(S["spacer"], 1)
            act.dma_start(dst, YOUT[j % OUTS][0:n, :]).then_inc(S[f"outputs{j % OUTS}"], 16)
        for i in range(OUTS):
            act.wait_ge(S[f"outputs{i}"], 16 * len(range(i, NT, OUTS)))
        act.wait_ge(S["stage_out"], 16 * 7 * DEPTH)
        act.wait_ge(S["v_out"], 32 * DEPTH)

    @block.vector
    def _(dve):
        v = Engine(dve, S["dve_own"])
        conv, q, m = Count(S["lo_ready"]), Count(S["evicted"]), Count(S["misc_free"])
        req, split = Count(S["act_req"]), Count(S["split_done"])
        sreq = Count(S["split_req"])
        kp = [0, kinds]
        def convert():
            kind, norm = kp[1][kp[0] // 2]
            kp[0] += 1
            dve.wait_ge(S["hi_ready"], conv.at(conv.n + 1))
            s = conv.n % HL
            v.do(dve.tensor_tensor(WLO[s][:], raw_view(conv.n // 2 % RAW, conv.n % 2, kind), WHI[s][:].bitcast(F32), ALU.subtract), conv)

        def main_ready():
            dve.wait_ge(S["mm_done"], q.at(q.n + 1))
            return PS[:, q.n % BANKS, :]

        def misc_ready():
            dve.wait_ge(S["misc_done"], m.at(m.n + 1))
            return PS[:, 6 + m.n % 2, :]

        pending = []

        def finish_x():
            if not pending:
                return
            d, j, src, n_req, low, add = pending.pop()
            t0, n = BLOCKS[j]
            dve.wait_ge(S["split_hi"], sreq.at(n_req))
            if low:
                v.do(dve.tensor_tensor(XLO[:, d, t0:t0 + n], src, XHF[:, d, t0:t0 + n], ALU.subtract), None if add else split)
            if not add:
                v.sync()
                return
            sq = T[2 + (n_req - 1) % 2][:, 0:n]
            if d == 0:
                v.do(dve.tensor_copy(SQS[:, t0:t0 + n], sq), split)
            else:
                v.do(dve.tensor_tensor(SQS[:, t0:t0 + n], SQS[:, t0:t0 + n], sq, ALU.add), split)
            v.sync()

        def split_x(d, j, src, low=True, add=True):
            dve.sem_inc(sreq.next(), 1)
            finish_x()
            pending.append((d, j, src, sreq.n, low, add))

        def norm_tokens():
            ps = misc_ready()
            v.do(dve.tensor_copy(RTOK[:, 0:NT - 1], ps[:, 0:NT - 1]))
            v.do(dve.tensor_copy(RTOK[0:64, NT - 1:NT], ps[0:64, NT - 1:NT]), m)
            request()
            v.do(dve.reciprocal(RTOK[:], RTOK[:]))
            v.sync()

        def diagonals():
            for j, (t0, n) in enumerate(BLOCKS):
                whole = n // P
                dst = T[j][:, 0:whole * P].rearrange("p (j t) -> p j t", t=P)
                c0 = t0 // P
                v.do(dve.tensor_tensor(dst, IDF[:].unsqueeze(1).to_broadcast([P, whole, P]),
                                       RTOK[:, c0:c0 + whole].unsqueeze(2).to_broadcast([P, whole, P]), ALU.mult))
                if n % P:
                    v.do(dve.tensor_scalar(T[j][:, whole * P:n], IDF[:, 0:n % P], RTOK[:, c0 + whole:c0 + whole + 1], None, ALU.mult))
            v.sync()
            dve.sem_inc(S["diag_ready"], 1)

        def spread_rstd():
            for t0, n in BLOCKS:
                ps = misc_ready()
                v.do(dve.tensor_copy(RSTD[:, t0:t0 + n], ps[:, 0:n]), m)
            v.sync()

        def norm():
            norm_tokens()
            diagonals()
            spread_rstd()

        def request():
            v.sync()
            dve.sem_inc(req.next(), 1)
            dve.wait_ge(S["act_done"], req.at(req.n))

        pw = Count()

        def split_pw():
            dve.wait_ge(S["pw_hi"], pw.n + 1)
            s = pw.n % 2
            v.do(dve.tensor_tensor(PWL[s][:], PWR[s][:], PWH[s][:].bitcast(F32), ALU.subtract))
            v.sync()
            dve.sem_inc(S["pw_lo"], 1)
            pw.n += 1

        def split_branch(Y, parts):
            v.sync()
            dve.sem_inc(req.next(), 1)
            dve.sem_inc(req.next(), 1)
            for c in range(2):
                dve.wait_ge(S["act_done"], req.at(req.n - 1 + c))
                v.do(dve.tensor_tensor(parts[1][:, c, :], Y[:, c, :], parts[0][:, c, :].bitcast(F32), ALU.subtract))
            v.sync()

        bg = [iter(())]

        def background(k):
            for _ in range(k):
                next(bg[0], None)

        def merge_low(d):
            dve.wait_ge(S["split_hi"], split.at(split.n + 1))
            v.do(dve.tensor_tensor(MLO[:, d, :], MIXED[:, d, :], MHI[:, d, :].bitcast(F32), ALU.subtract), split)

        def gate_project(br_first, br_pulls, merge=False):
            split_pw()
            for d in range(KC):
                convert()
                if merge and 1 <= d <= MERGE_EARLY:
                    merge_low(d - 1)
                for j, (t0, n) in enumerate(BLOCKS):
                    if j == 2 and d < KC - 1:
                        split_pw()
                    ps = main_ready()
                    t = T[req.n % 2][:, 0:n]
                    v.do(dve.tensor_tensor(t, ps[:, 0:n], RSTD[:, t0:t0 + n], ALU.mult), q)
                    v.sync()
                    dve.sem_inc(req.next(), 1)
                    background(br_pulls)
                    ps = main_ready()
                    dve.wait_ge(S["act_done"], req.at(req.n))
                    dst = MIXED[:, d, t0:t0 + n]
                    if br_first:
                        v.do(dve.tensor_tensor(dst, ps[:, 0:n], t, ALU.mult), q)
                        v.sync()
                    else:
                        mk = v.do(dve.tensor_tensor(t, ps[:, 0:n], t, ALU.mult), q)
                        v.sync(mk)
                        v.do(dve.tensor_tensor(dst, dst, t, ALU.add))
                        v.sync()
                if merge:
                    dve.sem_inc(sreq.next(), 1)

        def padded_unit(buf, pad, c, times=False, tmp=[0]):
            convert()
            for j, (t0, n) in enumerate(BLOCKS):
                ps = main_ready()
                if times:
                    t = T[2 + tmp[0] % 2]
                    tmp[0] += 1
                    v.do(dve.tensor_tensor(t[:, 0:n], ps[:, 0:n], RSTD[:, t0:t0 + n], ALU.mult), q)
                    v.sync()
                    for a, b, dst in pieces(j, buf[:, c, :], pad):
                        v.do(dve.tensor_tensor(dst, dst, shaped(t[:, a:a + b], dst), ALU.mult))
                    v.sync()
                else:
                    ds = pieces(j, buf[:, c, :], pad)
                    for x, (a, b, dst) in enumerate(ds):
                        v.do(dve.tensor_tensor(dst, shaped(ps[:, a:a + b], dst), shaped(RSTD[:, t0 + a:t0 + a + b], dst), ALU.mult),
                             q if x == len(ds) - 1 else None)
                background(1)
            v.sync()

        def pad_sample(buf, c, pad):
            return buf[:, c, pad + SEQ:].rearrange("p (s t) -> p s t", s=NSEQ)

        def states_out(buf, tmp, pad, lots):
            for c in range(2):
                x = pad_sample(buf, c, pad)[:, :, DSEQ:]
                v.do(dve.tensor_copy(tmp[:, c, 0:NSEQ * pad].rearrange("p (s t) -> p s t", s=NSEQ), x), tok if c == 1 else None)
            for h in range(lots + 1):
                n = NSEQ * pad // lots if h < lots else pad
                ps = misc_ready()
                if stage.n:
                    dve.wait_ge(S["stage_out"], 16 * stage.n)
                v.do(dve.tensor_copy(OUTST[0:n, :], ps[0:n, 0:DB]), stage)
                v.sync()
                dve.sem_inc(m.next(), 1)

        tok, stage = Count(S["tok_ready"]), Count(S["stage_full"])

        for t_, val in ((ONES, 1.0), (EPSC, EPS)):
            v.do(dve.memset(t_[:], val))
        v.do(dve.memset(BDRAW[:], 0.0))
        v.do(dve.memset(PBD[:], 0.0))
        for c in range(2):
            for h in range(2):
                v.do(dve.memset(WIN[64 * h:64 * h + 64, c:c + 1], float(WINDOWS[2 * c + h])))
        v.sync()
        dve.sem_inc(S["sgu_zeroed"], 1)
        v.do(dve.reciprocal(WINV[:], WIN[:]))
        dve.wait_ge(S["consts"], 3)
        v.do(dve.tensor_copy(IDR[:], IDF[:]))
        for c in range(2):
            v.do(dve.tensor_scalar(FIXT[:, c, :], FIXT[:, c, :], WIN[:, c:c + 1], None, ALU.min))
        v.sync()
        v.do(dve.reciprocal(FIXT[:], FIXT[:]))
        v.sync()
        sqc = Count(S["sq_ready"])
        v.do(dve.memset(RTOK[:], 1.0))
        for j, (t0, n) in enumerate(BLOCKS):
            for c in range(KC):
                ps = main_ready()
                dve.wait_ge(S["split_hi"], split.n + 1)
                sreq.n += 1
                v.do(dve.tensor_tensor(XLO[:, c, t0:t0 + n], ps[:, 0:n], XHF[:, c, t0:t0 + n], ALU.subtract), q)
                sq = T[2 + split.n % 2][:, 0:n]
                if c == 0:
                    v.do(dve.tensor_copy(SQS[:, t0:t0 + n], sq), split)
                else:
                    v.do(dve.tensor_tensor(SQS[:, t0:t0 + n], SQS[:, t0:t0 + n], sq, ALU.add), split)
                v.sync()
            if j == 1:
                ps = misc_ready()
                v.do(dve.tensor_copy(PAR[:], ps[:, 0:4 * 38 + 7 * KC]), m)
                v.sync()
                dve.sem_inc(S["par_ready"], 1)
        dve.sem_inc(S["split_req"], sreq.n)
        dve.sem_inc(sqc.next(), 1)
        for _ in range(LOOK):
            convert()

        for l in range(DEPTH):
            if l:
                for d in range(KC):
                    dve.wait_ge(S["split_hi"], sreq.at(sreq.n - KC + d + 1))
                    v.do(dve.tensor_tensor(XLO[:, d, :], XNEW[:, d, :], XHF[:, d, :], ALU.subtract), split)
                v.sync()
                v.do(dve.memset(BDRAW[:], 0.0))
                v.sync()
                dve.sem_inc(S["sgu_zeroed"], 1)
            norm()
            v.do(dve.memset(MV[:], 1.0))
            for c in range(2):
                convert()
                for t0, n in BLOCKS:
                    ps = main_ready()
                    v.do(dve.tensor_tensor(UB[:, c, t0:t0 + n], ps[:, 0:n], RSTD[:, t0:t0 + n], ALU.mult), q)
            convert()
            for j in range(NT):
                n = tokens(j)
                ps = misc_ready()
                v.do(dve.tensor_scalar(V[0:n, j, :], ps[0:n, 0:DB], RTOK[0:n, j:j + 1], None, ALU.mult), m)
                v.sync()
                v.do(dve.bn_stats(BNS[0:n, j, :], V[0:n, j, :]))
                v.sync()
                v.do(dve.bn_aggr(MV[0:n, j, :], BNS[0:n, j, :]))
            ps = misc_ready()
            v.do(dve.tensor_tensor(WT[:], ps.rearrange("p (g t) -> p g t", g=GROUPS), TRIL[:].unsqueeze(1).to_broadcast([P, GROUPS, P]),
                                   ALU.mult), m)
            ps = misc_ready()
            v.do(dve.tensor_tensor(BD[:], ps[0:64, 0:GROUPS * 64].rearrange("p (g t) -> p g t", g=GROUPS),
                                   TRIL[0:64, 0:64].unsqueeze(1).to_broadcast([64, GROUPS, 64]), ALU.mult), m)
            v.do(dve.memset(GLU[:, :, 0:PB], 0.0))
            ps = misc_ready()
            for c in range(2):
                for h in range(2):
                    x = (c * 2 + h) * 120
                    v.do(dve.tensor_copy(pad_sample(GLU, c, PB)[:, 4 * h:4 * h + 4, 0:PB], ps[:, x:x + 120].rearrange("p (s t) -> p s t", s=4)),
                         m if (c, h) == (1, 1) else None)
            ps = misc_ready()
            v.do(dve.tensor_copy(KEEP[:], ps[:, 0:272]), m)
            v.sync()
            v.sync()
            dve.sem_inc(req.next(), 1)
            dve.wait_ge(S["act_done"], req.at(req.n))
            v.do(dve.reciprocal(VR[:], VR[:]))
            v.sync()
            for j in range(NT):
                n = tokens(j)
                v.do(dve.tensor_scalar(V[0:n, j, :], V[0:n, j, :], MV[0:n, j, 0:1], VR[0:n, j:j + 1], ALU.subtract, ALU.mult))
            v.sync()
            dve.wait_ge(S["sgu_loaded"], 16 * (1 + NSEQ + GROUPS + 2) * (l + 1))
            for j in range(NT):
                n = tokens(j)
                v.do(dve.tensor_tensor(V[0:n, j, :], V[0:n, j, :], LNG[0:n, :], ALU.mult))
            v.sync()
            for j in range(NT):
                n = tokens(j)
                v.do(dve.tensor_tensor(V[0:n, j, :], V[0:n, j, :], LNB[0:n, :], ALU.add))
            v.sync()
            dve.sem_inc(S["v_ready"], 1)
            convert()
            for c in range(2):
                padded_unit(GLU, PB, c)
                dve.sem_inc(req.next(), 1)
                dve.wait_ge(S["act_done"], req.at(req.n))
            padded_unit(GLU, PB, 0, times=True)
            for c in range(2):
                for jj in range(2):
                    ps = misc_ready()
                    t4 = YB[:, c, jj * 512:jj * 512 + 512]
                    v.do(dve.tensor_tensor(t4.rearrange("p (j t) -> p j t", j=4), ps.rearrange("p (j t) -> p j t", j=4),
                                           BIAS[:, c, :].unsqueeze(1).to_broadcast([P, 4, P]), ALU.add), m)
                    v.sync()
                    u4 = UB[:, c, jj * 512:jj * 512 + 512]
                    v.do(dve.tensor_tensor(u4, u4, t4, ALU.mult))
            ps = misc_ready()
            for c in range(2):
                v.do(dve.tensor_tensor(YB[:, c, SEQ:].rearrange("p (s t) -> p s t", s=NSEQ), ps[:, c * 64:c * 64 + 64].rearrange("p (s t) -> p s t", s=NSEQ),
                                       BIAS[:, c, 0:DSEQ].unsqueeze(1).to_broadcast([P, NSEQ, DSEQ]), ALU.add), m if c else None)
            v.sync()
            v.do(dve.tensor_tensor(UB[:, :, SEQ:], UB[:, :, SEQ:], YB[:, :, SEQ:], ALU.mult))
            v.sync()
            split_branch(UB, U_SPLIT)
            dve.sem_inc(S["br_d"], 1)
            padded_unit(GLU, PB, 1, times=True)
            states_out(GLU, YB, PB, 2)

            def conv_b():
                parts = []
                for c in range(2):
                    parts.append((c, lambda k, c=c: GLU[:, c, k:k + SEQ], YB[:, c, 0:SEQ]))
                    parts.append((c, lambda k, c=c: pad_sample(GLU, c, PB)[:, :, k:k + DSEQ], YB[:, c, SEQ:].rearrange("p (s t) -> p s t", s=NSEQ)))
                marks = [None] * 4
                for k in range(PB + 1):
                    for x, (c, src, dst) in enumerate(parts):
                        w = par(l, c, R_CB + k)
                        if k == 0:
                            marks[x] = v.do(dve.tensor_scalar(dst, src(k), w, par(l, c, R_BIAS), ALU.mult, ALU.add))
                        else:
                            v.sync(marks[x])
                            marks[x] = v.do(dve.scalar_tensor_tensor(dst, src(k), w, dst, ALU.mult, ALU.add))
                        yield

            bg[0] = conv_b()
            dve.wait_ge(S["v_out"], 32 * (l + 1))
            gate_project(True, 2)
            v.do(dve.memset(ZA[:, :, 0:PA], 0.0))
            for c in range(2):
                v.do(dve.tensor_copy(pad_sample(ZA, c, PA)[:, :, 0:PA], KEEP[:, 240 + c * 16:256 + c * 16].rearrange("p (s t) -> p s t", s=NSEQ)))
            for c in range(2):
                padded_unit(ZA, PA, c)
            for c in range(2):
                padded_unit(ZA, PA, c, times=True)
            states_out(ZA, YA, PA, 1)
            for k in range(PA + 1):
                for c in range(2):
                    for src, dst in ((ZA[:, c, k:k + SEQ], YA[:, c, 0:SEQ]),
                                     (pad_sample(ZA, c, PA)[:, :, k:k + DSEQ], YA[:, c, SEQ:].rearrange("p (s t) -> p s t", s=NSEQ))):
                        w = par(l, c, R_CA + k)
                        if k == 0:
                            v.do(dve.tensor_scalar(dst, src, w, None, ALU.mult))
                        else:
                            v.do(dve.scalar_tensor_tensor(dst, src, w, dst, ALU.mult, ALU.add))
                v.sync()
            for c in range(2):
                convert()
                for t0, n in BLOCKS:
                    ps = main_ready()
                    t = T[2]
                    v.do(dve.tensor_tensor(t[:, 0:n], ps[:, 0:n], RSTD[:, t0:t0 + n], ALU.mult), q)
                    v.sync()
                    v.do(dve.tensor_tensor(YA[:, c, t0:t0 + n], YA[:, c, t0:t0 + n], t[:, 0:n], ALU.mult))
                    v.sync()
            split_branch(YA, YA_SPLIT)
            dve.sem_inc(S["br_a"], 1)
            gate_project(False, 3)
            for _ in bg[0]:
                pass
            v.sync()
            dve.sem_inc(S["yb_ready"], 1)
            for t0, n in BLOCKS:
                ps = misc_ready()
                for c in range(2):
                    v.do(dve.scalar_tensor_tensor(YB[:, c, t0:t0 + n], ps[:, 0:n], -1.0 / DB, YB[:, c, t0:t0 + n], ALU.mult, ALU.add), m if c else None)
                v.sync()
                v.do(dve.tensor_tensor(SQB[:, :, t0:t0 + n], YB[:, :, t0:t0 + n], YB[:, :, t0:t0 + n], ALU.mult))
            v.sync()
            dve.sem_inc(S["lnsq_ready"], 1)
            v.do(dve.memset(ZP[:, :, 0:PC], 0.0))
            for c in range(2):
                v.do(dve.tensor_copy(pad_sample(ZP, c, PC)[:, :, 0:PC], KEEP[:, c * 120:c * 120 + 120].rearrange("p (s t) -> p s t", s=NSEQ)))
            padded_unit(ZP, PC, 0)
            norm_tokens()
            diagonals()
            for t0, n in BLOCKS:
                ps = misc_ready()
                for c in range(2):
                    y = YB[:, c, t0:t0 + n]
                    v.do(dve.tensor_tensor(y, y, ps[:, 0:n], ALU.mult), m if c else None)
            v.sync()
            dve.sem_inc(req.next(), 1)
            dve.wait_ge(S["act_done"], req.at(req.n))
            split_branch(YB, YB_SPLIT)
            dve.sem_inc(S["br_b"], 1)
            padded_unit(ZP, PC, 1)
            states_out(ZP, YP, PC, 1)

            def pool_c():
                def at_(c, s, h):
                    a, b = (64 * h if h is not None else 0), (64 * h + 64 if h is not None else P)
                    return ((ZP[a:b, c, PC - s:PC - s + SEQ], YP[a:b, c, 0:SEQ]),
                            (pad_sample(ZP, c, PC)[a:b, :, PC - s:PC - s + DSEQ], YP[a:b, c, SEQ:].rearrange("p (s t) -> p s t", s=NSEQ)))
                last = [None, None]
                for s in range(1, POOL_MAX):
                    for c in range(2):
                        w0, w1 = WINDOWS[2 * c], WINDOWS[2 * c + 1]
                        if s >= w1:
                            continue
                        h = None if s < w0 else 1
                        if last[c]:
                            v.sync(last[c])
                        for x, (src, dst) in enumerate(at_(c, s, h)):
                            first = at_(c, 0, h)[x][0] if s == 1 else dst
                            last[c] = v.do(dve.tensor_tensor(dst, first, src, ALU.add))
                            yield
                v.sync()
                for c in range(2):
                    v.do(dve.tensor_tensor(YP[:, c, 0:16], YP[:, c, 0:16], FIXT[:, c, :], ALU.mult))
                    (src, dst), (ssrc, sdst) = at_(c, 0, None)
                    v.do(dve.scalar_tensor_tensor(dst[:, 16:], dst[:, 16:], WINV[:, c:c + 1], src[:, 16:], ALU.mult, ALU.subtract))
                    v.do(dve.scalar_tensor_tensor(sdst, sdst, WINV[:, c:c + 1], ssrc, ALU.mult, ALU.subtract))
                    yield
                v.sync()
                for c in range(2):
                    v.do(dve.tensor_tensor(YP[:, c, 0:16], YP[:, c, 0:16], ZP[:, c, PC:PC + 16], ALU.subtract))
                v.sync()
                yield

            bg[0] = pool_c()
            gate_project(False, 2)
            for _ in bg[0]:
                pass
            v.sync()
            dve.sem_inc(S["pooled"], 1)
            for c in range(2):
                for t0, n in BLOCKS:
                    ps = misc_ready()
                    v.do(dve.tensor_scalar(YP[:, c, t0:t0 + n], ps[:, 0:n], par(l, c, R_PS), None, ALU.mult), m)
            v.sync()
            split_branch(YP, YP_SPLIT)
            dve.sem_inc(S["br_c"], 1)
            gate_project(False, 0, merge=True)
            for d in range(MERGE_EARLY, KC):
                merge_low(d)
            v.sync()
            for d in range(KC):
                if not (l == 1 and d >= KC - LOOK):
                    convert()
                for j, (t0, n) in enumerate(BLOCKS):
                    ps = main_ready()
                    t = T[sreq.n % 2][:, 0:n]
                    v.do(dve.tensor_tensor(t, ps[:, 0:n], XHF[:, d, t0:t0 + n], ALU.add), q)
                    v.sync()
                    v.do(dve.tensor_tensor(t, t, XLF[:, d, t0:t0 + n], ALU.add))
                    v.sync()
                    split_x(d, j, t)
            finish_x()
            dve.sem_inc(sqc.next(), 1)
            dve.wait_ge(S["stage_out"], 16 * stage.n)
            if l == 0:
                norm()
                for d in range(KC):
                    v.do(dve.tensor_tensor(ACC[:, d, :], XHF[:, d, :], XLF[:, d, :], ALU.add))
                v.sync()

                def step(kind, g, last=False):
                    if kind == "GU":
                        for f in range(2):
                            convert()
                            for t0, n in BLOCKS:
                                ps = main_ready()
                                v.do(dve.tensor_tensor(GS[:, f, t0:t0 + n], ps[:, 0:n], RSTD[:, t0:t0 + n], ALU.mult), q)
                                v.sync()
                                dve.sem_inc(req.next(), 1)
                        for f in range(2):
                            convert()
                            for j, (t0, n) in enumerate(BLOCKS):
                                ps = main_ready()
                                t = T[sreq.n % 2][:, 0:n]
                                if f == 0 and j == 0:
                                    dve.wait_ge(S["act_done"], req.at(req.n))
                                v.do(dve.tensor_tensor(t, ps[:, 0:n], RSTD[:, t0:t0 + n], ALU.mult), q)
                                v.sync()
                                v.do(dve.tensor_tensor(t, t, GS[:, f, t0:t0 + n], ALU.mult))
                                v.sync()
                                dve.sem_inc(sreq.next(), 1)
                                dve.wait_ge(S["split_hi"], sreq.at(sreq.n))
                                v.do(dve.tensor_tensor(HLO[g % 2][:, f, t0:t0 + n], t, HHI[g % 2][:, f, t0:t0 + n].bitcast(F32), ALU.subtract), split)
                                v.sync()
                    else:
                        convert()
                        for d in range(KC):
                            for j, (t0, n) in enumerate(BLOCKS):
                                ps = main_ready()
                                if last:
                                    t = T[sreq.n % 2][:, 0:n]
                                    v.do(dve.tensor_tensor(t, ps[:, 0:n], ACC[:, d, t0:t0 + n], ALU.add), q)
                                    v.sync()
                                    split_x(d, j, t, add=False)
                                else:
                                    a = ACC[:, d, t0:t0 + n]
                                    v.do(dve.tensor_tensor(a, ps[:, 0:n], a, ALU.add), q)
                        finish_x()
                        v.sync()
                        convert()

                head, body, tail = ffn_schedule(FFN_GROUPS, FFN_LOOP)
                for s in head:
                    step(*s)
                cs = [conv, q, req, split, sreq, v.own]
                per = {conv: 12, q: 72, req: 12, split: 12, sreq: 12, v.own: 12}
                with dve.Fori(0, FFN_LOOP) as i:
                    st = looped(cs, i, per)
                    for s in body:
                        step(*s)
                leave(cs, st, per, FFN_LOOP)
                kp[0] += 12 * (FFN_LOOP - 1)
                for s in tail:
                    step(*s, last=(s == tail[-1]))
                dve.wait_ge(S["squares_added"], 3 * KC)
                dve.sem_inc(sqc.next(), 1)
            else:
                v.do(dve.memset(XG[:], 0.0))
                v.sync()
                dve.sem_inc(S["phase_clear"], 1)
                v.do(dve.tensor_tensor(TRIS[:], TRIL[:], IDF[:], ALU.subtract))
                v.do(dve.memset(LG[:], 0.0))
                dve.wait_ge(S["rw_loaded"], 16)
                v.do(dve.tensor_tensor(RW[:], RW[:], gain(3).unsqueeze(2).to_broadcast([P, KC, NE]), ALU.mult))
                v.sync()
                v.do(dve.tensor_copy(RWH[:], RW[:]))
                v.sync()
                v.do(dve.tensor_tensor(RWL[:], RW[:], RWH[:].bitcast(F32), ALU.subtract))
                v.sync()
                dve.sem_inc(S["tri_ready"], 1)
                norm_tokens()
                for j, (t0, n) in enumerate(BLOCKS):
                    for d in ((0, 1, 2), (3, 4, 5), (6, 7))[j]:
                        v.do(dve.tensor_tensor(XF[:, d, :], XHF[:, d, :], XLF[:, d, :], ALU.add))
                    ps = misc_ready()
                    v.do(dve.tensor_copy(LGT[:, t0:t0 + n], ps[0:NE, 0:n]), m)
                v.sync()
                dve.sem_inc(S["x_whole"], 1)
                dve.sem_inc(S["logits_ready"], 1)
                ps = misc_ready()
                full, rest = NT - 1, tokens(NT - 1)
                v.do(dve.tensor_tensor(LG[:, 0:full, :], ps[:, 0:full * NE].rearrange("p (j e) -> p j e", e=NE),
                                       RTOK[:, 0:full].unsqueeze(2).to_broadcast([P, full, NE]), ALU.mult))
                v.do(dve.tensor_scalar(LG[0:rest, full, :], ps[0:rest, full * NE:NT * NE], RTOK[0:rest, full:NT], None, ALU.mult), m)
                v.sync()
                for j in range(NT):
                    v.do(dve.max(MX[:, j, :], LG[:, j, :]))
                v.sync()
                for j in range(NT):
                    v.do(dve.max_index(IX[:, j, :], MX[:, j, :], LG[:, j, :]))
                for k in range(2):
                    v.do(dve.tensor_tensor(TW[:, k, :], MX[:, :, k], MX[:, :, 1 - k], ALU.subtract))
                v.sync()
                dve.sem_inc(req.next(), 1)
                v.do(dve.tensor_copy(IXF[:], IX[:]))
                v.sync()
                dve.wait_ge(S["consts"], 5)
                for k in range(2):
                    v.do(dve.tensor_tensor(OH[k][:], IOT[:].unsqueeze(1).to_broadcast([P, NT, NE]),
                                           IXF[:, :, k:k + 1].to_broadcast([P, NT, NE]), ALU.is_equal))
                v.sync()
                v.do(dve.tensor_tensor(SS[:], OH[0][:], OH[1][:], ALU.add))
                v.do(dve.memset(CS[:, 0, :], 0.0))
                v.sync()
                v.do(dve.memset(SS[rest:P, full, :], 0.0))
                v.sync()
                for j in range(1, NT + 1):
                    v.do(dve.tensor_tensor(CS[:, j, :] if j < NT else TM[:, 0, :], CS[:, j - 1, :], SS[:, j - 1, :], ALU.add))
                    v.sync()
                dve.sem_inc(S["counts_ready"], 1)
                ps = misc_ready()
                v.do(dve.tensor_copy(CNT[:], ps[:, NT * NE:(NT + 1) * NE]))
                v.do(dve.memset(BASE[:, 0:1], 0.0))
                v.sync()
                for e in range(1, NE):
                    v.do(dve.tensor_tensor(BASE[:, e:e + 1], BASE[:, e - 1:e], CNT[:, e - 1:e], ALU.add))
                    v.sync()
                v.do(dve.tensor_tensor(TM[:], ps[:, 0:NT * NE].rearrange("p (j e) -> p j e", e=NE),
                                       BASE[:].unsqueeze(1).to_broadcast([P, NT, NE]), ALU.add), m)
                v.sync()
                for k in range(2):
                    v.do(dve.tensor_tensor(OH[k][:], OH[k][:], TM[:], ALU.mult))
                v.sync()
                for k in range(2):
                    v.do(dve.tensor_reduce(POSF[:, k, :], OH[k][:], AXX, ALU.add))
                v.sync()
                v.do(dve.tensor_copy(POSI[:], POSF[:]))
                v.sync()
                dve.sem_inc(S["places_ready"], 1)
                lrow = lambda r: LROW[0:1, r, :]
                further = lambda r, p_: LROW[0:1, r, 0:NE * EXTRA].rearrange("o (e x) -> o e x", x=EXTRA)[:, :, p_ - 1]
                firsts = lambda r: LROW[0:1, r, NE * EXTRA:NJ]
                ACTIVE, PLACE, EXPERT, ROW, OTHER, SIZE = range(6)
                for p_ in range(EXTRA + 1):
                    dst = further(SIZE, p_) if p_ else firsts(SIZE)
                    v.do(dve.tensor_scalar(dst, CNT[0:1, :], float(-CAP * p_), None, ALU.add))
                for p_ in range(1, EXTRA + 1):
                    v.do(dve.tensor_scalar(further(ACTIVE, p_), CNT[0:1, :], CAP * p_ + 0.5, None, ALU.is_ge))
                    v.do(dve.tensor_copy(further(EXPERT, p_), IOT[0:1, :]))
                    v.do(dve.tensor_scalar(further(ROW, p_), BASE[0:1, :], float(CAP * p_), None, ALU.add))
                v.do(dve.memset(firsts(ACTIVE), 1.0))
                v.do(dve.tensor_copy(firsts(EXPERT), IOT[0:1, :]))
                v.do(dve.tensor_copy(firsts(ROW), BASE[0:1, :]))
                v.sync()
                v.do(dve.memset(lrow(OTHER), 0.0))
                for size in SIZES[:-1]:
                    v.do(dve.tensor_scalar(lrow(PLACE), lrow(SIZE), size + 0.5, None, ALU.is_ge))
                    v.sync()
                    v.do(dve.tensor_tensor(lrow(OTHER), lrow(OTHER), lrow(PLACE), ALU.add))
                    v.sync()
                v.do(dve.tensor_copy(lrow(SIZE), lrow(OTHER)))
                v.sync()
                v.do(dve.tensor_copy(lrow(PLACE), lrow(ACTIVE)))
                v.sync()
                step_, a, b = 1, PLACE, OTHER
                while step_ < NJ:
                    v.do(dve.tensor_copy(LROW[0:1, b, 0:step_], LROW[0:1, a, 0:step_]))
                    v.do(dve.tensor_tensor(LROW[0:1, b, step_:], LROW[0:1, a, step_:], LROW[0:1, a, 0:NJ - step_], ALU.add))
                    v.sync()
                    a, b, step_ = b, a, step_ * 2
                v.do(dve.tensor_copy(LOUT[0:1, 3, 0:1], LROW[0:1, a, NJ - 1:NJ]))
                v.do(dve.tensor_tensor(lrow(b), lrow(a), lrow(ACTIVE), ALU.subtract))
                v.sync()
                wide = lambda ap: ap.unsqueeze(1).to_broadcast([1, SLOTS, NJ])
                for r, out in ((EXPERT, 0), (ROW, 1), (SIZE, 2)):
                    v.do(dve.tensor_tensor(LSEL[:], wide(lrow(b)), SLI[:].unsqueeze(2).to_broadcast([1, SLOTS, NJ]), ALU.is_equal))
                    v.sync()
                    for r2 in (ACTIVE, r):
                        v.do(dve.tensor_tensor(LSEL[:], LSEL[:], wide(lrow(r2)), ALU.mult))
                        v.sync()
                    v.do(dve.tensor_reduce(LOUT[0:1, out, :], LSEL[:], AXX, ALU.add))
                    v.sync()
                v.do(dve.memset(ITEMS[:], 0))
                v.sync()
                v.do(dve.memset(ITEMS[0:1, L_ROW:L_ROW + 1], PAIRS))
                for r, l0 in ((0, L_EXPERT), (1, L_ROW + 1), (2, L_SIZE)):
                    v.do(dve.tensor_copy(ITEMS[0:1, l0:l0 + SLOTS], LOUT[0:1, r, :]))
                v.do(dve.tensor_copy(ITEMS[0:1, L_NUM:L_NUM + 1], LOUT[0:1, 3, 0:1]))
                v.sync()
                dve.sem_inc(S["items_ready"], 1)
                q.n += 2 * NT
                n_items = dve.value_load(ITEMS[0:1, L_NUM:L_NUM + 1], min_val=NE, max_val=SLOTS)
                cs = [conv, q, m, req, split, sreq]
                per = {conv: 2 * len(item_kinds), q: 12 * MOE_GROUPS, m: 14, req: 2 * MOE_GROUPS, split: KC + 2 * MOE_GROUPS,
                       sreq: KC + 2 * MOE_GROUPS}
                kp_main = kp[0]
                kp[0], kp[1] = 0, item_kinds * 2
                for _ in range(LOOK):
                    convert()
                for i in range(3):
                    dve.wait_ge(S[f"rows_gone{i}"], 32 * (NT // 3))
                v.do(dve.memset(EACC[:], 0.0))

                def prepare(k):
                    dve.wait_ge(S["split_hi"], split.at(split.n + 1))
                    spacer(dve)
                    v.do(dve.scalar_tensor_tensor(XSL[:, k, :], PS[:, 6 + m.n % 2, 0:CAP], gain(3)[:, k:k + 1], XSH[:, k, :].bitcast(F32),
                                                  ALU.mult, ALU.subtract), m)
                    v.sync()
                    dve.sem_inc(split.next(), 1)
                    if k == KC - 1:
                        dve.sem_inc(S["split_req"], KC)
                        sreq.n += KC
                        dve.sem_inc(S["xg_used"], 1)

                def item_out(number, j):
                    r0, n = XBLK[j]
                    if j == 0:
                        dve.wait_ge(S["ys_out"], number * 48)
                    for h in range(2):
                        ps = misc_ready()
                        v.do(dve.tensor_copy(YT[j][0:n, h * 512:h * 512 + 512], ps[0:n, :]), m)
                    v.sync()
                    dve.sem_inc(S["ys_full"], 1)

                for k in range(KC):
                    prepare(k)
                with dve.Fori(0, SLOTS) as it:
                    with dve.If(it < n_items):
                        size = dve.value_load(ITEMS[0:1, bass.ds(it + L_SIZE, 1)], min_val=0, max_val=len(SIZES) - 1)
                        st = looped(cs, it, per)

                        def item(rows):
                            kp[0] = LOOK

                            def step(kind, g, between=lambda d: None):
                                if kind == "GU":
                                    for f in range(2):
                                        ps = main_ready()
                                        v.do(dve.tensor_copy(EG[:, f, 0:rows], ps[:, 0:rows]), q)
                                        v.sync()
                                        dve.sem_inc(req.next(), 1)
                                        convert()
                                        between(f)
                                    for f in range(2):
                                        ps = main_ready()
                                        t = T[sreq.n % 2][:, 0:rows]
                                        if f == 0:
                                            dve.wait_ge(S["act_done"], req.at(req.n))
                                        v.do(dve.tensor_tensor(t, ps[:, 0:rows], EG[:, f, 0:rows], ALU.mult), q)
                                        v.sync()
                                        dve.sem_inc(sreq.next(), 1)
                                        convert()
                                        dve.wait_ge(S["split_hi"], sreq.at(sreq.n))
                                        v.do(dve.tensor_tensor(ELO[g % 2][:, f, 0:rows], t, EHI[g % 2][:, f, 0:rows].bitcast(F32), ALU.subtract), split)
                                        v.sync()
                                        between(2 + f)
                                else:
                                    for d in range(KC):
                                        if d == 3:
                                            convert()
                                        ps = main_ready()
                                        a = EACC[:, d, 0:rows]
                                        v.do(dve.tensor_tensor(a, ps[:, 0:rows], a, ALU.add), q)
                                        between(d)
                                    v.sync()
                                    convert()

                            head, body, tail = ffn_schedule(MOE_GROUPS, MOE_LOOP)
                            for s in head:
                                step(*s, between=lambda u: item_out(it, u) if u < len(XBLK) else None)
                            dve.wait_ge(S["sums_clear"], it + 1)
                            cs2 = [conv, q, req, split, sreq]
                            per2 = {conv: 12, q: 24, req: 4, split: 4, sreq: 4}
                            spacer(dve)
                            with dve.Fori(0, MOE_LOOP) as i:
                                st2 = looped(cs2, i, per2)
                                for s in body:
                                    step(*s)
                            leave(cs2, st2, per2, MOE_LOOP)
                            kp[0] += 12 * (MOE_LOOP - 1)
                            step(*tail[0])
                            step(*tail[1], between=prepare)
                            step(*tail[2])

                        sized(dve, size, cs, item)
                        leave_items(cs, st, per, n_items)
                kp[0], kp[1] = kp_main + LOOK, kinds
                for j in range(len(XBLK)):
                    item_out(n_items, j)
                dve.wait_ge(S["act_done"], req.at(req.n))
                def combine(j):
                    n = tokens(j)
                    y0, y1 = YG[j % GATHERS][0][0:n, :], YG[j % GATHERS][1][0:n, :]
                    dve.wait_ge(S["weighted"], j + 1)
                    v.do(dve.scalar_tensor_tensor(y0, y1, TW[0:n, 1, j:j + 1], y0, ALU.mult, ALU.add))
                    v.sync()
                    dve.sem_inc(S["combined"], 1)

                combine(0)
                for j in range(NT):
                    n = tokens(j)
                    if j + 1 < NT:
                        combine(j + 1)
                    for h in range(2):
                        dve.wait_ge(S["split_hi"], split.at(split.n + 1))
                        spacer(dve)
                        ps = PS[:, 6 + m.n % 2, 0:4 * P].rearrange("p (k t) -> p k t", k=4)[:, :, 0:n]
                        x0 = XLO[:, 4 * h:4 * h + 4, j * P:j * P + n]
                        v.do(dve.tensor_tensor(x0, ps, XHF[:, 4 * h:4 * h + 4, j * P:j * P + n], ALU.subtract), m)
                        sq = SQS[:, j * P:j * P + n]
                        squares = TC[h][:, :, 0:n].rearrange("p k t -> p t k")
                        if h == 0:
                            v.do(dve.tensor_reduce(sq, squares, AXX, ALU.add), split)
                        else:
                            v.do(dve.tensor_reduce(T[2][:, 0:n], squares, AXX, ALU.add), split)
                            v.sync()
                            v.do(dve.tensor_tensor(sq, sq, T[2][:, 0:n], ALU.add))
                            v.sync()
                    dve.sem_inc(S["gather_used"], 1)
                sreq.n += 2 * NT
                dve.sem_inc(S["split_req"], 2 * NT)
                dve.sem_inc(sqc.next(), 1)
            for c in range(2):
                for t0, n in BLOCKS:
                    ps = misc_ready()
                    v.do(dve.tensor_copy(PT[:, c, t0:t0 + n], ps[:, 0:n]), m)
            v.sync()
            split_branch(PT, P_SPLIT)
            dve.sem_inc(S["p_ready"], 1)
            norm()
            split_pw()
            for d in range(KC):
                if not (l == 1 and d >= KC - LOOK):
                    convert()
                for j, (t0, n) in enumerate(BLOCKS):
                    if j == 2 and d < KC - 1:
                        split_pw()
                    ps = main_ready()
                    t = T[req.n % 2][:, 0:n]
                    v.do(dve.tensor_tensor(t, ps[:, 0:n], RSTD[:, t0:t0 + n], ALU.mult), q)
                    v.sync()
                    dve.sem_inc(req.next(), 1)
                    finish_x()
                    ps = main_ready()
                    dve.wait_ge(S["act_done"], req.at(req.n))
                    v.do(dve.tensor_tensor(t, ps[:, 0:n], t, ALU.mult), q)
                    v.sync()
                    x = XNEW[:, d, t0:t0 + n]
                    v.do(dve.tensor_tensor(x, t, XHF[:, d, t0:t0 + n], ALU.add))
                    v.sync()
                    v.do(dve.tensor_tensor(x, x, XLF[:, d, t0:t0 + n], ALU.add))
                    v.sync()
                    split_x(d, j, x, low=False)
            finish_x()
            dve.sem_inc(sqc.next(), 1)
            if l == 0:
                sreq.n += KC
                dve.sem_inc(S["split_req"], KC)
        norm_tokens()
        dve.sem_inc(S["rtok_ready"], 1)
        for j in range(NT):
            n = tokens(j)
            if j >= OUTS:
                dve.wait_ge(S[f"outputs{j % OUTS}"], 16 * (j // OUTS))
            ps = main_ready()
            v.do(dve.tensor_scalar(YOUT[j % OUTS][0:n, 0:512], ps[0:n, :], RTOK[0:n, j:j + 1], None, ALU.mult), q)
            v.sync()
            dve.sem_inc(S["y_full"], 1)

    es.close()


_INS = ["x_prompt", "x_sample", "state_conv_a", "state_conv_b", "state_pool", "p_prompt", "p_sample", "norm_mix_g", "w_in",
        "conv_a_w", "conv_b_w", "conv_b_bias", "conv_b_ln_g", "conv_b_ln_b", "pool_w", "pool_scale", "sgu_ln_g", "sgu_ln_b",
        "sgu_w", "sgu_b", "w_branch", "w_out", "norm_ffn_g", "ffn_w_gate", "ffn_w_up", "ffn_w_down", "router_w", "moe_w_gate",
        "moe_w_up", "moe_w_down", "norm_ple_g", "ple_w_gate", "ple_w_proj", "final_norm_g"]
_OUTS = [("y_p", (1, SEQ, D)), ("y_s", (NSEQ, DSEQ, D)),
         ("a_p", (DEPTH, 1, 2, DB)), ("b_p", (DEPTH, 1, 30, DB)), ("c_p", (DEPTH, 1, 15, DB)), ("v_p", (DEPTH, 1, P, DB)),
         ("a_s", (DEPTH, NSEQ, 2, DB)), ("b_s", (DEPTH, NSEQ, 30, DB)), ("c_s", (DEPTH, NSEQ, 15, DB)), ("v_s", (DEPTH, NSEQ, DSEQ, DB))]


def kernel(**inputs):
    import numpy as _np
    import concourse.bacc as _bacc
    from concourse import mybir as _mybir
    from concourse.bass_utils import run_bass_kernel_spmd as _run

    nc = _bacc.Bacc("TRN2", target_bir_lowering=False, num_devices=1)
    arrays, a, o = {}, {}, {}
    for name in _INS:
        x = _np.ascontiguousarray(inputs[name])
        arrays[f"in_{name}"] = x
        a[name] = nc.dram_tensor(f"in_{name}", x.shape, _mybir.dt.from_np(x.dtype), kind="ExternalInput").ap()
    for name, shape in _OUTS:
        o[name] = nc.dram_tensor(f"out_{name}", shape, _mybir.dt.float32, kind="ExternalOutput").ap()
    build(nc, a, o)
    r = _run(nc, [arrays], core_ids=[0])
    return tuple(r.results[0][f"out_{name}"] for name, _ in _OUTS)
```
